# Optimizing a Trainium2 kernel written in Bass

```python
import math
import jax, jax.numpy as jnp
from jax import lax
import numpy as np

D_MODEL = 1024
BATCH = 1
SEQ = 1024
DEPTH = 1

GLA_HEADS = 4
GLA_DK = 128
GLA_DV = 128
GLA_GATE_RANK = 16
GLA_GATE_TEMP = 16.0
GLA_CHUNK = 32
SB_HEADS = 4
SB_DH = 128
NSA_HEADS = 8
NSA_GROUPS = 1
NSA_DH = 64
CMP_BLOCK = 32
CMP_STRIDE = 16
CMP_HIDDEN = 256
SEL_BLOCK = 64
SEL_TOP_N = 8
WINDOW = 512
SEL_FORCE = 1000.0
REL_BUCKETS = 32
REL_MAX_DIST = 1024
FFN_HIDDEN = 4 * D_MODEL
Q_BLOCK = 128
N_BRANCHES = 3
RMS_EPS = 1e-6
NEG_BIG = -1e30

GLA_QK = GLA_HEADS * GLA_DK
GLA_V = GLA_HEADS * GLA_DV
SB_W = SB_HEADS * SB_DH
NSA_Q = NSA_HEADS * NSA_DH
NSA_KV = NSA_GROUPS * NSA_DH
IN_SIZES = (GLA_QK, GLA_QK, GLA_V, GLA_GATE_RANK, GLA_V,
            SB_W, SB_W, SB_W,
            NSA_Q, NSA_KV, NSA_KV, NSA_KV, NSA_KV, NSA_KV, NSA_KV, NSA_HEADS * N_BRANCHES,
            N_BRANCHES * D_MODEL)
N_IN = sum(IN_SIZES)

kernel_name = 'hybrid_gla_stickbreak_nsa_trunk'

def _rms(x, g):
    xf = x.astype(jnp.float32)
    y = xf * lax.rsqrt(jnp.mean(xf * xf, axis=-1, keepdims=True) + RMS_EPS)
    return (y * g.astype(jnp.float32)).astype(x.dtype)

def _masked_softmax(s, mask):
    s = jnp.where(mask, s.astype(jnp.float32), NEG_BIG)
    p = jax.nn.softmax(s, axis=-1)
    return jnp.where(mask, p, 0.0)

def _rel_bucket(dist):
    n = jnp.maximum(dist, 0)
    max_exact = REL_BUCKETS // 2
    nf = jnp.maximum(n, 1).astype(jnp.float32)
    large = max_exact + (jnp.log(nf / max_exact) / math.log(REL_MAX_DIST / max_exact)
                         * (REL_BUCKETS - max_exact)).astype(jnp.int32)
    large = jnp.minimum(large, REL_BUCKETS - 1)
    return jnp.where(n < max_exact, n, large)

def _gla(q, k, v, a_low, r, w_a2, b_a, norm_g):
    B, S, _ = q.shape
    H, DK, DV, C = GLA_HEADS, GLA_DK, GLA_DV, GLA_CHUNK
    nc = S // C
    f32 = jnp.float32
    log_a = jax.nn.log_sigmoid((a_low @ w_a2 + b_a).astype(f32)) / GLA_GATE_TEMP

    def chunks(t, d):
        return t.astype(f32).reshape(B, nc, C, H, d).transpose(1, 0, 3, 2, 4)

    qc, kc, vc, gc = chunks(q, DK) * (DK ** -0.5), chunks(k, DK), chunks(v, DV), chunks(log_a, DK)
    causal = jnp.tril(jnp.ones((C, C), bool))

    def step(state, inp):
        qi, ki, vi, gi = inp
        b = jnp.cumsum(gi, axis=2)
        o_inter = jnp.einsum('bhtk,bhkv->bhtv', qi * jnp.exp(b), state)
        diff = b[:, :, :, None, :] - b[:, :, None, :, :]
        decay = jnp.exp(jnp.where(causal[:, :, None], diff, -jnp.inf))
        scores = jnp.einsum('bhtk,bhsk,bhtsk->bhts', qi, ki, decay)
        o_intra = jnp.einsum('bhts,bhsv->bhtv', scores, vi)
        b_last = b[:, :, -1:, :]
        new_state = (state * jnp.exp(b_last[:, :, 0, :, None])
                     + jnp.einsum('bhsk,bhsv->bhkv', ki * jnp.exp(b_last - b), vi))
        return new_state, o_inter + o_intra

    _, o = lax.scan(step, jnp.zeros((B, H, DK, DV), f32), (qc, kc, vc, gc))
    o = o.transpose(1, 0, 3, 2, 4).reshape(B, S, H, DV)
    o = _rms(o, norm_g).reshape(B, S, H * DV) * jax.nn.silu(r.astype(f32))
    return o.astype(q.dtype)

def _stick_breaking(q, k, v):
    B, S, _ = q.shape
    H, DH = SB_HEADS, SB_DH
    nb = S // Q_BLOCK
    f32 = jnp.float32
    qt = q.reshape(B, S, H, DH).transpose(0, 2, 1, 3)
    kt = k.reshape(B, S, H, DH).transpose(0, 2, 1, 3)
    vt = v.reshape(B, S, H, DH).transpose(0, 2, 1, 3)
    idx = jnp.arange(Q_BLOCK)
    tri = (idx[:, None] > idx[None, :]).astype(f32)
    outs = []
    for c in range(nb):
        nk = c + 1
        K = nk * Q_BLOCK
        qi = qt[:, :, c * Q_BLOCK:K]
        kk = kt[:, :, :K]
        vv = vt[:, :, :K]
        qpos = c * Q_BLOCK + idx
        kpos = jnp.arange(K)
        causal = kpos[None, :] < qpos[:, None]
        z = jnp.einsum('bhqd,bhkd->bhqk', qi, kk).astype(f32) * (DH ** -0.5)
        l1mb = jnp.where(causal, jax.nn.log_sigmoid(-z), 0.0).reshape(B, H, Q_BLOCK, nk, Q_BLOCK)
        within = jnp.einsum('bhqnj,js->bhqns', l1mb, tri)
        blk = jnp.arange(nk)
        later = (blk[:, None] > blk[None, :]).astype(f32)
        after = jnp.einsum('bhqm,mn->bhqn', l1mb.sum(axis=-1), later)
        rest = (within + after[..., None]).reshape(B, H, Q_BLOCK, K)
        a = jnp.where(causal, jnp.exp(jax.nn.log_sigmoid(z) + rest), 0.0)
        outs.append(jnp.einsum('bhqk,bhkd->bhqd', a.astype(vv.dtype), vv))
    o = jnp.concatenate(outs, axis=2)
    return o.transpose(0, 2, 1, 3).reshape(B, S, H * DH)

def _nsa(q, kc, vc, ks, vs, kw, vw, gate, q_g, k_g, pe_k, pe_v, wk1, wk2, wv1, wv2, rel_bias):
    B, S, _ = q.shape
    H, G, D = NSA_HEADS, NSA_GROUPS, NSA_DH
    R = H // G
    f32 = jnp.float32
    scale = D ** -0.5
    q = _rms(q.reshape(B, S, H, D), q_g)
    ks = _rms(ks.reshape(B, S, G, D), k_g)
    kw = _rms(kw.reshape(B, S, G, D), k_g)
    vs = vs.reshape(B, S, G, D)
    vw = vw.reshape(B, S, G, D)
    kc = kc.reshape(B, S, G, D)
    vc = vc.reshape(B, S, G, D)

    n_cmp = (S - CMP_BLOCK) // CMP_STRIDE + 1
    tok_idx = jnp.arange(n_cmp)[:, None] * CMP_STRIDE + jnp.arange(CMP_BLOCK)[None, :]

    def compress(t, pe, w1, w2):
        blocks = t[:, tok_idx] + pe[:, None, :]
        blocks = blocks.transpose(0, 1, 3, 2, 4).reshape(B, n_cmp, G, CMP_BLOCK * D)
        return jax.nn.gelu(blocks @ w1) @ w2

    k_cmp = _rms(compress(kc, pe_k, wk1, wk2), k_g)
    v_cmp = compress(vc, pe_v, wv1, wv2)
    cmp_end = jnp.arange(n_cmp) * CMP_STRIDE + CMP_BLOCK - 1

    n_sel = S // SEL_BLOCK
    top_n = min(SEL_TOP_N, n_sel)
    span = CMP_BLOCK // CMP_STRIDE
    ratio = SEL_BLOCK // CMP_STRIDE
    ov_idx = jnp.arange(n_sel)[:, None] * ratio - (span - 1) + jnp.arange(ratio + span - 1)[None, :]
    ov_valid = (ov_idx >= 0) & (ov_idx < n_cmp)
    ov_idx = jnp.clip(ov_idx, 0, n_cmp - 1)
    ks_blk = ks.reshape(B, n_sel, SEL_BLOCK, G, D).transpose(0, 3, 1, 2, 4)
    vs_blk = vs.reshape(B, n_sel, SEL_BLOCK, G, D).transpose(0, 3, 1, 2, 4)
    kw_pad = jnp.pad(kw, ((0, 0), (WINDOW, 0), (0, 0), (0, 0)))
    vw_pad = jnp.pad(vw, ((0, 0), (WINDOW, 0), (0, 0), (0, 0)))
    bias_tab = rel_bias.reshape(REL_BUCKETS, G, R)
    nb = S // Q_BLOCK
    qb = q.reshape(B, nb, Q_BLOCK, G, R, D).transpose(1, 0, 2, 3, 4, 5)
    gb = jax.nn.sigmoid(gate.astype(f32)).reshape(B, nb, Q_BLOCK, G, R, N_BRANCHES).transpose(1, 0, 2, 3, 4, 5)
    b_ix = jnp.arange(B)[:, None, None, None]
    g_ix = jnp.arange(G)[None, None, :, None]
    blk = jnp.arange(n_sel)

    def block(args):
        qi, gi, c = args
        qpos = c * Q_BLOCK + jnp.arange(Q_BLOCK)
        s = jnp.einsum('bqgrd,bngd->bqgrn', qi, k_cmp).astype(f32) * scale
        s = s + bias_tab[_rel_bucket(qpos[:, None] - cmp_end[None, :])].transpose(0, 2, 3, 1)[None]
        m = (cmp_end[None, :] <= qpos[:, None])[None, :, None, None, :]
        p = _masked_softmax(s, m)
        o_cmp = jnp.einsum('bqgrn,bngd->bqgrd', p.astype(v_cmp.dtype), v_cmp)
        imp = p.sum(axis=3)
        imp = jnp.sum(jnp.where(ov_valid, imp[..., ov_idx], 0.0), axis=-1)
        cur = (qpos // SEL_BLOCK)[:, None]
        causal_blk = blk[None, :] * SEL_BLOCK <= qpos[:, None]
        forced = (blk[None, :] == cur) | (blk[None, :] == cur - 1) | (blk[None, :] == 0)
        score = jnp.where(causal_blk[None, :, None, :],
                          imp + jnp.where(forced, SEL_FORCE, 0.0)[None, :, None, :], NEG_BIG)
        _, sel = lax.top_k(score, top_n)
        k_sel = ks_blk[b_ix, g_ix, sel].reshape(B, Q_BLOCK, G, top_n * SEL_BLOCK, D)
        v_sel = vs_blk[b_ix, g_ix, sel].reshape(B, Q_BLOCK, G, top_n * SEL_BLOCK, D)
        kpos = (sel[..., None] * SEL_BLOCK + jnp.arange(SEL_BLOCK)).reshape(B, Q_BLOCK, G, top_n * SEL_BLOCK)
        dist = qpos[None, :, None, None] - kpos
        s = jnp.einsum('bqgrd,bqgld->bqgrl', qi, k_sel).astype(f32) * scale
        s = s + bias_tab[_rel_bucket(dist), g_ix].transpose(0, 1, 2, 4, 3)
        p = _masked_softmax(s, (dist >= 0)[:, :, :, None, :])
        o_slc = jnp.einsum('bqgrl,bqgld->bqgrd', p.astype(v_sel.dtype), v_sel)
        start = c * Q_BLOCK
        k_w = lax.dynamic_slice_in_dim(kw_pad, start, Q_BLOCK + WINDOW, axis=1)
        v_w = lax.dynamic_slice_in_dim(vw_pad, start, Q_BLOCK + WINDOW, axis=1)
        kpos_w = start - WINDOW + jnp.arange(Q_BLOCK + WINDOW)
        dist_w = qpos[:, None] - kpos_w[None, :]
        m = (dist_w >= 0) & (dist_w < WINDOW) & (kpos_w >= 0)[None, :]
        s = jnp.einsum('bqgrd,bkgd->bqgrk', qi, k_w).astype(f32) * scale
        s = s + bias_tab[_rel_bucket(dist_w)].transpose(0, 2, 3, 1)[None]
        p = _masked_softmax(s, m[None, :, None, None, :])
        o_win = jnp.einsum('bqgrk,bkgd->bqgrd', p.astype(v_w.dtype), v_w)
        o = gi[..., 0:1] * o_cmp + gi[..., 1:2] * o_slc + gi[..., 2:3] * o_win
        return o.reshape(B, Q_BLOCK, H * D)

    o = lax.map(block, (qb, gb, jnp.arange(nb)))
    return o.transpose(1, 0, 2, 3).reshape(B, S, H * D).astype(q.dtype)

def setup_inputs(seed: int = 0) -> dict:
    key = jax.random.key(seed)
    ks = jax.random.split(key, 24)
    f32 = jnp.float32
    L = DEPTH

    def nrm(k, shape, scale):
        return jax.random.normal(k, shape, f32) * scale

    def gain(k, shape):
        return 1.0 + 0.05 * jax.random.normal(k, shape, f32)

    return {
        'x': nrm(ks[0], (BATCH, SEQ, D_MODEL), 1.0),
        'ln_mix_g': gain(ks[1], (L, D_MODEL)),
        'ln_mlp_g': gain(ks[2], (L, D_MODEL)),
        'w_in': nrm(ks[3], (L, D_MODEL, N_IN), D_MODEL ** -0.5),
        'gla_w_a2': nrm(ks[4], (L, GLA_GATE_RANK, GLA_QK), GLA_GATE_RANK ** -0.5),
        'gla_b_a': nrm(ks[5], (L, GLA_QK), 0.1),
        'gla_norm_g': gain(ks[6], (L, GLA_DV)),
        'nsa_q_norm_g': gain(ks[7], (L, NSA_DH)),
        'nsa_k_norm_g': gain(ks[8], (L, NSA_DH)),
        'nsa_pe_k': nrm(ks[9], (L, CMP_BLOCK, NSA_DH), 0.1),
        'nsa_pe_v': nrm(ks[10], (L, CMP_BLOCK, NSA_DH), 0.1),
        'nsa_wk1': nrm(ks[11], (L, CMP_BLOCK * NSA_DH, CMP_HIDDEN), (CMP_BLOCK * NSA_DH) ** -0.5),
        'nsa_wk2': nrm(ks[12], (L, CMP_HIDDEN, NSA_DH), CMP_HIDDEN ** -0.5),
        'nsa_wv1': nrm(ks[13], (L, CMP_BLOCK * NSA_DH, CMP_HIDDEN), (CMP_BLOCK * NSA_DH) ** -0.5),
        'nsa_wv2': nrm(ks[14], (L, CMP_HIDDEN, NSA_DH), CMP_HIDDEN ** -0.5),
        'rel_bias': nrm(ks[15], (REL_BUCKETS, NSA_HEADS), 0.2),
        'w_br_gla': nrm(ks[16], (L, GLA_V, D_MODEL), GLA_V ** -0.5),
        'w_br_sb': nrm(ks[17], (L, SB_W, D_MODEL), SB_W ** -0.5),
        'w_br_nsa': nrm(ks[18], (L, NSA_Q, D_MODEL), NSA_Q ** -0.5),
        'w_out': nrm(ks[19], (L, D_MODEL, D_MODEL), D_MODEL ** -0.5),
        'w_up': nrm(ks[20], (L, D_MODEL, FFN_HIDDEN), D_MODEL ** -0.5),
        'w_down': nrm(ks[21], (L, FFN_HIDDEN, D_MODEL), FFN_HIDDEN ** -0.5),
    }

def reference(x, ln_mix_g, ln_mlp_g, w_in, gla_w_a2, gla_b_a, gla_norm_g, nsa_q_norm_g,
              nsa_k_norm_g, nsa_pe_k, nsa_pe_v, nsa_wk1, nsa_wk2, nsa_wv1, nsa_wv2, rel_bias,
              w_br_gla, w_br_sb, w_br_nsa, w_out, w_up, w_down):
    split_pts = np.cumsum(IN_SIZES)[:-1].tolist()
    for l in range(DEPTH):
        h = _rms(x, ln_mix_g[l])
        proj = h @ w_in[l]
        (gq, gk, gv, ga, gr, sq, sk, sv, nq, nkc, nvc, nks, nvs, nkw, nvw, ngate,
         mgate) = jnp.split(proj, split_pts, axis=-1)
        o_gla = _gla(gq, gk, gv, ga, gr, gla_w_a2[l], gla_b_a[l], gla_norm_g[l])
        o_sb = _stick_breaking(sq, sk, sv)
        o_nsa = _nsa(nq, nkc, nvc, nks, nvs, nkw, nvw, ngate, nsa_q_norm_g[l], nsa_k_norm_g[l],
                     nsa_pe_k[l], nsa_pe_v[l], nsa_wk1[l], nsa_wk2[l], nsa_wv1[l], nsa_wv2[l],
                     rel_bias)
        g_a, g_b, g_c = jnp.split(jax.nn.sigmoid(mgate), N_BRANCHES, axis=-1)
        merged = (g_a * (o_gla @ w_br_gla[l]) + g_b * (o_sb @ w_br_sb[l])
                  + g_c * (o_nsa @ w_br_nsa[l]))
        x = x + merged @ w_out[l]
        h = _rms(x, ln_mlp_g[l])
        x = x + jnp.square(jax.nn.relu(h @ w_up[l])) @ w_down[l]
    return x


_drawn_inputs = setup_inputs


def setup_inputs(seed=0):
    import zlib

    import numpy as np

    out = dict(_drawn_inputs(seed))
    spreads = {}
    factors = {'gla_b_a': 3.897,
     'gla_norm_g': 3.37,
     'nsa_q_norm_g': 8.0,
     'nsa_k_norm_g': 8.0,
     'nsa_pe_k': 8.0,
     'nsa_pe_v': 3.678,
     'rel_bias': 4.507}
    for name, (base, spread) in spreads.items():
        noise = np.random.default_rng([zlib.crc32(name.encode()), seed]).standard_normal(out[name].shape)
        drawn = base * np.exp(spread * noise) if base else spread * noise
        out[name] = __import__('jax').numpy.asarray(drawn.astype(out[name].dtype))
    for name, factor in factors.items():
        out[name] = (out[name] * factor).astype(out[name].dtype)
    return out
```

```python
from contextlib import ExitStack

import concourse.bass as bass
from concourse import mybir

P = 128
ALU = mybir.AluOpType
ACT = mybir.ActivationFunctionType
F32 = mybir.dt.float32
F32R = mybir.dt.float32r
BF16 = mybir.dt.bfloat16
U32 = mybir.dt.uint32
AX = mybir.AxisListType

D = 1024
S = 1024
KT = D // P
NT = S // P
HALF = 512
GH, GD, RANK, GTEMP = 4, 128, 16, 16.0
SH, SD = 4, 128
NH, ND = 8, 64
CMP_BLOCK, CMP_STRIDE, CMP_HID, NCMP = 32, 16, 256, 63
SEL, TOPN, NSEL, WINDOW = 64, 8, 16, 512
FF = 4 * D
EPS = 1e-6
NEG = -1e30
BUCKET_START = [0, 1, 2, 3, 4, 5, 6, 7, 8, 9, 10, 11, 12, 13, 14, 15,
                16, 21, 27, 35, 46, 59, 77, 99, 128, 166, 216, 280, 363, 470, 609, 790]

SIZES = [("gq", 512), ("gk", 512), ("gv", 512), ("ga", 16), ("gr", 512), ("sq", 512), ("sk", 512), ("sv", 512),
         ("nq", 512), ("kc", 64), ("vc", 64), ("ks", 64), ("vs", 64), ("kw", 64), ("vw", 64), ("ng", 24), ("mg", 3072)]
COL = {}
_at = 0
for _n, _w in SIZES:
    COL[_n] = _at
    _at += _w

CONST_COLS = [("ident", 128), ("tri", 128), ("ones", 128), ("strict", 128), ("strictneg", 128),
              ("window", 128), ("selbase", NT * NSEL), ("tie", NSEL * NSEL), ("flip", 128)]
CONST_AT = {}
_at = 0
for _n, _w in CONST_COLS:
    CONST_AT[_n] = (_at, _at + _w)
    _at += _w
CONST_W = _at
REV = S + P - 1


def with_dim(ap, axis, count):
    dims = [list(d) for d in ap.ap]
    dims.insert(axis, [0, count])
    return bass.AP(ap.tensor, ap.offset, dims)


def build(nc, x, w, out):
    ctx = ExitStack()
    with ctx:
        BASE = 17 * 1024
        KB = 1024

        def at(name, kb, shape, dt=F32):
            return nc.alloc_sbuf_tensor_at(name, list(shape), dt, offset=int(BASE + kb * KB))

        phase_sems = []

        def sem(name, keep=False):
            s = nc.alloc_semaphore(name=name)
            if not keep:
                phase_sems.append(s)
            return s

        def recycle():
            with nc.Block() as block:
                @block.gpsimd
                def _(pool):
                    for s in phase_sems:
                        pool.sem_clear(s)
            for s in phase_sems:
                nc.release_semaphore(s)
            phase_sems.clear()

        pairs = [ctx.enter_context(nc.psum_tensor(f"pair{i}", [P, 1024], F32)) for i in range(4)]
        bank = [pairs[i // 2][:, (i % 2) * 512:(i % 2 + 1) * 512] for i in range(8)]

        CONSTS, RING, RH, RM, RX = 0, 14, 38, 102, 134
        cst = at("cst", CONSTS, [P, CONST_W])
        kb = CONSTS + (CONST_W * 4 + 1023) / 1024.0
        kb = float(int(kb))
        causal = at("causal", kb, [P, P], U32); kb += 0.5
        identb = at("identb", kb, [P, P], BF16); kb += 0.25
        windowb = at("windowb", kb, [P, P], BF16); kb += 0.25
        gnorm = at("gnorm", kb, [P, GD]); kb += 0.5
        qgain = at("qgain", kb, [P, ND]); kb += 0.25
        kgain = at("kgain", kb, [P, ND]); kb += 0.25
        stat = at("stat", kb, [P, 8, 64]); kb += 2
        gatef = at("gatef", kb, [P, NT, 24]); kb += 0.75
        assert kb <= RING, kb

        def const(name, rows=P):
            a, b = CONST_AT[name]
            return cst[0:rows, a:b]

        stage = [at(f"stage{i}", RING + 4 * i, [P, 2, 512]) for i in range(2)]
        WH = [at(f"wh{i}", RING + 8 + 4 * i, [P, 2, 512], F32R) for i in range(2)]
        WL = [at(f"wl{i}", RING + 16 + 4 * i, [P, 2, 512], F32R) for i in range(2)]
        hH = at("hH", RH, [P, KT, S], F32R)
        hL = at("hL", RH + 32, [P, KT, S], F32R)
        merged = at("merged", RM, [P, KT, S])

        w_loaded = [sem("w_loaded0", True), sem("w_loaded1", True)]
        w_high = sem("w_high", True)
        w_split = sem("w_split", True)
        w_used = sem("w_used", True)
        bank_full = sem("bank_full", True)
        out_done = sem("out_done", True)

        done = {"slot": 0, "full": 0}

        class Product:

            def __init__(self, kind, mat, row0, col0, nslots, ncols=512, nbanks=8):
                self.kind, self.mat, self.row0, self.col0 = kind, mat, row0, col0
                self.nslots, self.ncols, self.nbanks = nslots, ncols, nbanks
                self.slot0, self.full0 = done["slot"], done["full"]
                done["slot"] += nslots
                done["full"] += nbanks - 1

        def more(n, per, i):
            return n if i is None else n + per * i

        def load_weights(sp, g, i=None, slots=0, src=None):
            for j in range(g.nslots):
                s = g.slot0 + j
                if s >= 2:
                    sp.wait_ge(w_split, more(s - 1, slots, i))
                if src is None:
                    r = g.row0 + 256 * j
                    ap = g.mat[r:r + 256, g.col0:g.col0 + g.ncols].rearrange("(k p) n -> p k n", p=P)
                else:
                    ap = src(j)
                sp.dma_start(stage[s % 2][:, :, 0:g.ncols], ap).then_inc(w_loaded[s % 2], 16)

        def split_weights(pool, g, i=None, slots=0):
            n = g.ncols
            for j in range(g.nslots):
                s = g.slot0 + j
                pool.wait_ge(w_loaded[s % 2], more(16 * (s // 2 + 1), 8 * slots, i))
                if s >= 2:
                    pool.wait_ge(w_used, more(s - 1, slots, i))
                pool.tensor_tensor(WH[s % 2][:, :, 0:n], stage[s % 2][:, :, 0:n],
                                   with_dim(with_dim(const("ones")[:, 0], 1, 2), 2, n), ALU.mult).then_inc(w_high, 1)
                pool.wait_ge(w_high, more(s + 1, slots, i))
                pool.tensor_tensor(WL[s % 2][:, :, 0:n], stage[s % 2][:, :, 0:n],
                                   WH[s % 2][:, :, 0:n].bitcast(F32), ALU.subtract).then_inc(w_split, 1)

        def product(pe, g, XH, XL, free, i=None, slots=0, before=None):
            for j in range(g.nslots):
                s = g.slot0 + j
                pe.wait_ge(w_split, more(s + 1, slots, i))
                if before is not None:
                    before(j)
                for b in range(g.nbanks):
                    if j == 0:
                        free(b)
                    n = 0
                    for kk in range(2):
                        kt = 2 * j + kk
                        for wt, xt in ((WH, XH), (WH, XL), (WL, XH)):
                            if g.kind == "T":
                                m, half = b // 2, b % 2
                                lhs = wt[s % 2][:, kk, m * P:(m + 1) * P]
                                rhs = xt[:, kt, half * HALF:(half + 1) * HALF]
                                dst = bank[b][:, :]
                            else:
                                lhs = xt[:, kt, b * P:(b + 1) * P]
                                rhs = wt[s % 2][:, kk, 0:g.ncols]
                                dst = bank[b][:, 0:g.ncols]
                            last = pe.matmul(dst, lhs, rhs, start=(j == 0 and n == 0),
                                             stop=(j == g.nslots - 1 and n == 5))
                            n += 1
                    if b == g.nbanks - 1:
                        last.then_inc(w_used, 1)
                    elif j == g.nslots - 1:
                        last.then_inc(bank_full, 1)

        def wait_bank(eng, g, b, i=None, slots=0, fulls=0):
            if b < g.nbanks - 1:
                eng.wait_ge(bank_full, more(g.full0 + b + 1, fulls, i))
            else:
                eng.wait_ge(w_used, more(g.slot0 + g.nslots, slots, i))

        def always(b):
            pass

        def inv_root(act, dve, ready, steps, ss, ms, r, t, count, part):
            mean, ln, ex, nwt = steps
            if part == "dve1":
                dve.tensor_scalar(ms, ss, 1.0 / count, EPS, ALU.mult, ALU.add).then_inc(mean, 1)
            elif part == "act":
                act.activation(r, ms, ACT.Ln).then_inc(ln, 1)
                act.wait_ge(ln, ready)
                act.activation(r, r, ACT.Exp, scale=-0.5).then_inc(ex, 1)
            else:
                dve.tensor_tensor(t, r, r, ALU.mult).then_inc(nwt, 1)
                dve.wait_ge(nwt, 4 * ready - 3)
                dve.tensor_tensor(t, t, ms, ALU.mult).then_inc(nwt, 1)
                dve.wait_ge(nwt, 4 * ready - 2)
                dve.tensor_scalar(t, t, -0.5, 1.5, ALU.mult, ALU.add).then_inc(nwt, 1)
                dve.wait_ge(nwt, 4 * ready - 1)
                dve.tensor_tensor(r, r, t, ALU.mult).then_inc(nwt, 1)
                dve.wait_ge(nwt, 4 * ready)

        def norm_transpose(tag, xin, gain_dram, load_x):
            gB = at(tag + "gB", RING + 8, [P, D])
            junk = at(tag + "junk", RING + 12, [P, D])
            xn = [at(tag + f"xn{i}", RING + 16 + 4 * i, [P, D]) for i in range(2)]
            x_loaded = [sem(tag + f"x_loaded{t}") for t in range(NT)] if load_x else None
            g_loaded = sem(tag + "g_loaded")
            sq_done = sem(tag + "sq_done")
            steps = tuple(sem(tag + n) for n in ("mean", "ln", "exp", "newton"))
            xn_ready = sem(tag + "xn_ready")
            turned = sem(tag + "turned")
            high_out, low_out = sem(tag + "high_out"), sem(tag + "low_out")
            ss, ms, r, t = (stat[:, k, 0:NT] for k in range(4))
            with nc.Block() as block:
                @block.sync
                def _(sp):
                    if load_x:
                        for i in range(NT):
                            sp.dma_start(xin[:, i, :], x[i * P:(i + 1) * P, :]).then_inc(x_loaded[i], 16)
                    sp.dma_start(gB[:, :], gain_dram.partition_broadcast(P)).then_inc(g_loaded, 16)
                    if load_x:
                        sp.dma_start(cst[:, :], w["cst"]).then_inc(g_loaded, 16)
                        sp.dma_start(causal[:, :], w["causal"]).then_inc(g_loaded, 16)
                        for dst, src in ((gnorm, "gla_norm_g"), (qgain, "nsa_q_norm_g"), (kgain, "nsa_k_norm_g")):
                            sp.dma_start(dst[:, :], w[src].partition_broadcast(P)).then_inc(g_loaded, 16)

                @block.scalar
                def _(act):
                    for i in range(NT):
                        if load_x:
                            act.wait_ge(x_loaded[i], 16)
                        if i:
                            act.wait_ge(sq_done, i)
                        act.activation(junk[:, :], xin[:, i, :], ACT.Square, accum_out=ss[:, i:i + 1]).then_inc(sq_done, 1)
                    act.wait_ge(steps[0], 1)
                    inv_root(act, None, 1, steps, ss, ms, r, t, D, "act")
                    for i in range(NT):
                        for q in range(2):
                            n = 2 * i + q
                            act.wait_ge(turned, n + 1)
                            act.copy(hH[:, 4 * q:4 * q + 4, i * P:(i + 1) * P],
                                     bank[n % 4][:, :].rearrange("p (k c) -> p k c", k=4)).then_inc(high_out, 1)

                @block.vector
                def _(dve):
                    dve.wait_ge(sq_done, NT)
                    inv_root(None, dve, 1, steps, ss, ms, r, t, D, "dve1")
                    dve.wait_ge(steps[2], 1)
                    dve.wait_ge(g_loaded, 96 if load_x else 16)
                    inv_root(None, dve, 1, steps, ss, ms, r, t, D, "dve2")

                    def low(n):
                        i, q = n // 2, n % 2
                        dve.wait_ge(high_out, n + 1)
                        dst = slice(i * P, (i + 1) * P)
                        dve.tensor_tensor(hL[:, 4 * q:4 * q + 4, dst],
                                          bank[n % 4][:, :].rearrange("p (k c) -> p k c", k=4),
                                          hH[:, 4 * q:4 * q + 4, dst].bitcast(F32), ALU.subtract).then_inc(low_out, 1)

                    for i in range(NT):
                        if i >= 2:
                            dve.wait_ge(turned, 2 * (i - 1))
                        dve.scalar_tensor_tensor(out=xn[i % 2][:, :], in0=xin[:, i, :], scalar=r[:, i:i + 1],
                                                 in1=gB[:, :], op0=ALU.mult, op1=ALU.mult).then_inc(xn_ready, 1)
                        if i:
                            low(2 * i - 2)
                            low(2 * i - 1)
                    low(2 * NT - 2)
                    low(2 * NT - 1)

                @block.tensor
                def _(pe):
                    if load_x:
                        pe.wait_ge(g_loaded, 96)
                    for i in range(NT):
                        pe.wait_ge(xn_ready, i + 1)
                        for q in range(2):
                            n = 2 * i + q
                            if n >= 4:
                                pe.wait_ge(low_out, n - 3)
                            for k in range(4):
                                kt = 4 * q + k
                                last = pe.transpose(bank[n % 4][:, k * P:(k + 1) * P],
                                                    xn[i % 2][:, kt * P:(kt + 1) * P], const("ident"))
                            last.then_inc(turned, 1)

        xin = at("xin", RX, [P, NT, D])
        norm_transpose("n1", xin, w["ln_mix_g"], True)

        def gla():
            la = at("la", RM, [P, GH, S])
            sr = at("sr", RM, [P, NT, 512])
            u = at("gu", RM + 16, [P, S])
            e = at("ge", RM + 20, [P, S])
            rsig = at("rsig", RM + 24, [P, 2, 512])
            q = at("gqT", RX, [P, GH, S])
            k = at("gkT", RX + 16, [P, GH, S])
            v = at("gv", RX + 32, [P, NT, 512])
            o = at("go", RX + 48, [P, NT, 512])
            sTm = [at(f"gsT{i}", RX + 64 + 2 * i, [P, GH, P]) for i in range(2)]
            ktok = at("gktok", RX + 68, [P, GH, P])
            St = at("gSt", RX + 70, [P, GH, P])
            St0 = at("gS", RM + 16, [P, GH, P])
            upd = at("gupd", RM + 18, [P, GH, P])
            wa2 = at("wa2", RX + 64, [RANK, 512])
            ba = at("ba", RX + 66, [P, GH])
            keep = at("gkeep", RM + 28, [P, S])
            lowT = at("glowT", RX + 48, [RANK, S])
            em, eb, ebm = (at(f"gem{n}", CONSTS + 13.25 + 0.125 * n, [P, GH, NT]) for n in range(3))

            prods = [("q", Product("T", w["w_in"], 0, COL["gq"], 4)), ("k", Product("T", w["w_in"], 0, COL["gk"], 4)),
                     ("v", Product("N", w["w_in"], 0, COL["gv"], 4)),
                     ("a", Product("T", w["w_in"], 0, COL["ga"], 4, ncols=128, nbanks=2)),
                     ("r", Product("N", w["w_in"], 0, COL["gr"], 4))]
            G = dict(prods)
            small = sem("g_small")
            out_q, out_k, out_v, out_a, out_r = (sem(f"g_out_{n}") for n in "qkvar")
            a_full, u_out, neg_abs, ex1, ln1, la_out, cum_out, dev_out = (
                sem(n) for n in ("g_a_full", "g_u_out", "g_negabs", "g_exp1", "g_ln1", "g_la", "g_cum", "g_dev"))
            eplus, eminus, decayed, mids, mid_e, keep_ok, rs_ok, sr_ok = (
                sem(n) for n in ("g_eplus", "g_eminus", "g_decayed", "g_mids", "g_mid_e", "g_keep", "g_rsig", "g_sr"))
            sc_full, sc_out, kt_full, kt_out, o_full, o_out, kv_full, st_upd, st_tmp = (
                sem(n) for n in ("g_scores", "g_scores_out", "g_kturn", "g_kturn_out", "g_o", "g_o_out", "g_kv",
                                 "g_state", "g_state_tmp"))
            osq, oss, steps = sem("g_osq"), sem("g_oss"), tuple(sem("g_" + n) for n in ("mean", "ln", "exp", "newton"))
            on1, on2, on3, turned, high_out, low_out = (
                sem(n) for n in ("g_on1", "g_on2", "g_on3", "g_turned", "g_high", "g_low"))
            oH = at("goH", RX, [P, GH, S], F32R)
            oL = at("goL", RX + 16, [P, GH, S], F32R)
            sq = at("gsq", RM + 20, [P, 2, 512])
            def low(dve, t):
                cs = slice(t * P, (t + 1) * P)
                dve.tensor_tensor(oL[:, :, cs], bank[t % 2][:, :].rearrange("p (h c) -> p h c", h=GH),
                                  oH[:, :, cs].bitcast(F32), ALU.subtract).then_inc(low_out, 1)

            with nc.Block() as block:
                @block.sync
                def _(sp):
                    sp.dma_start(wa2[:, :], w["gla_w_a2"]).then_inc(small, 16)
                    with nc.allow_non_contiguous_dma(reason="512 biases onto partitions"):
                        sp.dma_start(ba[:, :], w["gla_b_a"].rearrange("(h p) -> p h", p=P)).then_inc(small, 16)
                    for _, g in prods:
                        load_weights(sp, g)

                @block.gpsimd
                def _(pool):
                    pool.memset(keep[:, :], 1.0).then_inc(keep_ok, 1)
                    pool.wait_ge(keep_ok, 1)
                    pool.memset(keep[:, :].rearrange("p (c t) -> p c t", t=P)[:, :, 0:1], 0.0).then_inc(keep_ok, 1)
                    for _, g in prods:
                        split_weights(pool, g)

                @block.tensor
                def _(pe):
                    product(pe, G["q"], hH, hL, always)
                    product(pe, G["k"], hH, hL, lambda b: pe.wait_ge(out_q, b + 1))
                    product(pe, G["v"], hH, hL, lambda b: pe.wait_ge(out_k, b + 1))
                    product(pe, G["a"], hH, hL, lambda b: pe.wait_ge(out_v, b + 1))
                    pe.wait_ge(small, 32)
                    pe.wait_ge(out_a, 2)
                    pe.wait_ge(out_v, 8)
                    for h in range(GH):
                        for half in range(2):
                            n = 2 * h + half
                            if n >= 6:
                                pe.wait_ge(u_out, n - 5)
                            pe.matmul(bank[2 + n % 6][:, :], wa2[:, h * P:(h + 1) * P],
                                      lowT[:, half * HALF:(half + 1) * HALF], start=True, stop=True).then_inc(a_full, 1)
                    pe.wait_ge(u_out, 8)
                    product(pe, G["r"], hH, hL, always)
                    pe.wait_ge(out_r, 8)
                    pe.wait_ge(decayed, 2 * GH)
                    for c in range(NT):
                        p2 = c % 2
                        cs = slice(c * P, (c + 1) * P)
                        if c >= 2:
                            pe.wait_ge(sc_out, c - 1)
                        for h in range(GH):
                            last = pe.matmul(bank[p2][:, h * P:(h + 1) * P], k[:, h, cs], q[:, h, cs],
                                             start=True, stop=True)
                        last.then_inc(sc_full, 1)
                        if c < NT - 1:
                            if c >= 2:
                                pe.wait_ge(kt_out, c - 1)
                            for h in range(GH):
                                last = pe.transpose(bank[2 + p2][:, h * P:(h + 1) * P], k[:, h, cs], const("ident"))
                            last.then_inc(kt_full, 1)
                        pe.wait_ge(sc_out, c + 1)
                        if c >= 2:
                            pe.wait_ge(o_out, c - 1)
                        if c:
                            pe.wait_ge(st_upd, c)
                        for h in range(GH):
                            hs = slice(h * P, (h + 1) * P)
                            last = pe.matmul(bank[4 + p2][:, hs], sTm[p2][:, h, :], v[:, c, hs], start=True, stop=(c == 0))
                            if c:
                                last = pe.matmul(bank[4 + p2][:, hs], q[:, h, cs], St[:, h, :], start=False, stop=True)
                        last.then_inc(o_full, 1)
                        if c < NT - 1:
                            pe.wait_ge(kt_out, c + 1)
                            if c >= 2:
                                pe.wait_ge(st_upd, c)
                            for h in range(GH):
                                hs = slice(h * P, (h + 1) * P)
                                last = pe.matmul(bank[6 + p2][:, hs], ktok[:, h, :], v[:, c, hs], start=True, stop=True)
                            last.then_inc(kv_full, 1)
                    for t in range(NT):
                        pe.wait_ge(on3, t + 1)
                        if t >= 2:
                            pe.wait_ge(low_out, t - 1)
                        for h in range(GH):
                            last = pe.transpose(bank[t % 2][:, h * P:(h + 1) * P], o[:, t, h * P:(h + 1) * P], const("ident"))
                        last.then_inc(turned, 1)

                @block.scalar
                def _(act):
                    for b in range(8):
                        wait_bank(act, G["q"], b)
                        act.copy(q[:, b // 2, (b % 2) * HALF:(b % 2 + 1) * HALF], bank[b][:, :]).then_inc(out_q, 1)
                    for b in range(8):
                        wait_bank(act, G["k"], b)
                        act.copy(k[:, b // 2, (b % 2) * HALF:(b % 2 + 1) * HALF], bank[b][:, :]).then_inc(out_k, 1)
                    for b in range(8):
                        wait_bank(act, G["v"], b)
                        act.copy(v[:, b, :], bank[b][:, :]).then_inc(out_v, 1)
                    for b in range(2):
                        wait_bank(act, G["a"], b)
                        act.copy(lowT[:, b * HALF:(b + 1) * HALF], bank[b][0:RANK, :]).then_inc(out_a, 1)
                    for h in range(GH):
                        act.wait_ge(neg_abs, h + 1)
                        act.activation(e[:, :], e[:, :], ACT.Exp).then_inc(ex1, 1)
                        act.wait_ge(ex1, h + 1)
                        act.activation(e[:, :], e[:, :], ACT.Ln, bias=1.0).then_inc(ln1, 1)
                    act.wait_ge(mids, 3)
                    for src, dst in ((0, em), (1, eb), (2, ebm)):
                        act.activation(dst[:, :, :], dst[:, :, :], ACT.Exp, scale=1.0 / GTEMP).then_inc(mid_e, 1)
                    for h in range(GH):
                        act.wait_ge(dev_out, h + 1)
                        act.activation(e[:, :], u[:, :], ACT.Exp, scale=1.0 / GTEMP).then_inc(eplus, 1)
                        act.wait_ge(decayed, 2 * h + 1)
                        act.activation(e[:, :], u[:, :], ACT.Exp, scale=-1.0 / GTEMP).then_inc(eminus, 1)
                    for b in range(8):
                        wait_bank(act, G["r"], b)
                        if b >= 2:
                            act.wait_ge(sr_ok, b - 1)
                        act.activation(rsig[:, b % 2, :], bank[b][:, :], ACT.Sigmoid).then_inc(rs_ok, 1)
                    for c in range(NT):
                        if c < NT - 1:
                            act.wait_ge(kt_full, c + 1)
                            if c:
                                act.wait_ge(kv_full, c)
                            act.copy(ktok[:, :, :].rearrange("p h c -> p (h c)"), bank[2 + c % 2][:, :]).then_inc(kt_out, 1)
                        act.wait_ge(o_full, c + 1)
                        act.copy(o[:, c, :], bank[4 + c % 2][:, :]).then_inc(o_out, 1)
                    act.wait_ge(steps[0], 1)
                    inv_root(act, None, 1, steps, stat[:, 0, 0:32], stat[:, 1, 0:32], stat[:, 2, 0:32], stat[:, 3, 0:32], GD, "act")
                    for t in range(NT):
                        act.wait_ge(turned, t + 1)
                        act.copy(oH[:, :, t * P:(t + 1) * P],
                                 bank[t % 2][:, :].rearrange("p (h c) -> p h c", h=GH)).then_inc(high_out, 1)

                @block.vector
                def _(dve):
                    dve.wait_ge(small, 32)
                    for h in range(GH):
                        for half in range(2):
                            n = 2 * h + half
                            dve.wait_ge(a_full, n + 1)
                            if h and not half:
                                dve.wait_ge(la_out, h)
                            dve.tensor_scalar(u[:, half * HALF:(half + 1) * HALF], bank[2 + n % 6][:, :], ba[:, h:h + 1],
                                              None, ALU.add).then_inc(u_out, 1)
                        dve.wait_ge(u_out, 2 * h + 2)
                        dve.scalar_tensor_tensor(out=e[:, :], in0=u[:, :], scalar=-1.0, in1=u[:, :],
                                                 op0=ALU.mult, op1=ALU.min).then_inc(neg_abs, 1)
                        dve.wait_ge(ln1, h + 1)
                        dve.scalar_tensor_tensor(out=la[:, h, :], in0=u[:, :], scalar=0.0, in1=e[:, :],
                                                 op0=ALU.min, op1=ALU.subtract).then_inc(la_out, 1)
                        dve.wait_ge(la_out, h + 1)
                        if h == 0:
                            dve.wait_ge(keep_ok, 2)
                        dve.tensor_tensor_scan(la[:, h, :], keep[:, :], la[:, h, :], 0.0, ALU.mult, ALU.add).then_inc(cum_out, 1)
                    dve.wait_ge(cum_out, GH)
                    lac = la[:, :, :].rearrange("p h (c t) -> p h c t", t=P)
                    dve.tensor_copy(em[:, :, :], lac[:, :, :, P // 2 - 1]).then_inc(mids, 1)
                    dve.tensor_copy(eb[:, :, :], lac[:, :, :, P - 1]).then_inc(mids, 1)
                    dve.tensor_tensor(ebm[:, :, :], lac[:, :, :, P - 1], lac[:, :, :, P // 2 - 1],
                                      ALU.subtract).then_inc(mids, 1)
                    for h in range(GH):
                        if h:
                            dve.wait_ge(eminus, h)
                        dve.tensor_tensor(u[:, :].rearrange("p (c t) -> p c t", t=P), lac[:, h, :, :],
                                          with_dim(lac[:, h, :, P // 2 - 1], 2, P), ALU.subtract).then_inc(dev_out, 1)
                        dve.wait_ge(eplus, h + 1)
                        dve.wait_ge(out_q, 8)
                        dve.scalar_tensor_tensor(out=q[:, h, :], in0=q[:, h, :], scalar=GD ** -0.5, in1=e[:, :],
                                                 op0=ALU.mult, op1=ALU.mult).then_inc(decayed, 1)
                        dve.wait_ge(eminus, h + 1)
                        dve.wait_ge(out_k, 8)
                        dve.tensor_tensor(k[:, h, :], k[:, h, :], e[:, :], ALU.mult).then_inc(decayed, 1)
                    for b in range(8):
                        dve.wait_ge(rs_ok, b + 1)
                        dve.tensor_tensor(sr[:, b, :], bank[b][:, :], rsig[:, b % 2, :], ALU.mult).then_inc(out_r, 1)
                        dve.wait_ge(out_r, b + 1)
                        dve.tensor_tensor(sr[:, b, :].rearrange("p (h d) -> p h d", h=GH),
                                          sr[:, b, :].rearrange("p (h d) -> p h d", h=GH),
                                          with_dim(gnorm[:, :], 1, GH), ALU.mult).then_inc(sr_ok, 1)
                    for i in range(2):
                        dve.memset(sTm[i][:, :, :], 0.0).then_inc(st_tmp, 1)
                    dve.wait_ge(st_tmp, 2)
                    dve.wait_ge(mid_e, 3)
                    n = 2
                    for c in range(NT):
                        dve.wait_ge(sc_full, c + 1)
                        if c >= 2:
                            dve.wait_ge(o_full, c - 1)
                        dve.copy_predicated(sTm[c % 2][:, :, :], with_dim(causal[:, :], 1, GH),
                                            bank[c % 2][:, :].rearrange("p (h t) -> p h t", h=GH)).then_inc(sc_out, 1)
                        if c == NT - 1:
                            break
                        dve.wait_ge(kv_full, c + 1)
                        kv = bank[6 + c % 2][:, :].rearrange("p (h d) -> p h d", h=GH)
                        if c == 0:
                            dve.tensor_tensor(St0[:, :, :], kv, with_dim(ebm[:, :, c], 2, P), ALU.mult).then_inc(st_tmp, 1)
                            n += 1
                        else:
                            dve.tensor_tensor(upd[:, :, :], kv, with_dim(ebm[:, :, c], 2, P), ALU.mult).then_inc(st_tmp, 1)
                            dve.tensor_tensor(St0[:, :, :], St0[:, :, :], with_dim(eb[:, :, c], 2, P), ALU.mult).then_inc(st_tmp, 1)
                            dve.wait_ge(st_tmp, n + 2)
                            dve.tensor_tensor(St0[:, :, :], St0[:, :, :], upd[:, :, :], ALU.add).then_inc(st_tmp, 1)
                            n += 3
                        dve.wait_ge(st_tmp, n)
                        if c:
                            dve.wait_ge(o_full, c + 1)
                        dve.tensor_tensor(St[:, :, :], St0[:, :, :], with_dim(em[:, :, c + 1], 2, P),
                                          ALU.mult).then_inc(st_upd, 1)
                    for t in range(NT):
                        dve.wait_ge(o_out, t + 1)
                        if t >= 2:
                            dve.wait_ge(oss, t - 1)
                        dve.tensor_tensor(sq[:, t % 2, :], o[:, t, :], o[:, t, :], ALU.mult).then_inc(osq, 1)
                        dve.wait_ge(osq, t + 1)
                        dve.tensor_reduce(stat[:, 0, 4 * t:4 * t + 4], sq[:, t % 2, :].rearrange("p (h d) -> p h d", h=GH),
                                          AX.X, ALU.add).then_inc(oss, 1)
                    dve.wait_ge(oss, NT)
                    args = (steps, stat[:, 0, 0:32], stat[:, 1, 0:32], stat[:, 2, 0:32], stat[:, 3, 0:32], GD)
                    inv_root(None, dve, 1, *args, "dve1")
                    dve.wait_ge(steps[2], 1)
                    inv_root(None, dve, 1, *args, "dve2")
                    dve.wait_ge(sr_ok, 8)
                    for t in range(NT):
                        ot = o[:, t, :].rearrange("p (h d) -> p h d", h=GH)
                        dve.tensor_tensor(ot, ot, with_dim(stat[:, 2, 4 * t:4 * t + 4], 2, GD), ALU.mult).then_inc(on1, 1)
                        dve.wait_ge(on1, t + 1)
                        dve.tensor_tensor(o[:, t, :], o[:, t, :], sr[:, t, :], ALU.mult).then_inc(on3, 1)
                        if t:
                            dve.wait_ge(high_out, t)
                            low(dve, t - 1)
                    dve.wait_ge(high_out, NT)
                    low(dve, NT - 1)

            return oH, oL

        def merge(m, oH, oL, w_br, first):
            tag = f"m{m}_"
            gate = at(tag + "gate", RX + 48, [P, 4, S])
            tmp = [at(tag + f"tmp{i}", RX + 64 + 2 * i, [P, 512]) for i in range(2)]
            gates, branches = [], []
            for g in range(2):
                gates.append(Product("T", w["w_in"], 0, COL["mg"] + m * D + g * 512, 4))
                branches.append(Product("T", w_br, 0, g * 512, 2))
            gate_out, br_out, summed = sem(tag + "gate_out"), sem(tag + "br_out"), sem(tag + "summed")
            with nc.Block() as block:
                @block.sync
                def _(sp):
                    for g in range(2):
                        load_weights(sp, gates[g])
                        load_weights(sp, branches[g])

                @block.gpsimd
                def _(pool):
                    for g in range(2):
                        split_weights(pool, gates[g])
                        split_weights(pool, branches[g])

                @block.tensor
                def _(pe):
                    for g in range(2):
                        product(pe, gates[g], hH, hL, (lambda b: pe.wait_ge(br_out, b + 1)) if g else always)
                        product(pe, branches[g], oH, oL, lambda b: pe.wait_ge(gate_out, 8 * g + b + 1))

                @block.scalar
                def _(act):
                    for g in range(2):
                        for b in range(8):
                            wait_bank(act, gates[g], b)
                            if g:
                                act.wait_ge(br_out, b + 1)
                            act.activation(gate[:, b // 2, (b % 2) * HALF:(b % 2 + 1) * HALF], bank[b][:, :],
                                           ACT.Sigmoid).then_inc(gate_out, 1)

                @block.vector
                def _(dve):
                    for g in range(2):
                        for b in range(8):
                            n = 8 * g + b
                            cols = slice((b % 2) * HALF, (b % 2 + 1) * HALF)
                            dve.wait_ge(gate_out, n + 1)
                            wait_bank(dve, branches[g], b)
                            dst = merged[:, 4 * g + b // 2, cols]
                            if first:
                                dve.tensor_tensor(dst, bank[b][:, :], gate[:, b // 2, cols], ALU.mult).then_inc(br_out, 1)
                            else:
                                dve.tensor_tensor(tmp[n % 2][:, :], bank[b][:, :], gate[:, b // 2, cols],
                                                  ALU.mult).then_inc(br_out, 1)
                                dve.wait_ge(br_out, n + 1)
                                dve.tensor_tensor(dst, dst, tmp[n % 2][:, :], ALU.add).then_inc(summed, 1)

        def stick_breaking():
            q = at("sqT", RX, [P, SH, S])
            k = at("skT", RX + 16, [P, SH, S])
            v = at("sv", RX + 32, [P, NT, 512])
            e = [at(f"se{i}", RX + 48 + 2 * i, [P, 512]) for i in range(2)]
            spl = [at(f"ssp{i}", RX + 52 + 2 * i, [P, 512]) for i in range(2)]
            later = [at(f"slater{i}", RX + 56 + 2 * i, [P, 512]) for i in range(2)]
            a = [at(f"sa{i}", RX + 60 + 2 * i, [P, 512]) for i in range(2)]
            zs = [at(f"szs{i}", RX + 64 + 2 * i, [P, 512]) for i in range(3)]
            oT = at("soT", RX, [P, SH, S])
            oH = at("soH", RX + 16, [P, SH, S], F32R)
            oL = at("soL", RX + 32, [P, SH, S], F32R)
            Q, K, V = Product("T", w["w_in"], 0, COL["sq"], 4), Product("T", w["w_in"], 0, COL["sk"], 4), \
                Product("N", w["w_in"], 0, COL["sv"], 4)
            units = [(h, half, kb) for h in range(SH) for half in range(2) for kb in range(4 * half + 3, -1, -1)]
            first = [u for u, (h, half, kb) in enumerate(units) if kb == 4 * half + 3]
            ends = [u for u, (h, half, kb) in enumerate(units) if kb == 0]
            out_q, out_k, out_v = sem("s_out_q"), sem("s_out_k"), sem("s_out_v")
            z_full, na, ex, ln, spr, spm, lat, c_full, arg, argm, prob, pv, o_out = (
                sem("s_" + n) for n in ("z_full", "negabs", "exp", "ln", "softplus", "softplus_diag", "later", "c_full", "arg",
                                        "arg_diag", "prob", "pv", "o_out"))
            oh_done, ol_done = sem("s_oh"), sem("s_ol")
            scale = SD ** -0.5

            def off(u):
                h, half, kb = units[u]
                return max(0, kb - 4 * half) * P

            def diag(u):
                h, half, kb = units[u]
                return kb >= 4 * half

            ndiag = [0]
            for u in range(len(units)):
                ndiag.append(ndiag[-1] + diag(u))
            nend = [0]
            for u in range(len(units)):
                nend.append(nend[-1] + (u in ends))
            nlat, npart = [0], [0]
            for u in range(len(units)):
                nlat.append(nlat[-1] + (u not in ends))
                npart.append(npart[-1] + (u not in ends and u not in first and off(u) != off(u - 1)))
            zs_ok, lat_p = sem("s_z_scaled"), sem("s_later_part")

            with nc.Block() as block:
                @block.sync
                def _(sp):
                    for g in (Q, K, V):
                        load_weights(sp, g)

                @block.gpsimd
                def _(pool):
                    for g in (Q, K, V):
                        split_weights(pool, g)

                def ready_sp(eng, u):
                    if diag(u):
                        eng.wait_ge(spm, ndiag[u + 1])
                    else:
                        eng.wait_ge(spr, u + 1)

                @block.tensor
                def _(pe):
                    product(pe, Q, hH, hL, always)
                    product(pe, K, hH, hL, lambda b: pe.wait_ge(out_q, b + 1))
                    product(pe, V, hH, hL, lambda b: pe.wait_ge(out_k, b + 1))
                    pe.wait_ge(out_v, 8)

                    def scores(u):
                        h, half, kb = units[u]
                        o_ = off(u)
                        if u >= 3:
                            pe.wait_ge(zs_ok, u - 2)
                        pe.matmul(bank[u % 3][:, o_:512], k[:, h, kb * P:(kb + 1) * P],
                                  q[:, h, half * HALF + o_:(half + 1) * HALF], start=True, stop=True).then_inc(z_full, 1)

                    def sums(u):
                        o_ = off(u)
                        if u >= 3:
                            pe.wait_ge(arg, u - 2)
                        ready_sp(pe, u)
                        fst = u in first
                        last = pe.matmul(bank[3 + u % 3][:, o_:512], const("tri"), spl[u % 2][:, o_:512],
                                         start=True, stop=fst)
                        if not fst:
                            pe.wait_ge(lat, nlat[u])
                            if npart[u] > npart[u - 1]:
                                pe.wait_ge(lat_p, npart[u])
                            o1 = off(u - 1)
                            last = pe.matmul(bank[3 + u % 3][:, o1:512], const("ones"), later[(u + 1) % 2][:, o1:512],
                                             start=False, stop=True)
                        last.then_inc(c_full, 1)

                    def values(u):
                        h, half, kb = units[u]
                        o_ = off(u)
                        pe.wait_ge(prob, u + 1)
                        if u in first and nend[u] >= 2:
                            pe.wait_ge(o_out, nend[u] - 1)
                        last = pe.matmul(bank[6 + nend[u] % 2][:, o_:512], v[:, kb, h * P:(h + 1) * P],
                                         a[u % 2][:, o_:512], start=(u in first), stop=(kb == 0), skip_group_check=True)
                        last.then_inc(pv, 1)

                    n = len(units)
                    for s in range(n + 2):
                        if s < n:
                            scores(s)
                        if 1 <= s <= n:
                            sums(s - 1)
                        if s >= 2:
                            values(s - 2)

                @block.scalar
                def _(act):
                    for b in range(8):
                        wait_bank(act, Q, b)
                        act.copy(q[:, b // 2, (b % 2) * HALF:(b % 2 + 1) * HALF], bank[b][:, :]).then_inc(out_q, 1)
                    for b in range(8):
                        wait_bank(act, K, b)
                        act.copy(k[:, b // 2, (b % 2) * HALF:(b % 2 + 1) * HALF], bank[b][:, :]).then_inc(out_k, 1)
                    for b in range(8):
                        wait_bank(act, V, b)
                        act.copy(v[:, b, :], bank[b][:, :]).then_inc(out_v, 1)

                    def logs(u):
                        o_ = off(u)
                        act.wait_ge(z_full, u + 1)
                        if u >= 3:
                            act.wait_ge(arg, u - 2)
                        act.activation(zs[u % 3][:, o_:512], bank[u % 3][:, o_:512], ACT.Copy, scale=scale).then_inc(zs_ok, 1)
                        act.wait_ge(na, u + 1)
                        act.activation(e[u % 2][:, o_:512], e[u % 2][:, o_:512], ACT.Exp).then_inc(ex, 1)
                        act.wait_ge(ex, u + 1)
                        act.activation(e[u % 2][:, o_:512], e[u % 2][:, o_:512], ACT.Ln, bias=1.0).then_inc(ln, 1)

                    def probs(u):
                        o_ = off(u)
                        if diag(u):
                            act.wait_ge(argm, ndiag[u + 1])
                        else:
                            act.wait_ge(arg, u + 1)
                        act.activation(a[u % 2][:, o_:512], a[u % 2][:, o_:512], ACT.Exp).then_inc(prob, 1)

                    n = len(units)
                    for s in range(n + 1):
                        if s < n:
                            logs(s)
                        if s:
                            probs(s - 1)
                    for h in range(SH):
                        act.wait_ge(o_out, 2 * h + 2)
                        act.copy(oH[:, h, :], oT[:, h, :]).then_inc(oh_done, 1)

                @block.vector
                def _(dve):
                    def front(u):
                        o_ = off(u)
                        dve.wait_ge(zs_ok, u + 1)
                        if u >= 2:
                            dve.wait_ge(spr, u - 1)
                        z = zs[u % 3][:, o_:512]
                        dve.scalar_tensor_tensor(out=e[u % 2][:, o_:512], in0=z, scalar=-1.0, in1=z,
                                                 op0=ALU.mult, op1=ALU.min).then_inc(na, 1)

                    def softplus(u):
                        o_ = off(u)
                        dve.wait_ge(ln, u + 1)
                        if u >= 2:
                            dve.wait_ge(c_full, u - 1)
                        dve.scalar_tensor_tensor(out=spl[u % 2][:, o_:512], in0=zs[u % 3][:, o_:512], scalar=0.0,
                                                 in1=e[u % 2][:, o_:512], op0=ALU.max, op1=ALU.add).then_inc(spr, 1)
                        dve.wait_ge(spr, u + 1)
                        if diag(u):
                            dve.tensor_tensor(spl[u % 2][:, o_:o_ + P], spl[u % 2][:, o_:o_ + P], const("strict"),
                                              ALU.mult).then_inc(spm, 1)
                            dve.wait_ge(spm, ndiag[u + 1])
                        if u not in ends:
                            if u >= 2:
                                dve.wait_ge(c_full, u - 1)
                            if u in first:
                                dve.tensor_copy(later[u % 2][:, o_:512], spl[u % 2][:, o_:512]).then_inc(lat, 1)
                            else:
                                o1 = off(u - 1)
                                dve.wait_ge(lat, nlat[u])
                                if npart[u] > npart[u - 1]:
                                    dve.wait_ge(lat_p, npart[u])
                                dve.tensor_tensor(later[u % 2][:, o1:512], later[(u + 1) % 2][:, o1:512],
                                                  spl[u % 2][:, o1:512], ALU.add).then_inc(lat, 1)
                                if o1 != o_:
                                    dve.tensor_copy(later[u % 2][:, o_:o1], spl[u % 2][:, o_:o1]).then_inc(lat_p, 1)

                    def argument(u):
                        o_ = off(u)
                        dve.wait_ge(c_full, u + 1)
                        if u >= 2:
                            dve.wait_ge(pv, u - 1)
                        dve.tensor_tensor(a[u % 2][:, o_:512], zs[u % 3][:, o_:512], bank[3 + u % 3][:, o_:512],
                                          ALU.subtract).then_inc(arg, 1)
                        if diag(u):
                            dve.wait_ge(arg, u + 1)
                            dve.tensor_tensor(a[u % 2][:, o_:o_ + P], a[u % 2][:, o_:o_ + P], const("strictneg"),
                                              ALU.add).then_inc(argm, 1)

                    def out(i):
                        h, half, _ = units[ends[i]]
                        dve.wait_ge(pv, ends[i] + 1)
                        dve.tensor_copy(oT[:, h, half * HALF:(half + 1) * HALF], bank[6 + i % 2][:, :]).then_inc(o_out, 1)

                    n = len(units)
                    outs = 0
                    for s in range(n + 1):
                        if s < n:
                            front(s)
                        if s:
                            argument(s - 1)
                        if s < n:
                            softplus(s)
                        if s >= 3 and (s - 3) in ends:
                            out(outs)
                            outs += 1
                    out(outs)
                    for h in range(SH):
                        dve.wait_ge(oh_done, h + 1)
                        dve.tensor_tensor(oL[:, h, :], oT[:, h, :], oH[:, h, :].bitcast(F32), ALU.subtract).then_inc(ol_done, 1)
            return oH, oL
        def nsa():
            RH_T, RH_Q, RH_K, RH_S = RH, RH + 32, RH + 48, RH + 56
            qtok = at("nq", RX, [P, NT, 512])
            KVW = 280
            kvtok = at("nkv", RX + 16, [P, NT, KVW])
            kcv = at("nkcv", RX + 25, [P, S])
            kc2, vc2 = at("nkc2", RX + 29, [P, S]), at("nvc2", RX + 33, [P, S])
            sqt = at("nsqt", RX + 37, [P, 512])
            gC = at("ngateC", RX + 40, [P, KT, S])
            onehot, urev = at("nonehot", RX + 42, [33, REV]), at("nurev", RX + 48, [NH, REV + 1])
            relb = at("nrelb", RX + 41, [33, NH])
            NQ = Product("N", w["w_in"], 0, COL["nq"], 4)
            CV = Product("T", w["w_in"], 0, COL["kc"], 4, ncols=128, nbanks=2)
            KV = Product("N", w["w_in"], 0, COL["ks"], 4, ncols=KVW)
            GC = [Product("T", w["w_in"], 0, COL["mg"] + 2 * D + g * 512, 4) for g in range(2)]
            rel_in, rel_neg, rel_full, rel_out, rel_put = (sem("n_rel_" + n) for n in ("in", "neg", "full", "out", "put"))
            out_q, out_cv, out_kv, moved, out_gc = (sem("n_out_" + n) for n in ("q", "cv", "kv", "moved", "gc"))
            sq_a, sq_b, qn1, qn2, kn1, kn2 = (sem("n_" + n) for n in ("sq", "sumsq", "qn1", "qn2", "kn1", "kn2"))
            steps = tuple(sem("na_" + n) for n in ("mean", "ln", "exp", "newton"))
            steps2 = tuple(sem("nb_" + n) for n in ("mean", "ln", "exp", "newton"))
            q4 = qtok[:, :, :].rearrange("p t (h d) -> p t h d", h=NH)
            qstat = [stat[:, n, 0:64] for n in range(4)]
            kstat = [stat[:, 4 + n, 0:16] for n in range(4)]
            with nc.Block() as block:
                @block.sync
                def _(sp):
                    sp.dma_start(relb[0:32, :], w["rel_bias"]).then_inc(rel_in, 16)
                    sp.dma_start(onehot[:, :], w["onehot"]).then_inc(rel_in, 16)
                    for g in (NQ, CV, KV):
                        load_weights(sp, g)
                    sp.wait_ge(rel_out, 3)
                    sp.dma_start(w["bias_rev"][:, 0:REV], urev[:, 0:REV]).then_inc(rel_put, 16)
                    sp.wait_ge(out_cv, 2)
                    sp.dma_start(kc2[0:64, :], kcv[0:64, :]).then_inc(moved, 16)
                    sp.dma_start(kc2[64:128, 0:S - 1], kcv[0:64, 1:S]).then_inc(moved, 16)
                    sp.dma_start(vc2[0:64, :], kcv[64:128, :]).then_inc(moved, 16)
                    sp.dma_start(vc2[64:128, 0:S - 1], kcv[64:128, 1:S]).then_inc(moved, 16)
                    for g in GC:
                        load_weights(sp, g)
                    sp.wait_ge(moved, 64)
                    sp.wait_ge(rel_put, 16)

                @block.gpsimd
                def _(pool):
                    pool.memset(relb[32:33, :], NEG).then_inc(rel_neg, 1)
                    pool.wait_ge(rel_neg, 1)
                    for g in [NQ, CV, KV] + GC:
                        split_weights(pool, g)

                @block.tensor
                def _(pe):
                    pe.wait_ge(rel_in, 32)
                    pe.wait_ge(rel_neg, 1)
                    for n in range(3):
                        a, b = n * 512, min(REV, n * 512 + 512)
                        pe.matmul(bank[n][0:NH, 0:b - a], relb[:, :], onehot[:, a:b], start=True, stop=True).then_inc(rel_full, 1)
                    product(pe, NQ, hH, hL, lambda b: pe.wait_ge(rel_out, b + 1) if b < 3 else None)
                    product(pe, CV, hH, hL, lambda b: pe.wait_ge(out_q, b + 1))
                    product(pe, KV, hH, hL, lambda b: pe.wait_ge(out_cv, b + 1) if b < 2 else pe.wait_ge(out_q, b + 1))
                    product(pe, GC[0], hH, hL, lambda b: pe.wait_ge(out_kv, b + 1))
                    product(pe, GC[1], hH, hL, lambda b: pe.wait_ge(out_gc, b + 1))

                @block.scalar
                def _(act):
                    for n in range(3):
                        a, b = n * 512, min(REV, n * 512 + 512)
                        act.wait_ge(rel_full, n + 1)
                        act.copy(urev[:, a:b], bank[n][0:NH, 0:b - a]).then_inc(rel_out, 1)
                    for b in range(8):
                        wait_bank(act, NQ, b)
                        act.copy(qtok[:, b, :], bank[b][:, :]).then_inc(out_q, 1)
                    for b in range(2):
                        wait_bank(act, CV, b)
                        act.copy(kcv[:, b * HALF:(b + 1) * HALF], bank[b][:, :]).then_inc(out_cv, 1)
                    for b in range(8):
                        wait_bank(act, KV, b)
                        act.copy(kvtok[:, b, :], bank[b][:, 0:KVW]).then_inc(out_kv, 1)
                    act.wait_ge(steps[0], 1)
                    inv_root(act, None, 1, steps, *qstat, ND, "act")
                    act.wait_ge(steps2[0], 1)
                    inv_root(act, None, 1, steps2, *kstat, ND, "act")
                    act.wait_ge(rel_put, 16)
                    act.activation(gatef[:, :, :], kvtok[:, :, 256:280], ACT.Sigmoid)
                    for g in range(2):
                        for b in range(8):
                            wait_bank(act, GC[g], b)
                            act.activation(gC[:, 4 * g + b // 2, (b % 2) * HALF:(b % 2 + 1) * HALF], bank[b][:, :],
                                           ACT.Sigmoid).then_inc(out_gc, 1)

                @block.vector
                def _(dve):
                    for t in range(NT):
                        dve.wait_ge(out_q, t + 1)
                        if t:
                            dve.wait_ge(sq_b, t)
                        dve.tensor_tensor(sqt[:, :], qtok[:, t, :], qtok[:, t, :], ALU.mult).then_inc(sq_a, 1)
                        dve.wait_ge(sq_a, t + 1)
                        dve.tensor_reduce(qstat[0][:, 8 * t:8 * t + 8], sqt[:, :].rearrange("p (h d) -> p h d", h=NH),
                                          AX.X, ALU.add).then_inc(sq_b, 1)
                    dve.wait_ge(sq_b, NT)
                    inv_root(None, dve, 1, steps, *qstat, ND, "dve1")
                    n = NT
                    for t in range(NT):
                        for k in range(2):
                            dve.wait_ge(out_kv, t + 1)
                            dve.wait_ge(sq_b, n)
                            src = kvtok[:, t, 128 * k:128 * k + 64]
                            dve.tensor_tensor(sqt[:, 0:64], src, src, ALU.mult).then_inc(sq_a, 1)
                            n += 1
                            dve.wait_ge(sq_a, n)
                            dve.tensor_reduce(kstat[0][:, 2 * t + k:2 * t + k + 1], sqt[:, 0:64], AX.X, ALU.add).then_inc(sq_b, 1)
                    dve.wait_ge(sq_b, n)
                    inv_root(None, dve, 1, steps2, *kstat, ND, "dve1")
                    dve.wait_ge(steps[2], 1)
                    inv_root(None, dve, 1, steps, *qstat, ND, "dve2")
                    for t in range(NT):
                        dve.tensor_tensor(q4[:, t, :, :], q4[:, t, :, :],
                                          with_dim(qstat[2][:, 8 * t:8 * t + 8], 2, ND), ALU.mult).then_inc(qn1, 1)
                        dve.wait_ge(qn1, t + 1)
                        dve.scalar_tensor_tensor(out=q4[:, t, :, :], in0=q4[:, t, :, :], scalar=ND ** -0.5,
                                                 in1=with_dim(qgain[:, :], 1, NH), op0=ALU.mult, op1=ALU.mult).then_inc(qn2, 1)
                    dve.wait_ge(steps2[2], 1)
                    inv_root(None, dve, 1, steps2, *kstat, ND, "dve2")
                    for t in range(NT):
                        for k in range(2):
                            src = kvtok[:, t, 128 * k:128 * k + 64]
                            dve.scalar_tensor_tensor(out=src, in0=src, scalar=kstat[2][:, 2 * t + k:2 * t + k + 1],
                                                     in1=kgain[:, :], op0=ALU.mult, op1=ALU.mult).then_inc(kn2, 1)

            Tt = at("nT", RH_T, [P, NH, S])
            qT = at("nqT", RH_Q, [P, 4, S])
            ksT, kwT = at("nksT", RH_K, [P, S]), at("nkwT", RH_K + 4, [P, S])
            w1 = [at("nw1k", RH_T, [P, 16, CMP_HID]), at("nw1v", RH_T + 16, [P, 16, CMP_HID])]
            flipped = [at(f"nflip{i}", RING + 8 * i, [P, 2, S]) for i in range(2)]
            blk = [at(f"nblk{i}", RING + 16 + 4 * i, [P, 16, NCMP]) for i in range(2)]
            w2 = [at(f"nw2{i}", RX + 37 + 0.5 * i, [P, 2, ND]) for i in range(2)]
            pe2 = [at(f"npe{i}", RX + 38 + 0.0625 * i, [P, 16]) for i in range(2)]
            RP = RH_S
            hx, hu, hg = (at(f"nhid{i}", RP + i, [P, 4, NCMP]) for i in range(3))
            kcr, kcd = at("nkcr", RP + 3, [NCMP, ND]), at("nkcd", RP + 3.25, [NCMP, ND])
            vcn = at("nvcn", RX + 38.25, [NCMP, ND])
            kcT = at("nkcT", RX + 38.5, [P, NCMP])
            expandb = at("nexpandb", RX + 25, [NSEL, S], BF16)
            expandf = at("nexpandf", RP + 4, [NSEL, S])
            k_in = [sem(f"n_w1_in{i}") for i in range(2)]
            ex_in, tt_in = sem("n_expand_in"), [sem("n_table_in0"), sem("n_table_in1")]
            tt_full, tt_out = sem("n_table_full"), sem("n_table_out")
            blk_ok, hid_full, hx_ok, hs1, hs2, hs3, hsig, hg_ok, kc_full, kcs = (
                sem("n_" + n) for n in ("blk", "hid_full", "hx", "hs1", "hs2", "hs3", "hsig", "hg", "kc_full", "kcs"))
            kc_ok, kct_full, kct_out, tfull, tout, casts = (
                sem("n_" + n) for n in ("kc_ok", "kct_full", "kct_out", "tfull", "tout", "casts"))
            steps3 = tuple(sem("nc_" + n) for n in ("mean", "ln", "exp", "newton"))
            cstat = [stat[0:NCMP, n, 0:1] for n in range(4)]

            def skew(h0, h1):
                return bass.AP(w["bias_rev"].tensor, h0 * (REV + 1), [[1, P], [REV + 1, h1 - h0], [1, S]])

            with nc.Block() as block:
                @block.sync
                def _(sp):
                    sp.dma_start(w1[0][:, :, :], w["nsa_wk1"].rearrange("(m q) n -> q m n", q=P)).then_inc(k_in[0], 16)
                    with nc.allow_non_contiguous_dma(reason="2048 positional terms onto partitions"):
                        for i, src in enumerate(("nsa_pe_k", "nsa_pe_v")):
                            sp.dma_start(pe2[i][:, :], w[src].rearrange("(m p) d -> (p d) m", p=2)).then_inc(k_in[0], 16)
                    for i, src in enumerate(("nsa_wk2", "nsa_wv2")):
                        sp.dma_start(w2[i][:, :, :], w[src].rearrange("(j p) d -> p j d", p=P)).then_inc(k_in[0], 16)
                    sp.dma_start(w1[1][:, :, :], w["nsa_wv1"].rearrange("(m q) n -> q m n", q=P)).then_inc(k_in[1], 16)
                    sp.dma_start(expandf[:, :], w["expand"]).then_inc(ex_in, 16)
                    for g in range(4):
                        if g >= 2:
                            sp.wait_ge(tt_full, 4 * (g - 1))
                        sp.dma_start(flipped[g % 2][:, :, :], skew(2 * g, 2 * g + 2)).then_inc(tt_in[g % 2], 16)

                @block.tensor
                def _(pe):
                    n = 0
                    for t in range(NT):
                        for half in range(2):
                            if n >= 2:
                                pe.wait_ge(tout, n - 1)
                            if half == 0:
                                for j in range(4):
                                    last = pe.transpose(bank[n % 2][:, j * P:(j + 1) * P], qtok[:, t, j * P:(j + 1) * P],
                                                        const("ident"))
                            else:
                                for j in range(2):
                                    last = pe.transpose(bank[n % 2][0:64, j * P:(j + 1) * P],
                                                        kvtok[:, t, 128 * j:128 * j + 64], const("ident"))
                            last.then_inc(tfull, 1)
                            n += 1
                    pe.wait_ge(k_in[0], 80)
                    for i in range(2):
                        if i:
                            pe.wait_ge(k_in[1], 16)
                        pe.wait_ge(blk_ok, i + 1)
                        for j in range(2):
                            c0 = (2 * i + j) * NCMP
                            for m in range(16):
                                last = pe.matmul(bank[2][:, c0:c0 + NCMP], w1[i][:, m, j * P:(j + 1) * P], blk[i][:, m, :],
                                                 start=(m == 0), stop=(m == 15))
                        last.then_inc(hid_full, 1)
                    for g in range(4):
                        pe.wait_ge(tt_in[g % 2], 16 * (g // 2 + 1))
                        for j in range(4):
                            n = 4 * g + j
                            if n >= 2:
                                pe.wait_ge(tt_out, n - 1)
                            pe.matmul(bank[5 + n % 2][:, :], const("flip"), flipped[g % 2][:, j // 2, (j % 2) * 512:(j % 2 + 1) * 512],
                                      start=True, stop=True).then_inc(tt_full, 1)
                    pe.wait_ge(hg_ok, 1)
                    for i in range(2):
                        for j in range(2):
                            last = pe.matmul(bank[3][0:NCMP, i * ND:(i + 1) * ND], hg[:, 2 * i + j, :], w2[i][:, j, :],
                                             start=(j == 0), stop=(j == 1))
                    last.then_inc(kc_full, 1)
                    pe.wait_ge(kc_ok, 1)
                    pe.transpose(bank[4][0:64, 0:NCMP], kcd[:, :], const("ident", NCMP)[:, 0:NCMP]).then_inc(kct_full, 1)

                @block.scalar
                def _(act):
                    n = 0
                    for t in range(NT):
                        for half in range(2):
                            act.wait_ge(tfull, n + 1)
                            cs = slice(t * P, (t + 1) * P)
                            if half == 0:
                                act.copy(qT[:, :, cs], bank[n % 2][:, :].rearrange("p (j c) -> p j c", j=4)).then_inc(tout, 1)
                            else:
                                for j, dst in enumerate((ksT, kwT)):
                                    act.copy(dst[0:64, cs], bank[n % 2][0:64, j * P:(j + 1) * P]).then_inc(casts, 1)
                                    last = act.copy(dst[64:128, cs], bank[n % 2][0:64, j * P:(j + 1) * P])
                                    if j == 0:
                                        last.then_inc(casts, 1)
                                last.then_inc(tout, 1)
                            n += 1
                    act.wait_ge(hs3, 1)
                    act.activation(hu[:, :, :], hu[:, :, :], ACT.Sigmoid, scale=2 * 0.7978845608028654).then_inc(hsig, 1)
                    act.wait_ge(kc_full, 1)
                    act.copy(vcn[:, :], bank[3][0:NCMP, ND:2 * ND])
                    act.copy(kcr[:, :], bank[3][0:NCMP, 0:ND]).then_inc(kcs, 1)
                    act.wait_ge(steps3[0], 1)
                    inv_root(act, None, 1, steps3, *cstat, ND, "act")
                    act.wait_ge(kct_full, 1)
                    act.copy(kcT[0:64, :], bank[4][0:64, 0:NCMP])
                    act.copy(kcT[64:128, :], bank[4][0:64, 0:NCMP])
                    act.wait_ge(ex_in, 16)
                    act.copy(expandb[:, :], expandf[:, :])
                    act.copy(identb[:, :], const("ident"))
                    act.copy(windowb[:, :], const("window"))

                @block.vector
                def _(dve):
                    dve.wait_ge(k_in[0], 80)
                    for i, src in enumerate((kc2, vc2)):
                        row = src[:, :].ap[0][0]
                        win = bass.AP(src[:, :].tensor, src[:, :].offset, [[row, P], [2, 16], [CMP_STRIDE, NCMP]])
                        dve.tensor_tensor(blk[i][:, :, :], win, with_dim(pe2[i][:, :], 2, NCMP), ALU.add).then_inc(blk_ok, 1)
                    dve.wait_ge(hid_full, 2)
                    dve.tensor_copy(hx[:, :, :].rearrange("p a n -> p (a n)"), bank[2][:, 0:4 * NCMP]).then_inc(hx_ok, 1)
                    dve.wait_ge(hx_ok, 1)
                    dve.tensor_tensor(hu[:, :, :], hx[:, :, :], hx[:, :, :], ALU.mult).then_inc(hs1, 1)
                    dve.wait_ge(hs1, 1)
                    dve.tensor_scalar(hu[:, :, :], hu[:, :, :], 0.044715, 1.0, ALU.mult, ALU.add).then_inc(hs2, 1)
                    dve.wait_ge(hs2, 1)
                    dve.tensor_tensor(hu[:, :, :], hu[:, :, :], hx[:, :, :], ALU.mult).then_inc(hs3, 1)
                    dve.wait_ge(hsig, 1)
                    dve.tensor_tensor(hg[:, :, :], hx[:, :, :], hu[:, :, :], ALU.mult).then_inc(hg_ok, 1)
                    for n in range(16):
                        dve.wait_ge(tt_full, n + 1)
                        dve.tensor_copy(Tt[:, n // 2, (n % 2) * 512:(n % 2 + 1) * 512], bank[5 + n % 2][:, :]).then_inc(tt_out, 1)
                    dve.wait_ge(kcs, 1)
                    dve.tensor_tensor(kcd[:, :], kcr[:, :], kcr[:, :], ALU.mult).then_inc(hx_ok, 1)
                    dve.wait_ge(hx_ok, 2)
                    dve.tensor_reduce(cstat[0], kcd[:, :], AX.X, ALU.add).then_inc(hx_ok, 1)
                    dve.wait_ge(hx_ok, 3)
                    inv_root(None, dve, 1, steps3, *cstat, ND, "dve1")
                    dve.wait_ge(steps3[2], 1)
                    inv_root(None, dve, 1, steps3, *cstat, ND, "dve2")
                    dve.scalar_tensor_tensor(out=kcd[:, :], in0=kcr[:, :], scalar=cstat[2], in1=kgain[0:NCMP, :],
                                             op0=ALU.mult, op1=ALU.mult).then_inc(kc_ok, 1)

            sB = [at("nsB0", RH_S, [P, S]), at("nsB1", RH_S + 4, [P, S]), at("nsB2", RX + 29, [P, S])]
            pT = [at(f"npT{i}", RX + 4 * i, [P, 8, P]) for i in range(2)]
            osum = [at(f"nosum{i}", RX + 8 + 2 * i, [P, 512]) for i in range(2)]
            opart = at("nopart", RX + 12, [P, 512])
            gt, eq = at("ngt", RX + 14, [P, NSEL, NSEL]), at("neq", RX + 15, [P, NSEL, NSEL])
            impp = at("nimp", RX + 33, [P, 72])
            bscore, pen = at("nbscore", RX + 33.5, [P, NSEL]), at("npen", RX + 33.75, [P, NSEL])
            penT = at("npenT", RX + 34, [NSEL, P], BF16)
            rows = [at(f"nrows{i}", RX + 34.5 + 0.0625 * i, [P, NH]) for i in range(3)]
            nmax = [at(f"nnmax{i}", RX + 34.75 + 0.0625 * i, [P, NH]) for i in range(3)]
            coef = at("ncoef", RX + 35, [P, NH])
            cmx, csm = at("ncmx", RX + 35.25, [P, NH]), at("ncsm", RX + 35.5, [P, NH])
            oT = at("noT", RING, [P, 4, S])
            units = []
            for c in range(NT):
                units.append(("cmp", c, 0))
                units += [("win", c, h) for h in range(NH)] + [("slc", c, h) for h in range(NH)]
            N = len(units)
            group = [3 * c + ("cmp", "win", "slc").index(kind) for kind, c, _ in units]
            lastu = {g: max(u for u in range(N) if group[u] == g) for g in range(3 * NT)}
            firstu = {g: min(u for u in range(N) if group[u] == g) for g in range(3 * NT)}

            def ncmp(c):
                return min(NCMP, 8 * c + 7)

            def keys(u):
                kind, c, h = units[u]
                k0 = max(0, c - 4) if kind == "win" else 0
                return k0, c + 1 - k0

            uses = []
            for s in range(N + 6):
                u = s - 2
                if 0 <= u < N:
                    kind, c, h = units[u]
                    if kind == "cmp":
                        uses += [(s, "cmp", u, 0, 4), (s, "cmp", u, 4, 4)]
                    else:
                        nk = keys(u)[1]
                        uses += [(s, "p", u, a, min(4, nk - a)) for a in range(0, nk, 4)]
                    if kind == "win" and h == 3 and c >= 4:
                        uses.append((s, "pen", c, 0, 1))
                g = s - 5
                if 0 <= g < N and group[g] % 3 == 2 and lastu[group[g]] == g:
                    uses.append((s, "out", units[g][1], 0, 4))
            scores_full, add_out, max_out, exp_out, cmp_p, t_full, t_out, pv, grp_out = (
                sem("n_" + n) for n in ("scores", "biased", "rowmax", "exp", "cmp_p", "turned", "turn_out", "pv", "group_out"))
            chain, impz, pen_ok, pre_exp, o_ok, coef_ok = (sem("n_" + n) for n in (
                "chain", "impz", "pen", "cmp_biased", "o_sum", "coef"))
            npv = [0]
            for u in range(N):
                npv.append(npv[-1] + 1)
            ncmp_before = [sum(1 for v in range(u) if units[v][0] == "cmp") for u in range(N + 1)]
            pair = [pairs[0], pairs[1]]

            def table(c, h, k0, nk):
                a = S - P - P * c + P * k0
                return Tt[:, h, a:a + nk * P]

            with nc.Block() as block:
                @block.tensor
                def _(pe):
                    def scores(u):
                        kind, c, h = units[u]
                        if u >= 2:
                            pe.wait_ge(add_out, u - 1)
                        cs = slice(c * P, (c + 1) * P)
                        if kind == "cmp":
                            n = ncmp(c)
                            for h in range(NH):
                                rows_ = slice(64 * (h % 2), 64 * (h % 2) + 64)
                                col = 512 * (h % 2) + 64 * (h // 2)
                                last = pe.matmul(pair[u % 2][:, col:col + n], qT[rows_, h // 2, cs], kcT[rows_, 0:n],
                                                 start=True, stop=True)
                            last.then_inc(scores_full, 1)
                            return
                        k0, nk = keys(u)
                        kT = kwT if kind == "win" else ksT
                        rows_ = slice(64 * (h % 2), 64 * (h % 2) + 64)
                        if kind == "slc" and c >= 4 and h == 0:
                            pe.wait_ge(t_out, 1 + [n for n, x in enumerate(uses) if x[1] == "pen" and x[2] == c][0])
                        for a in range(0, nk, 4):
                            m = min(4, nk - a)
                            dst = pair[u % 2][:, a * P:(a + m) * P]
                            more_ = (kind == "slc" and c >= 4) or (kind == "win" and c >= 4 and a == 0)
                            last = pe.matmul(dst, qT[rows_, h // 2, cs], kT[rows_, (k0 + a) * P:(k0 + a + m) * P],
                                             start=True, stop=not (more_ and kind == "slc"))
                            if more_ and kind == "slc":
                                last = pe.matmul(dst, penT[:, :], expandb[:, (k0 + a) * P:(k0 + a + m) * P],
                                                 start=False, stop=True)
                            elif more_:
                                last = pe.matmul(pair[u % 2][:, 0:P], identb[:, :], windowb[:, :], start=False, stop=True,
                                                 skip_group_check=True)
                        last.then_inc(scores_full, 1)

                    def values(u):
                        kind, c, h = units[u]
                        g = group[u]
                        if u == firstu[g] and g >= 2:
                            pe.wait_ge(grp_out, g - 1)
                        ob = bank[6 + g % 2]
                        need = max(n for n, x in enumerate(uses) if x[1] in ("cmp", "p") and x[2] == u) + 1
                        pe.wait_ge(t_out, need)
                        if kind == "cmp":
                            n = ncmp(c)
                            for h in range(NH):
                                last = pe.matmul(ob[:, h * ND:(h + 1) * ND], pT[u % 2][0:n, h, :], vcn[0:n, :],
                                                 start=True, stop=True)
                        else:
                            k0, nk = keys(u)
                            at_ = 64 if kind == "slc" else 192
                            for a in range(nk):
                                last = pe.matmul(ob[:, h * ND:(h + 1) * ND], pT[u % 2][:, a, :], kvtok[:, k0 + a, at_:at_ + ND],
                                                 start=(a == 0), stop=(a == nk - 1))
                        last.then_inc(pv, 1)

                    n = 0
                    for s in range(N + 6):
                        if s < N:
                            scores(s)
                        while n < len(uses) and uses[n][0] == s:
                            _, what, u, a, m = uses[n]
                            if n >= 2:
                                pe.wait_ge(t_out, n - 1)
                            tb = bank[4 + n % 2]
                            if what == "cmp":
                                pe.wait_ge(cmp_p, ncmp_before[u + 1])
                                k = ncmp(units[u][1])
                                for j in range(4):
                                    last = pe.transpose(tb[0:k, j * P:(j + 1) * P],
                                                        sB[u % 3][:, (a + j) * 64:(a + j) * 64 + k], const("ident"))
                            elif what == "p":
                                pe.wait_ge(exp_out, u + 1)
                                for j in range(m):
                                    last = pe.transpose(tb[:, j * P:(j + 1) * P], sB[u % 3][:, (a + j) * P:(a + j + 1) * P],
                                                        const("ident"))
                            elif what == "pen":
                                pe.wait_ge(pen_ok, u - 3)
                                last = pe.transpose(tb[0:NSEL, 0:P], pen[:, :], const("ident"))
                            else:
                                pe.wait_ge(o_ok, u + 1)
                                for j in range(4):
                                    last = pe.transpose(tb[:, j * P:(j + 1) * P], osum[u % 2][:, j * P:(j + 1) * P], const("ident"))
                            last.then_inc(t_full, 1)
                            n += 1
                        if 0 <= s - 3 < N:
                            values(s - 3)

                @block.scalar
                def _(act):
                    n = 0
                    for s in range(N + 6):
                        while n < len(uses) and uses[n][0] == s:
                            _, what, u, a, m = uses[n]
                            act.wait_ge(t_full, n + 1)
                            tb = bank[4 + n % 2]
                            if what in ("cmp", "p") and u >= 2:
                                act.wait_ge(pv, u - 1)
                            if what == "cmp":
                                k = ncmp(units[u][1])
                                act.copy(pT[u % 2][0:k, a:a + 4, :], tb[0:k, :].rearrange("p (j c) -> p j c", j=4)).then_inc(t_out, 1)
                            elif what == "p":
                                act.copy(pT[u % 2][:, a:a + m, :],
                                         tb[:, 0:m * P].rearrange("p (j c) -> p j c", j=m)).then_inc(t_out, 1)
                            elif what == "pen":
                                act.copy(penT[:, :], tb[0:NSEL, 0:P]).then_inc(t_out, 1)
                            else:
                                act.copy(oT[:, :, u * P:(u + 1) * P], tb[:, :].rearrange("p (j c) -> p j c", j=4)).then_inc(t_out, 1)
                            n += 1
                        if s < N:
                            kind, c, h = units[s]
                            if kind == "cmp":
                                k = ncmp(c)
                                act.wait_ge(pre_exp, ncmp_before[s + 1])
                                v = sB[s % 3][:, 0:512].rearrange("p (h n) -> p h n", h=NH)[:, :, 0:k]
                                act.activation(v, v, ACT.Exp).then_inc(exp_out, 1)
                            else:
                                nk = keys(s)[1]
                                act.wait_ge(max_out, s + 1 - ncmp_before[s])
                                g = group[s]
                                v = sB[s % 3][:, 0:nk * P]
                                if h == 0 and g >= 3:
                                    act.wait_ge(grp_out, g - 2)
                                act.activation(v, v, ACT.Exp, bias=nmax[s % 3][:, 0:1],
                                               accum_out=rows[g % 3][:, h:h + 1]).then_inc(exp_out, 1)

                @block.vector
                def _(dve):
                    count = [0]

                    def link(ins):
                        count[0] += 1
                        ins.then_inc(chain, 1)
                        dve.wait_ge(chain, count[0])

                    def head_view(u, k):
                        return sB[u % 3][:, 0:512].rearrange("p (h n) -> p h n", h=NH)[:, :, 0:k]

                    def front(u):
                        kind, c, h = units[u]
                        dve.wait_ge(scores_full, u + 1)
                        if kind == "cmp":
                            k = ncmp(c)
                            v = head_view(u, k)
                            a = S - P - P * c + CMP_BLOCK - 1
                            full, banks = Tt[:, :, :], pair[u % 2][:, :]
                            bias = bass.AP(full.tensor, full.offset + a, [list(full.ap[0]), [2 * S, 4], [S, 2], [CMP_STRIDE, k]])
                            sc = bass.AP(banks.tensor, banks.offset, [list(banks.ap[0]), [64, 4], [512, 2], [1, k]])
                            dve.tensor_tensor(v.rearrange("p (i r) n -> p i r n", r=2), sc, bias, ALU.add).then_inc(add_out, 1)
                            dve.wait_ge(add_out, u + 1)
                            link(dve.tensor_reduce(cmx[:, :], v, AX.X, ALU.max))
                            link(dve.tensor_scalar(cmx[:, :], cmx[:, :], -1e20, None, ALU.max))
                            dve.tensor_tensor(v, v, with_dim(cmx[:, :], 2, k), ALU.subtract).then_inc(pre_exp, 1)
                            return
                        k0, nk = keys(u)
                        v = sB[u % 3][:, 0:nk * P]
                        dve.tensor_tensor(v, pair[u % 2][:, 0:nk * P], table(c, h, k0, nk), ALU.add).then_inc(add_out, 1)
                        dve.wait_ge(add_out, u + 1)
                        dve.tensor_reduce(nmax[u % 3][:, 0:1], v, AX.X, ALU.max, negate=True).then_inc(max_out, 1)

                    def cmp_normal(u):
                        c = units[u][1]
                        k = ncmp(c)
                        v = head_view(u, k)
                        dve.wait_ge(exp_out, u + 1)
                        link(dve.tensor_reduce(csm[:, :], v, AX.X, ALU.add))
                        link(dve.tensor_scalar(csm[:, :], csm[:, :], 1e-30, None, ALU.max))
                        link(dve.reciprocal(csm[:, :], csm[:, :]))
                        dve.tensor_tensor(v, v, with_dim(csm[:, :], 2, k), ALU.mult).then_inc(cmp_p, 1)
                        if c >= 4:
                            dve.wait_ge(cmp_p, c + 1)
                            link(dve.tensor_reduce(impp[:, 1:1 + k], v.rearrange("p h n -> p n h"), AX.X, ALU.add))

                    def choose(c):
                        full = impp[:, :]
                        win = bass.AP(full.tensor, full.offset, [list(full.ap[0]), [4, NSEL], [1, 5]])
                        link(dve.tensor_reduce(bscore[:, :], win, AX.X, ALU.add))
                        link(dve.tensor_tensor(bscore[:, :], bscore[:, :], const("selbase")[:, c * NSEL:(c + 1) * NSEL], ALU.add))
                        sj, si = with_dim(bscore[:, :], 1, NSEL), with_dim(bscore[:, :], 2, NSEL)
                        dve.tensor_tensor(gt[:, :, :], sj, si, ALU.is_gt).then_inc(impz, 1)
                        link(dve.tensor_tensor(eq[:, :, :], sj, si, ALU.is_equal))
                        link(dve.tensor_tensor(eq[:, :, :].rearrange("p a b -> p (a b)"), eq[:, :, :].rearrange("p a b -> p (a b)"),
                                               const("tie"), ALU.mult))
                        dve.wait_ge(impz, c - 4 + 2)
                        link(dve.tensor_tensor(gt[:, :, :], gt[:, :, :], eq[:, :, :], ALU.add))
                        link(dve.tensor_reduce(pen[:, :], gt[:, :, :], AX.X, ALU.add))
                        dve.tensor_scalar(pen[:, :], pen[:, :], TOPN - 0.5, NEG, ALU.is_gt, ALU.mult).then_inc(pen_ok, 1)

                    def finish(g):
                        c, br = g // 3, g % 3
                        gate = gatef[:, c, :].rearrange("p (h b) -> p h b", b=3)[:, :, (0, 2, 1)[br]]
                        ob = bank[6 + g % 2][:, :].rearrange("p (h d) -> p h d", h=NH)
                        dve.wait_ge(pv, lastu[g] + 1)
                        dst = (osum[c % 2] if br == 0 else opart)[:, :]
                        if br == 0:
                            link(dve.tensor_copy(coef[:, :], gate))
                        else:
                            link(dve.reciprocal(coef[:, :], rows[g % 3][:, :]))
                            link(dve.tensor_tensor(coef[:, :], coef[:, :], gate, ALU.mult))
                        dve.tensor_tensor(dst.rearrange("p (h d) -> p h d", h=NH), ob, with_dim(coef[:, :], 2, ND),
                                          ALU.mult).then_inc(grp_out, 1)
                        if br:
                            dve.wait_ge(grp_out, g + 1)
                            ins = dve.tensor_tensor(osum[c % 2][:, :], osum[c % 2][:, :], opart[:, :], ALU.add)
                            if br == 1:
                                link(ins)
                            else:
                                ins.then_inc(o_ok, 1)

                    dve.memset(impp[:, :], 0.0).then_inc(impz, 1)
                    dve.wait_ge(impz, 1)
                    for s in range(N + 5):
                        if s < N:
                            front(s)
                        if 1 <= s <= N and units[s - 1][0] == "cmp":
                            cmp_normal(s - 1)
                        if 2 <= s < N and units[s - 2][0] == "cmp" and units[s - 2][1] >= 4:
                            choose(units[s - 2][1])
                        if 4 <= s and s - 4 < N and lastu[group[s - 4]] == s - 4:
                            finish(group[s - 4])

            oH, oL = at("noH", RH, [P, 4, S], F32R), at("noL", RH + 16, [P, 4, S], F32R)
            tmp = [at(f"nmtmp{i}", RX + 2 * i, [P, 512]) for i in range(2)]
            oTs = at("noTs", RH + 32, [P, 4, S])
            BR = [Product("T", w["w_br_nsa"], 0, g * 512, 2) for g in range(2)]
            shifted, oh, ol, br_out, summed = (sem("n4_" + n) for n in ("shift", "oh", "ol", "br_out", "summed"))
            with nc.Block() as block:
                @block.scalar
                def _(act):
                    act.copy(oTs[:, :, :], oT[:, :, :]).then_inc(shifted, 1)
                    act.wait_ge(shifted, 1)
                    for h in range(4):
                        act.copy(oH[:, h, :], oTs[:, h, :]).then_inc(oh, 1)

                @block.sync
                def _(sp):
                    sp.wait_ge(shifted, 1)
                    for g in BR:
                        load_weights(sp, g)

                @block.gpsimd
                def _(pool):
                    for g in BR:
                        split_weights(pool, g)

                @block.tensor
                def _(pe):
                    pe.wait_ge(ol, 4)
                    product(pe, BR[0], oH, oL, always)
                    product(pe, BR[1], oH, oL, lambda b: pe.wait_ge(br_out, b + 1))

                @block.vector
                def _(dve):
                    for h in range(4):
                        dve.wait_ge(oh, h + 1)
                        dve.tensor_tensor(oL[:, h, :], oTs[:, h, :], oH[:, h, :].bitcast(F32), ALU.subtract).then_inc(ol, 1)
                    for g in range(2):
                        for b in range(8):
                            n = 8 * g + b
                            cols = slice((b % 2) * HALF, (b % 2 + 1) * HALF)
                            wait_bank(dve, BR[g], b)
                            dst = merged[:, 4 * g + b // 2, cols]
                            dve.tensor_tensor(tmp[n % 2][:, :], bank[b][:, :], gC[:, 4 * g + b // 2, cols],
                                              ALU.mult).then_inc(br_out, 1)
                            dve.wait_ge(br_out, n + 1)
                            dve.tensor_tensor(dst, dst, tmp[n % 2][:, :], ALU.add).then_inc(summed, 1)

        def output_and_ffn():
            mH, mL = at("mH", RH, [P, KT, S], F32R), at("mL", RH + 32, [P, KT, S], F32R)
            x1 = at("x1", RX, [P, NT, D])
            prods = [Product("N", w["w_out"], 0, g * 512, 4) for g in range(2)]
            x_back, mh, ml, x1_out = sem("o_x_back"), sem("o_high"), sem("o_low"), sem("o_x1")
            with nc.Block() as block:
                @block.sync
                def _(sp):
                    sp.dma_start(x1[:, :, :], x.rearrange("(t p) d -> p t d", p=P)).then_inc(x_back, 16)
                    for g in prods:
                        load_weights(sp, g)

                @block.gpsimd
                def _(pool):
                    for g in prods:
                        split_weights(pool, g)

                @block.scalar
                def _(act):
                    for kt in range(KT):
                        act.copy(mH[:, kt, :], merged[:, kt, :]).then_inc(mh, 1)

                @block.tensor
                def _(pe):
                    pe.wait_ge(ml, KT)
                    product(pe, prods[0], mH, mL, always)
                    product(pe, prods[1], mH, mL, lambda b: pe.wait_ge(x1_out, b + 1))

                @block.vector
                def _(dve):
                    for kt in range(KT):
                        dve.wait_ge(mh, kt + 1)
                        dve.tensor_tensor(mL[:, kt, :], merged[:, kt, :], mH[:, kt, :].bitcast(F32),
                                          ALU.subtract).then_inc(ml, 1)
                    dve.wait_ge(x_back, 16)
                    for g in range(2):
                        for b in range(8):
                            wait_bank(dve, prods[g], b)
                            dst = x1[:, b, g * 512:(g + 1) * 512]
                            dve.tensor_tensor(dst, dst, bank[b][:, :], ALU.add).then_inc(x1_out, 1)

            norm_transpose("n2", x1, w["ln_mlp_g"], False)

            uH, uL = at("uH", RM, [P, 4, S], F32R), at("uL", RM + 16, [P, 4, S], F32R)
            rr = [at(f"rr{i}", RX + 32 + 2 * i, [P, 512]) for i in range(2)]
            sqr = [at(f"sqr{i}", RX + 36 + 2 * i, [P, 512]) for i in range(2)]
            CH = FF // 512
            up = Product("T", w["w_up"], 0, 0, 4)
            down = [Product("N", w["w_down"], 0, g * 512, 2) for g in range(2)]
            SLOTS, FULLS = 8, 21
            done["slot"] += SLOTS * (CH - 1)
            done["full"] += FULLS * (CH - 1)
            relu, sq_, uh, ul, added, seeded = (sem("f_" + n) for n in ("relu", "square", "high", "low", "added", "seeded"))
            with nc.Block() as block:
                @block.sync
                def _(sp):
                    with sp.Fori(0, CH) as i:
                        load_weights(sp, up, i, SLOTS, lambda j: w["w_up"][256 * j:256 * j + 256, bass.ds(i * 512, 512)]
                                     .rearrange("(k p) n -> p k n", p=P))
                        for g in range(2):
                            load_weights(sp, down[g], i, SLOTS, lambda j: w["w_down"][
                                bass.ds(i * 512 + 256 * j, 256), g * 512:(g + 1) * 512].rearrange("(k p) n -> p k n", p=P))
                    for t in range(NT):
                        sp.wait_ge(added, 8 + 16 * (CH - 1) + 8 + t + 1)
                        sp.dma_start(out[t * P:(t + 1) * P, :], x1[:, t, :]).then_inc(out_done, 16)
                    sp.wait_ge(out_done, 16 * NT)

                @block.gpsimd
                def _(pool):
                    with pool.Fori(0, CH) as i:
                        for g in [up] + down:
                            split_weights(pool, g, i, SLOTS)

                @block.tensor
                def _(pe):
                    pe.wait_ge(seeded, 1)
                    with pe.Fori(0, CH) as i:
                        product(pe, up, hH2, hL2, lambda b: pe.wait_ge(added, 16 * i + b + 1), i, SLOTS)

                        product(pe, down[0], uH, uL, lambda b: pe.wait_ge(relu, 8 * i + b + 1), i, SLOTS,
                                before=lambda j: pe.wait_ge(ul, 8 * i + 4 * j + 4))
                        product(pe, down[1], uH, uL, lambda b: pe.wait_ge(added, 16 * i + 8 + b + 1), i, SLOTS)

                @block.scalar
                def _(act):
                    with act.Fori(0, CH) as i:
                        for b in range(8):
                            wait_bank(act, up, b, i, SLOTS, FULLS)
                            act.activation(rr[b % 2][:, :], bank[b][:, :], ACT.Relu).then_inc(relu, 1)
                            act.wait_ge(sq_, 8 * i + b + 1)
                            act.copy(uH[:, b // 2, (b % 2) * HALF:(b % 2 + 1) * HALF], sqr[b % 2][:, :]).then_inc(uh, 1)

                @block.vector
                def _(dve):
                    for b in range(8):
                        last = dve.memset(stat[:, 7, b:b + 1], 0.0)
                        last.then_inc(added, 1)
                    dve.wait_ge(added, 8)
                    dve.memset(stat[:, 7, 8:9], 0.0).then_inc(seeded, 1)
                    with dve.Fori(0, CH) as i:
                        for b in range(8):
                            dve.wait_ge(relu, 8 * i + b + 1)
                            dve.tensor_tensor(sqr[b % 2][:, :], rr[b % 2][:, :], rr[b % 2][:, :], ALU.mult).then_inc(sq_, 1)
                            dve.wait_ge(uh, 8 * i + b + 1)
                            dve.tensor_tensor(uL[:, b // 2, (b % 2) * HALF:(b % 2 + 1) * HALF], sqr[b % 2][:, :],
                                              uH[:, b // 2, (b % 2) * HALF:(b % 2 + 1) * HALF].bitcast(F32),
                                              ALU.subtract).then_inc(ul, 1)
                        for g in range(2):
                            for b in range(8):
                                wait_bank(dve, down[g], b, i, SLOTS, FULLS)
                                dst = x1[:, b, g * 512:(g + 1) * 512]
                                dve.tensor_tensor(dst, dst, bank[b][:, :], ALU.add).then_inc(added, 1)

        hH2, hL2 = hH, hL
        oH, oL = gla()
        merge(0, oH, oL, w["w_br_gla"], True)
        oH, oL = stick_breaking()
        merge(1, oH, oL, w["w_br_sb"], False)
        recycle()
        if "nsa" in PARTS:
            nsa()
            recycle()
        output_and_ffn()


_IN_NAMES = ["x", "ln_mix_g", "ln_mlp_g", "w_in", "gla_w_a2", "gla_b_a", "gla_norm_g", "nsa_q_norm_g", "nsa_k_norm_g",
             "nsa_pe_k", "nsa_pe_v", "nsa_wk1", "nsa_wk2", "nsa_wv1", "nsa_wv2", "rel_bias", "w_br_gla", "w_br_sb",
             "w_br_nsa", "w_out", "w_up", "w_down"]


def shape_constants():
    import numpy as np
    i = np.arange(P)[:, None]
    j = np.arange(P)[None, :]
    c = {
        "ident": i == j, "flip": i == P - 1 - j, "tri": i >= j, "ones": i >= 0 * j, "strict": i < j,
        "strictneg": np.where(i < j, 0.0, NEG), "window": np.where(j > i, 0.0, NEG),
    }
    q = np.arange(S).reshape(NT, P, 1)
    blk = np.arange(NSEL)[None, None, :]
    cur = q // SEL
    base = np.where((blk == cur) | (blk == cur - 1) | (blk == 0), 1000.0, 0.0)
    base = np.where(blk * SEL <= q, base, NEG)
    c["selbase"] = base.transpose(1, 0, 2).reshape(P, NT * NSEL)
    c["tie"] = np.broadcast_to((np.arange(NSEL)[None, :] < np.arange(NSEL)[:, None]).reshape(1, -1), (P, NSEL * NSEL))
    cst = np.concatenate([np.asarray(c[n], np.float32) for n, _ in CONST_COLS], axis=1)
    dist = (S - 1) - np.arange(REV)
    starts = np.asarray(BUCKET_START)
    bucket = np.where(dist < 0, 32, np.searchsorted(starts, np.maximum(dist, 0), side="right") - 1)
    onehot = (np.arange(33)[:, None] == bucket[None, :]).astype(np.float32)
    expand = (np.arange(NSEL)[:, None] == (np.arange(S) // SEL)[None, :]).astype(np.float32)
    return {"cst": np.ascontiguousarray(cst), "causal": (i <= j).astype(np.uint32), "onehot": onehot, "expand": expand}


PARTS = ("nsa",)


def kernel(**inputs):
    import numpy as np
    import concourse.bacc as bacc
    from concourse.bass_utils import run_bass_kernel_spmd

    nc = bacc.Bacc("TRN2", target_bir_lowering=False, num_devices=1)
    arrays, aps = {}, {}
    for name in _IN_NAMES:
        a = np.ascontiguousarray(inputs[name])
        if name == "x" or (name != "rel_bias" and a.ndim > 1):
            a = a.reshape(a.shape[1:])
        arrays[name] = a
    arrays.update(shape_constants())
    for name, a in arrays.items():
        aps[name] = nc.dram_tensor(name, a.shape, mybir.dt.from_np(a.dtype), kind="ExternalInput").ap()
    out = nc.dram_tensor("out", (S, D), F32, kind="ExternalOutput").ap()
    aps["bias_rev"] = nc.dram_tensor("bias_rev", (NH, REV + 1), F32, kind="Internal").ap()
    build(nc, aps["x"], aps, out)
    r = run_bass_kernel_spmd(nc, [arrays], core_ids=[0])
    return r.results[0]["out"].reshape(1, S, D)
```

```python
from contextlib import ExitStack

import concourse.bass as bass
from concourse import mybir

P = 128
ALU = mybir.AluOpType
ACT = mybir.ActivationFunctionType
F32 = mybir.dt.float32
F32R = mybir.dt.float32r
BF16 = mybir.dt.bfloat16
U32 = mybir.dt.uint32
AX = mybir.AxisListType

D = 1024
S = 1024
KT = D // P
NT = S // P
HALF = 512
GH, GD, RANK, GTEMP = 4, 128, 16, 16.0
SH, SD = 4, 128
NH, ND = 8, 64
CMP_BLOCK, CMP_STRIDE, CMP_HID, NCMP = 32, 16, 256, 63
SEL, TOPN, NSEL, WINDOW = 64, 8, 16, 512
FF = 4 * D
EPS = 1e-6
NEG = -1e30
BUCKET_START = [0, 1, 2, 3, 4, 5, 6, 7, 8, 9, 10, 11, 12, 13, 14, 15,
                16, 21, 27, 35, 46, 59, 77, 99, 128, 166, 216, 280, 363, 470, 609, 790]

SIZES = [("gq", 512), ("gk", 512), ("gv", 512), ("ga", 16), ("gr", 512), ("sq", 512), ("sk", 512), ("sv", 512),
         ("nq", 512), ("kc", 64), ("vc", 64), ("ks", 64), ("vs", 64), ("kw", 64), ("vw", 64), ("ng", 24), ("mg", 3072)]
COL = {}
_at = 0
for _n, _w in SIZES:
    COL[_n] = _at
    _at += _w

CONST_COLS = [("ident", 128), ("tri", 128), ("ones", 128), ("strict", 128), ("strictneg", 128),
              ("window", 128), ("selbase", NT * NSEL), ("tie", NSEL * NSEL), ("flip", 128)]
CONST_AT = {}
_at = 0
for _n, _w in CONST_COLS:
    CONST_AT[_n] = (_at, _at + _w)
    _at += _w
CONST_W = _at
REV = S + P - 1


def with_dim(ap, axis, count):
    dims = [list(d) for d in ap.ap]
    dims.insert(axis, [0, count])
    return bass.AP(ap.tensor, ap.offset, dims)


def build(nc, x, w, out):
    ctx = ExitStack()
    with ctx:
        BASE = 17 * 1024
        KB = 1024

        def at(name, kb, shape, dt=F32):
            return nc.alloc_sbuf_tensor_at(name, list(shape), dt, offset=int(BASE + kb * KB))

        phase_sems = []

        def sem(name, keep=False):
            s = nc.alloc_semaphore(name=name)
            if not keep:
                phase_sems.append(s)
            return s

        def recycle():
            with nc.Block() as block:
                @block.gpsimd
                def _(pool):
                    for s in phase_sems:
                        pool.sem_clear(s)
            for s in phase_sems:
                nc.release_semaphore(s)
            phase_sems.clear()

        pairs = [ctx.enter_context(nc.psum_tensor(f"pair{i}", [P, 1024], F32)) for i in range(4)]
        bank = [pairs[i // 2][:, (i % 2) * 512:(i % 2 + 1) * 512] for i in range(8)]

        CONSTS, RING, RH, RM, RX = 0, 14, 38, 102, 134
        cst = at("cst", CONSTS, [P, CONST_W])
        kb = CONSTS + (CONST_W * 4 + 1023) / 1024.0
        kb = float(int(kb))
        causal = at("causal", kb, [P, P], U32); kb += 0.5
        identb = at("identb", kb, [P, P], BF16); kb += 0.25
        windowb = at("windowb", kb, [P, P], BF16); kb += 0.25
        gnorm = at("gnorm", kb, [P, GD]); kb += 0.5
        qgain = at("qgain", kb, [P, ND]); kb += 0.25
        kgain = at("kgain", kb, [P, ND]); kb += 0.25
        stat = at("stat", kb, [P, 8, 64]); kb += 2
        gatef = at("gatef", kb, [P, NT, 24]); kb += 0.75
        assert kb <= RING, kb

        def const(name, rows=P):
            a, b = CONST_AT[name]
            return cst[0:rows, a:b]

        stage = [at(f"stage{i}", RING + 4 * i, [P, 2, 512]) for i in range(2)]
        WH = [at(f"wh{i}", RING + 8 + 4 * i, [P, 2, 512], F32R) for i in range(2)]
        WL = [at(f"wl{i}", RING + 16 + 4 * i, [P, 2, 512], F32R) for i in range(2)]
        hH = at("hH", RH, [P, KT, S], F32R)
        hL = at("hL", RH + 32, [P, KT, S], F32R)
        merged = at("merged", RM, [P, KT, S])

        w_loaded = [sem("w_loaded0", True), sem("w_loaded1", True)]
        w_high = sem("w_high", True)
        w_split = sem("w_split", True)
        w_used = sem("w_used", True)
        bank_full = sem("bank_full", True)
        out_done = sem("out_done", True)

        KVW = 280
        done = {"slot": 0, "full": 0}

        class Product:

            def __init__(self, kind, mat, row0, col0, nslots, ncols=512, nbanks=8):
                self.kind, self.mat, self.row0, self.col0 = kind, mat, row0, col0
                self.nslots, self.ncols, self.nbanks = nslots, ncols, nbanks
                self.slot0, self.full0 = done["slot"], done["full"]
                done["slot"] += nslots
                done["full"] += nbanks - 1

        def more(n, per, i):
            return n if i is None else n + per * i

        def load_weights(sp, g, i=None, slots=0, src=None, start=0, stop=None):
            for j in range(start, g.nslots if stop is None else stop):
                s = g.slot0 + j
                if s >= 2:
                    sp.wait_ge(w_split, more(s - 1, slots, i))
                if src is None:
                    r = g.row0 + 256 * j
                    ap = g.mat[r:r + 256, g.col0:g.col0 + g.ncols].rearrange("(k p) n -> p k n", p=P)
                else:
                    ap = src(j)
                sp.dma_start(stage[s % 2][:, :, 0:g.ncols], ap).then_inc(w_loaded[s % 2], 16)

        def split_weights(pool, g, i=None, slots=0, start=0, stop=None):
            n = g.ncols
            for j in range(start, g.nslots if stop is None else stop):
                s = g.slot0 + j
                pool.wait_ge(w_loaded[s % 2], more(16 * (s // 2 + 1), 8 * slots, i))
                if s >= 2:
                    pool.wait_ge(w_used, more(s - 1, slots, i))
                pool.tensor_tensor(WH[s % 2][:, :, 0:n], stage[s % 2][:, :, 0:n],
                                   with_dim(with_dim(const("ones")[:, 0], 1, 2), 2, n), ALU.mult).then_inc(w_high, 1)
                pool.wait_ge(w_high, more(s + 1, slots, i))
                pool.tensor_tensor(WL[s % 2][:, :, 0:n], stage[s % 2][:, :, 0:n],
                                   WH[s % 2][:, :, 0:n].bitcast(F32), ALU.subtract).then_inc(w_split, 1)

        def product(pe, g, XH, XL, free, i=None, slots=0, before=None):
            for j in range(g.nslots):
                s = g.slot0 + j
                pe.wait_ge(w_split, more(s + 1, slots, i))
                if before is not None:
                    before(j)
                for b in range(g.nbanks):
                    if j == 0:
                        free(b)
                    n = 0
                    for kk in range(2):
                        kt = 2 * j + kk
                        for wt, xt in ((WH, XH), (WH, XL), (WL, XH)):
                            if g.kind == "T":
                                m, half = b // 2, b % 2
                                lhs = wt[s % 2][:, kk, m * P:(m + 1) * P]
                                rhs = xt[:, kt, half * HALF:(half + 1) * HALF]
                                dst = bank[b][:, :]
                            else:
                                lhs = xt[:, kt, b * P:(b + 1) * P]
                                rhs = wt[s % 2][:, kk, 0:g.ncols]
                                dst = bank[b][:, 0:g.ncols]
                            last = pe.matmul(dst, lhs, rhs, start=(j == 0 and n == 0),
                                             stop=(j == g.nslots - 1 and n == 5))
                            n += 1
                    if b == g.nbanks - 1:
                        last.then_inc(w_used, 1)
                    elif j == g.nslots - 1:
                        last.then_inc(bank_full, 1)

        def wait_bank(eng, g, b, i=None, slots=0, fulls=0):
            if b < g.nbanks - 1:
                eng.wait_ge(bank_full, more(g.full0 + b + 1, fulls, i))
            else:
                eng.wait_ge(w_used, more(g.slot0 + g.nslots, slots, i))

        def always(b):
            pass

        def w_in(kind, col, **shape):
            return Product(kind, w["w_in"], 0, col, 4, **shape)

        def merge_products(m, w_br):
            order = [(w_in("T", COL["mg"] + m * D + g * 512), Product("T", w_br, 0, g * 512, 2)) for g in range(2)]
            return [x[0] for x in order], [x[1] for x in order]

        G = {"q": w_in("T", COL["gq"]), "k": w_in("T", COL["gk"]), "v": w_in("N", COL["gv"]),
             "a": w_in("T", COL["ga"], ncols=128, nbanks=2), "r": w_in("N", COL["gr"])}
        MERGE0 = merge_products(0, w["w_br_gla"])
        SQ, SK, SV = w_in("T", COL["sq"]), w_in("T", COL["sk"]), w_in("N", COL["sv"])
        MERGE1 = merge_products(1, w["w_br_sb"])
        NQ, CV = w_in("N", COL["nq"]), w_in("T", COL["kc"], ncols=128, nbanks=2)
        KV = w_in("N", COL["ks"], ncols=KVW)
        GC = [w_in("T", COL["mg"] + 2 * D + g * 512) for g in range(2)]
        BR = [Product("T", w["w_br_nsa"], 0, g * 512, 2) for g in range(2)]
        WO = [Product("N", w["w_out"], 0, g * 512, 4) for g in range(2)]
        UP = Product("T", w["w_up"], 0, 0, 4)
        DOWN = [Product("N", w["w_down"], 0, g * 512, 2) for g in range(2)]

        def inv_root(act, dve, ready, steps, ss, ms, r, t, count, part):
            mean, ln, ex, nwt = steps
            if part == "dve1":
                dve.tensor_scalar(ms, ss, 1.0 / count, EPS, ALU.mult, ALU.add).then_inc(mean, 1)
            elif part == "act":
                act.preload_act_table_set("natural_log_exp_and_others")
                act.activation(r, ms, ACT.Ln).then_inc(ln, 1)
                act.wait_ge(ln, ready)
                act.activation(r, r, ACT.Exp, scale=-0.5).then_inc(ex, 1)
            else:
                dve.tensor_tensor(t, r, r, ALU.mult).then_inc(nwt, 1)
                dve.wait_ge(nwt, 4 * ready - 3)
                dve.tensor_tensor(t, t, ms, ALU.mult).then_inc(nwt, 1)
                dve.wait_ge(nwt, 4 * ready - 2)
                dve.tensor_scalar(t, t, -0.5, 1.5, ALU.mult, ALU.add).then_inc(nwt, 1)
                dve.wait_ge(nwt, 4 * ready - 1)
                dve.tensor_tensor(r, r, t, ALU.mult).then_inc(nwt, 1)
                dve.wait_ge(nwt, 4 * ready)

        def norm_transpose(tag, xin, gain_dram, load_x, load_ahead, split_ahead):
            gB = at(tag + "gB", RM, [P, D])
            junk = at(tag + "junk", RM + 4, [P, D])
            xn = [at(tag + f"xn{i}", RM + 8 + 4 * i, [P, D]) for i in range(2)]
            x_loaded = [sem(tag + f"x_loaded{t}") for t in range(NT)] if load_x else None
            g_loaded = sem(tag + "g_loaded")
            sq_done = sem(tag + "sq_done")
            steps = tuple(sem(tag + n) for n in ("mean", "ln", "exp", "newton"))
            xn_ready = sem(tag + "xn_ready")
            turned = sem(tag + "turned")
            high_out, low_out = sem(tag + "high_out"), sem(tag + "low_out")
            groups = 4 if load_x else 1
            per = NT // groups
            lag = per if groups > 1 else 1

            def cols(g):
                return tuple(stat[:, k, g * per:(g + 1) * per] for k in range(4))

            r = stat[:, 2, 0:NT]
            with nc.Block() as block:
                @block.sync
                def _(sp):
                    if load_x:
                        for i in range(2):
                            sp.dma_start(xin[:, i, :], x[i * P:(i + 1) * P, :]).then_inc(x_loaded[i], 16)
                    sp.dma_start(gB[:, :], gain_dram.partition_broadcast(P)).then_inc(g_loaded, 16)
                    if load_x:
                        sp.dma_start(cst[:, :], w["cst"]).then_inc(g_loaded, 16)
                        sp.dma_start(causal[:, :], w["causal"]).then_inc(g_loaded, 16)
                        for dst, src in ((gnorm, "gla_norm_g"), (qgain, "nsa_q_norm_g"), (kgain, "nsa_k_norm_g")):
                            sp.dma_start(dst[:, :], w[src].partition_broadcast(P)).then_inc(g_loaded, 16)
                        for i in range(2, NT):
                            sp.dma_start(xin[:, i, :], x[i * P:(i + 1) * P, :]).then_inc(x_loaded[i], 16)
                    load_ahead(sp)

                @block.gpsimd
                def _(pool):
                    if load_x:
                        pool.wait_ge(g_loaded, 96)
                    split_ahead(pool)

                @block.scalar
                def _(act):
                    def high(i):
                        for q in range(2):
                            n = 2 * i + q
                            act.wait_ge(turned, n + 1)
                            act.copy(hH[:, 4 * q:4 * q + 4, i * P:(i + 1) * P],
                                     bank[n % 8][:, :].rearrange("p (k c) -> p k c", k=4)).then_inc(high_out, 1)

                    for g in range(groups):
                        if load_x:
                            for i in range(g * per, (g + 1) * per):
                                act.wait_ge(x_loaded[i], 16)
                                if i:
                                    act.wait_ge(sq_done, i)
                                act.activation(junk[:, :], xin[:, i, :], ACT.Square,
                                               accum_out=stat[:, 0, i:i + 1]).then_inc(sq_done, 1)
                        act.wait_ge(steps[0], g + 1)
                        inv_root(act, None, g + 1, steps, *cols(g), D, "act")
                        if g:
                            for i in range((g - 1) * per, g * per):
                                high(i)
                    for i in range((groups - 1) * per, NT):
                        high(i)

                @block.vector
                def _(dve):
                    def roots(g):
                        if load_x:
                            dve.wait_ge(sq_done, (g + 1) * per)
                        inv_root(None, dve, g + 1, steps, *cols(g), D, "dve1")
                        dve.wait_ge(steps[2], g + 1)
                        inv_root(None, dve, g + 1, steps, *cols(g), D, "dve2")

                    def low(n):
                        i, q = n // 2, n % 2
                        dve.wait_ge(high_out, n + 1)
                        dst = slice(i * P, (i + 1) * P)
                        dve.tensor_tensor(hL[:, 4 * q:4 * q + 4, dst],
                                          bank[n % 8][:, :].rearrange("p (k c) -> p k c", k=4),
                                          hH[:, 4 * q:4 * q + 4, dst].bitcast(F32), ALU.subtract).then_inc(low_out, 1)

                    for i in range(NT):
                        if i % per == 0:
                            roots(i // per)
                        if i == 0:
                            dve.wait_ge(g_loaded, 96 if load_x else 16)
                        if i >= 2:
                            dve.wait_ge(turned, 2 * (i - 1))
                        dve.scalar_tensor_tensor(out=xn[i % 2][:, :], in0=xin[:, i, :], scalar=r[:, i:i + 1],
                                                 in1=gB[:, :], op0=ALU.mult, op1=ALU.mult).then_inc(xn_ready, 1)
                        if i >= lag:
                            low(2 * (i - lag))
                            low(2 * (i - lag) + 1)
                    for n in range(2 * (NT - lag), 2 * NT):
                        low(n)

                @block.tensor
                def _(pe):
                    if load_x:
                        pe.wait_ge(g_loaded, 96)
                    for i in range(NT):
                        pe.wait_ge(xn_ready, i + 1)
                        for q in range(2):
                            n = 2 * i + q
                            if n >= 8:
                                pe.wait_ge(low_out, n - 7)
                            for k in range(4):
                                kt = 4 * q + k
                                last = pe.transpose(bank[n % 8][:, k * P:(k + 1) * P],
                                                    xn[i % 2][:, kt * P:(kt + 1) * P], const("ident"))
                            last.then_inc(turned, 1)

        xin = at("xin", RX, [P, NT, D])
        norm_transpose("n1", xin, w["ln_mix_g"], True, lambda sp: load_weights(sp, G["q"], stop=2),
                       lambda pool: split_weights(pool, G["q"], stop=2))

        def gla():
            la = at("la", RM, [P, GH, S])
            sr = at("sr", RM, [P, NT, 512])
            u = at("gu", RM + 16, [P, S])
            e = at("ge", RM + 20, [P, S])
            rsig = at("rsig", RM + 24, [P, 2, 512])
            q = at("gqT", RX, [P, GH, S])
            k = at("gkT", RX + 16, [P, GH, S])
            v = at("gv", RX + 32, [P, NT, 512])
            o = at("go", RX + 48, [P, NT, 512])
            sTm = [at(f"gsT{i}", RX + 64 + 2 * i, [P, GH, P]) for i in range(2)]
            ktok = at("gktok", RX + 68, [P, GH, P])
            St = at("gSt", RX + 70, [P, GH, P])
            St0 = at("gS", RM + 16, [P, GH, P])
            upd = at("gupd", RM + 18, [P, GH, P])
            wa2 = at("wa2", RX + 64, [RANK, 512])
            ba = at("ba", RX + 66, [P, GH])
            keep = at("gkeep", RM + 28, [P, S])
            lowT = at("glowT", RX + 48, [RANK, S])
            em, eb, ebm = (at(f"gem{n}", CONSTS + 13.25 + 0.125 * n, [P, GH, NT]) for n in range(3))

            small = sem("g_small")
            out_q, out_k, out_v, out_a, out_r = (sem(f"g_out_{n}") for n in "qkvar")
            a_full, u_out, neg_abs, ex1, ln1, la_out, cum_out, dev_out = (
                sem(n) for n in ("g_a_full", "g_u_out", "g_negabs", "g_exp1", "g_ln1", "g_la", "g_cum", "g_dev"))
            eplus, eminus, decayed, mids, mid_e, keep_ok, rs_ok, sr_ok = (
                sem(n) for n in ("g_eplus", "g_eminus", "g_decayed", "g_mids", "g_mid_e", "g_keep", "g_rsig", "g_sr"))
            sc_full, sc_out, kt_full, kt_out, o_full, o_out, kv_full, st_upd, st_tmp = (
                sem(n) for n in ("g_scores", "g_scores_out", "g_kturn", "g_kturn_out", "g_o", "g_o_out", "g_kv",
                                 "g_state", "g_state_tmp"))
            osq, oss, steps = sem("g_osq"), sem("g_oss"), tuple(sem("g_" + n) for n in ("mean", "ln", "exp", "newton"))
            on1, on2, on3, turned, high_out, low_out = (
                sem(n) for n in ("g_on1", "g_on2", "g_on3", "g_turned", "g_high", "g_low"))
            oH = at("goH", RX, [P, GH, S], F32R)
            oL = at("goL", RX + 16, [P, GH, S], F32R)
            sq = at("gsq", RM + 20, [P, 2, 512])
            def low(dve, t):
                cs = slice(t * P, (t + 1) * P)
                dve.tensor_tensor(oL[:, :, cs], bank[t % 2][:, :].rearrange("p (h c) -> p h c", h=GH),
                                  oH[:, :, cs].bitcast(F32), ALU.subtract).then_inc(low_out, 1)

            with nc.Block() as block:
                @block.sync
                def _(sp):
                    sp.dma_start(wa2[:, :], w["gla_w_a2"]).then_inc(small, 16)
                    with nc.allow_non_contiguous_dma(reason="512 biases onto partitions"):
                        sp.dma_start(ba[:, :], w["gla_b_a"].rearrange("(h p) -> p h", p=P)).then_inc(small, 16)
                    load_weights(sp, G["q"], start=2)
                    for g in "kvar":
                        load_weights(sp, G[g])
                    load_weights(sp, MERGE0[0][0], stop=2)

                @block.gpsimd
                def _(pool):
                    pool.memset(keep[:, :], 1.0).then_inc(keep_ok, 1)
                    pool.wait_ge(keep_ok, 1)
                    pool.memset(keep[:, :].rearrange("p (c t) -> p c t", t=P)[:, :, 0:1], 0.0).then_inc(keep_ok, 1)
                    split_weights(pool, G["q"], start=2)
                    for g in "kvar":
                        split_weights(pool, G[g])
                    split_weights(pool, MERGE0[0][0], stop=2)

                @block.tensor
                def _(pe):
                    product(pe, G["q"], hH, hL, always)
                    product(pe, G["k"], hH, hL, lambda b: pe.wait_ge(out_q, b + 1))
                    product(pe, G["v"], hH, hL, lambda b: pe.wait_ge(out_k, b + 1))
                    product(pe, G["a"], hH, hL, lambda b: pe.wait_ge(out_v, b + 1))
                    pe.wait_ge(small, 32)
                    pe.wait_ge(out_a, 2)
                    pe.wait_ge(out_v, 8)
                    for h in range(GH):
                        for half in range(2):
                            n = 2 * h + half
                            if n >= 6:
                                pe.wait_ge(u_out, n - 5)
                            pe.matmul(bank[2 + n % 6][:, :], wa2[:, h * P:(h + 1) * P],
                                      lowT[:, half * HALF:(half + 1) * HALF], start=True, stop=True).then_inc(a_full, 1)
                    pe.wait_ge(u_out, 8)
                    product(pe, G["r"], hH, hL, always)
                    pe.wait_ge(out_r, 8)
                    pe.wait_ge(decayed, 2 * GH)
                    for c in range(NT):
                        p2 = c % 2
                        cs = slice(c * P, (c + 1) * P)
                        if c >= 2:
                            pe.wait_ge(sc_out, c - 1)
                        for h in range(GH):
                            last = pe.matmul(bank[p2][:, h * P:(h + 1) * P], k[:, h, cs], q[:, h, cs],
                                             start=True, stop=True)
                        last.then_inc(sc_full, 1)
                        if c < NT - 1:
                            if c >= 2:
                                pe.wait_ge(kt_out, c - 1)
                            for h in range(GH):
                                last = pe.transpose(bank[2 + p2][:, h * P:(h + 1) * P], k[:, h, cs], const("ident"))
                            last.then_inc(kt_full, 1)
                        pe.wait_ge(sc_out, c + 1)
                        if c >= 2:
                            pe.wait_ge(o_out, c - 1)
                        if c:
                            pe.wait_ge(st_upd, c)
                        for h in range(GH):
                            hs = slice(h * P, (h + 1) * P)
                            last = pe.matmul(bank[4 + p2][:, hs], sTm[p2][:, h, :], v[:, c, hs], start=True, stop=(c == 0))
                            if c:
                                last = pe.matmul(bank[4 + p2][:, hs], q[:, h, cs], St[:, h, :], start=False, stop=True)
                        last.then_inc(o_full, 1)
                        if c < NT - 1:
                            pe.wait_ge(kt_out, c + 1)
                            if c >= 2:
                                pe.wait_ge(st_upd, c)
                            for h in range(GH):
                                hs = slice(h * P, (h + 1) * P)
                                last = pe.matmul(bank[6 + p2][:, hs], ktok[:, h, :], v[:, c, hs], start=True, stop=True)
                            last.then_inc(kv_full, 1)
                    for t in range(NT):
                        pe.wait_ge(on3, t + 1)
                        if t >= 2:
                            pe.wait_ge(low_out, t - 1)
                        for h in range(GH):
                            last = pe.transpose(bank[t % 2][:, h * P:(h + 1) * P], o[:, t, h * P:(h + 1) * P], const("ident"))
                        last.then_inc(turned, 1)

                @block.scalar
                def _(act):
                    for b in range(8):
                        wait_bank(act, G["q"], b)
                        act.copy(q[:, b // 2, (b % 2) * HALF:(b % 2 + 1) * HALF], bank[b][:, :]).then_inc(out_q, 1)
                    for b in range(8):
                        wait_bank(act, G["k"], b)
                        act.copy(k[:, b // 2, (b % 2) * HALF:(b % 2 + 1) * HALF], bank[b][:, :]).then_inc(out_k, 1)
                    for b in range(8):
                        wait_bank(act, G["v"], b)
                        act.copy(v[:, b, :], bank[b][:, :]).then_inc(out_v, 1)
                    for b in range(2):
                        wait_bank(act, G["a"], b)
                        act.copy(lowT[:, b * HALF:(b + 1) * HALF], bank[b][0:RANK, :]).then_inc(out_a, 1)
                    act.preload_act_table_set("natural_log_exp_and_others")
                    for h in range(GH):
                        act.wait_ge(neg_abs, h + 1)
                        act.activation(e[:, :], e[:, :], ACT.Exp).then_inc(ex1, 1)
                        act.wait_ge(ex1, h + 1)
                        act.activation(e[:, :], e[:, :], ACT.Ln, bias=1.0).then_inc(ln1, 1)
                    act.wait_ge(mids, 3)
                    for src, dst in ((0, em), (1, eb), (2, ebm)):
                        act.activation(dst[:, :, :], dst[:, :, :], ACT.Exp, scale=1.0 / GTEMP).then_inc(mid_e, 1)
                    for h in range(GH):
                        act.wait_ge(dev_out, h + 1)
                        act.activation(e[:, :], u[:, :], ACT.Exp, scale=1.0 / GTEMP).then_inc(eplus, 1)
                        act.wait_ge(decayed, 2 * h + 1)
                        act.activation(e[:, :], u[:, :], ACT.Exp, scale=-1.0 / GTEMP).then_inc(eminus, 1)
                    for b in range(8):
                        wait_bank(act, G["r"], b)
                        if b >= 2:
                            act.wait_ge(sr_ok, b - 1)
                        act.activation(rsig[:, b % 2, :], bank[b][:, :], ACT.Sigmoid).then_inc(rs_ok, 1)
                    for c in range(NT):
                        if c < NT - 1:
                            act.wait_ge(kt_full, c + 1)
                            if c:
                                act.wait_ge(kv_full, c)
                            act.copy(ktok[:, :, :].rearrange("p h c -> p (h c)"), bank[2 + c % 2][:, :]).then_inc(kt_out, 1)
                        act.wait_ge(o_full, c + 1)
                        act.copy(o[:, c, :], bank[4 + c % 2][:, :]).then_inc(o_out, 1)
                    act.wait_ge(steps[0], 1)
                    inv_root(act, None, 1, steps, stat[:, 0, 0:32], stat[:, 1, 0:32], stat[:, 2, 0:32], stat[:, 3, 0:32], GD, "act")
                    for t in range(NT):
                        act.wait_ge(turned, t + 1)
                        act.copy(oH[:, :, t * P:(t + 1) * P],
                                 bank[t % 2][:, :].rearrange("p (h c) -> p h c", h=GH)).then_inc(high_out, 1)

                @block.vector
                def _(dve):
                    dve.wait_ge(small, 32)
                    for h in range(GH):
                        for half in range(2):
                            n = 2 * h + half
                            dve.wait_ge(a_full, n + 1)
                            if h and not half:
                                dve.wait_ge(la_out, h)
                            dve.tensor_scalar(u[:, half * HALF:(half + 1) * HALF], bank[2 + n % 6][:, :], ba[:, h:h + 1],
                                              None, ALU.add).then_inc(u_out, 1)
                        dve.wait_ge(u_out, 2 * h + 2)
                        dve.scalar_tensor_tensor(out=e[:, :], in0=u[:, :], scalar=-1.0, in1=u[:, :],
                                                 op0=ALU.mult, op1=ALU.min).then_inc(neg_abs, 1)
                        dve.wait_ge(ln1, h + 1)
                        dve.scalar_tensor_tensor(out=la[:, h, :], in0=u[:, :], scalar=0.0, in1=e[:, :],
                                                 op0=ALU.min, op1=ALU.subtract).then_inc(la_out, 1)
                        dve.wait_ge(la_out, h + 1)
                        if h == 0:
                            dve.wait_ge(keep_ok, 2)
                        dve.tensor_tensor_scan(la[:, h, :], keep[:, :], la[:, h, :], 0.0, ALU.mult, ALU.add).then_inc(cum_out, 1)
                    dve.wait_ge(cum_out, GH)
                    lac = la[:, :, :].rearrange("p h (c t) -> p h c t", t=P)
                    dve.tensor_copy(em[:, :, :], lac[:, :, :, P // 2 - 1]).then_inc(mids, 1)
                    dve.tensor_copy(eb[:, :, :], lac[:, :, :, P - 1]).then_inc(mids, 1)
                    dve.tensor_tensor(ebm[:, :, :], lac[:, :, :, P - 1], lac[:, :, :, P // 2 - 1],
                                      ALU.subtract).then_inc(mids, 1)
                    for h in range(GH):
                        if h:
                            dve.wait_ge(eminus, h)
                        dve.tensor_tensor(u[:, :].rearrange("p (c t) -> p c t", t=P), lac[:, h, :, :],
                                          with_dim(lac[:, h, :, P // 2 - 1], 2, P), ALU.subtract).then_inc(dev_out, 1)
                        dve.wait_ge(eplus, h + 1)
                        dve.wait_ge(out_q, 8)
                        dve.scalar_tensor_tensor(out=q[:, h, :], in0=q[:, h, :], scalar=GD ** -0.5, in1=e[:, :],
                                                 op0=ALU.mult, op1=ALU.mult).then_inc(decayed, 1)
                        dve.wait_ge(eminus, h + 1)
                        dve.wait_ge(out_k, 8)
                        dve.tensor_tensor(k[:, h, :], k[:, h, :], e[:, :], ALU.mult).then_inc(decayed, 1)
                    for b in range(8):
                        dve.wait_ge(rs_ok, b + 1)
                        dve.tensor_tensor(sr[:, b, :], bank[b][:, :], rsig[:, b % 2, :], ALU.mult).then_inc(out_r, 1)
                        dve.wait_ge(out_r, b + 1)
                        dve.tensor_tensor(sr[:, b, :].rearrange("p (h d) -> p h d", h=GH),
                                          sr[:, b, :].rearrange("p (h d) -> p h d", h=GH),
                                          with_dim(gnorm[:, :], 1, GH), ALU.mult).then_inc(sr_ok, 1)
                    for i in range(2):
                        dve.memset(sTm[i][:, :, :], 0.0).then_inc(st_tmp, 1)
                    dve.wait_ge(st_tmp, 2)
                    dve.wait_ge(mid_e, 3)
                    n = 2
                    for c in range(NT):
                        dve.wait_ge(sc_full, c + 1)
                        if c >= 2:
                            dve.wait_ge(o_full, c - 1)
                        dve.copy_predicated(sTm[c % 2][:, :, :], with_dim(causal[:, :], 1, GH),
                                            bank[c % 2][:, :].rearrange("p (h t) -> p h t", h=GH)).then_inc(sc_out, 1)
                        if c == NT - 1:
                            break
                        dve.wait_ge(kv_full, c + 1)
                        kv = bank[6 + c % 2][:, :].rearrange("p (h d) -> p h d", h=GH)
                        if c == 0:
                            dve.tensor_tensor(St0[:, :, :], kv, with_dim(ebm[:, :, c], 2, P), ALU.mult).then_inc(st_tmp, 1)
                            n += 1
                        else:
                            dve.tensor_tensor(upd[:, :, :], kv, with_dim(ebm[:, :, c], 2, P), ALU.mult).then_inc(st_tmp, 1)
                            dve.tensor_tensor(St0[:, :, :], St0[:, :, :], with_dim(eb[:, :, c], 2, P), ALU.mult).then_inc(st_tmp, 1)
                            dve.wait_ge(st_tmp, n + 2)
                            dve.tensor_tensor(St0[:, :, :], St0[:, :, :], upd[:, :, :], ALU.add).then_inc(st_tmp, 1)
                            n += 3
                        dve.wait_ge(st_tmp, n)
                        if c:
                            dve.wait_ge(o_full, c + 1)
                        dve.tensor_tensor(St[:, :, :], St0[:, :, :], with_dim(em[:, :, c + 1], 2, P),
                                          ALU.mult).then_inc(st_upd, 1)
                    for t in range(NT):
                        dve.wait_ge(o_out, t + 1)
                        if t >= 2:
                            dve.wait_ge(oss, t - 1)
                        dve.tensor_tensor(sq[:, t % 2, :], o[:, t, :], o[:, t, :], ALU.mult).then_inc(osq, 1)
                        dve.wait_ge(osq, t + 1)
                        dve.tensor_reduce(stat[:, 0, 4 * t:4 * t + 4], sq[:, t % 2, :].rearrange("p (h d) -> p h d", h=GH),
                                          AX.X, ALU.add).then_inc(oss, 1)
                    dve.wait_ge(oss, NT)
                    args = (steps, stat[:, 0, 0:32], stat[:, 1, 0:32], stat[:, 2, 0:32], stat[:, 3, 0:32], GD)
                    inv_root(None, dve, 1, *args, "dve1")
                    dve.wait_ge(steps[2], 1)
                    inv_root(None, dve, 1, *args, "dve2")
                    dve.wait_ge(sr_ok, 8)
                    for t in range(NT):
                        ot = o[:, t, :].rearrange("p (h d) -> p h d", h=GH)
                        dve.tensor_tensor(ot, ot, with_dim(stat[:, 2, 4 * t:4 * t + 4], 2, GD), ALU.mult).then_inc(on1, 1)
                        dve.wait_ge(on1, t + 1)
                        dve.tensor_tensor(o[:, t, :], o[:, t, :], sr[:, t, :], ALU.mult).then_inc(on3, 1)
                        if t:
                            dve.wait_ge(high_out, t)
                            low(dve, t - 1)
                    dve.wait_ge(high_out, NT)
                    low(dve, NT - 1)

            return oH, oL

        def merge(m, oH, oL, products, following, first):
            tag = f"m{m}_"
            gate = at(tag + "gate", RX + 48, [P, 4, S])
            tmp = [at(tag + f"tmp{i}", RX + 64 + 2 * i, [P, 512]) for i in range(2)]
            gates, branches = products
            gate_out, br_out, summed = sem(tag + "gate_out"), sem(tag + "br_out"), sem(tag + "summed")
            with nc.Block() as block:
                @block.sync
                def _(sp):
                    for g in range(2):
                        load_weights(sp, gates[g], start=0 if g else 2)
                        load_weights(sp, branches[g])
                    load_weights(sp, following, stop=2)

                @block.gpsimd
                def _(pool):
                    for g in range(2):
                        split_weights(pool, gates[g], start=0 if g else 2)
                        split_weights(pool, branches[g])
                    split_weights(pool, following, stop=2)

                @block.tensor
                def _(pe):
                    for g in range(2):
                        product(pe, gates[g], hH, hL, (lambda b: pe.wait_ge(br_out, b + 1)) if g else always)
                        product(pe, branches[g], oH, oL, lambda b: pe.wait_ge(gate_out, 8 * g + b + 1))

                @block.scalar
                def _(act):
                    for g in range(2):
                        for b in range(8):
                            wait_bank(act, gates[g], b)
                            if g:
                                act.wait_ge(br_out, b + 1)
                            act.activation(gate[:, b // 2, (b % 2) * HALF:(b % 2 + 1) * HALF], bank[b][:, :],
                                           ACT.Sigmoid).then_inc(gate_out, 1)

                @block.vector
                def _(dve):
                    for g in range(2):
                        for b in range(8):
                            n = 8 * g + b
                            cols = slice((b % 2) * HALF, (b % 2 + 1) * HALF)
                            dve.wait_ge(gate_out, n + 1)
                            wait_bank(dve, branches[g], b)
                            dst = merged[:, 4 * g + b // 2, cols]
                            if first:
                                dve.tensor_tensor(dst, bank[b][:, :], gate[:, b // 2, cols], ALU.mult).then_inc(br_out, 1)
                            else:
                                dve.tensor_tensor(tmp[n % 2][:, :], bank[b][:, :], gate[:, b // 2, cols],
                                                  ALU.mult).then_inc(br_out, 1)
                                dve.wait_ge(br_out, n + 1)
                                dve.tensor_tensor(dst, dst, tmp[n % 2][:, :], ALU.add).then_inc(summed, 1)

        def stick_breaking():
            q = at("sqT", RX, [P, SH, S])
            k = at("skT", RX + 16, [P, SH, S])
            v = at("sv", RX + 32, [P, NT, 512])
            e = [at(f"se{i}", RX + 48 + 2 * i, [P, 512]) for i in range(2)]
            spl = [at(f"ssp{i}", RX + 52 + 2 * i, [P, 512]) for i in range(2)]
            spL = [at(f"sspL{i}", RX + 52 + 2 * i, [P, 512], F32R) for i in range(2)]
            spH = [at(f"sspH{i}", RX + 56 + 2 * i, [P, 512], F32R) for i in range(2)]
            a = [at(f"sa{i}", RX + 60 + 2 * i, [P, 512]) for i in range(5)]
            triR, strictR = at("striR", RX + 70, [P, P], F32R), at("sstrictR", RX + 70.5, [P, P], F32R)
            zerob = at("szerob", RX + 71, [P, P], BF16)
            oT = at("soT", RX, [P, SH, S])
            oH = at("soH", RX + 16, [P, SH, S], F32R)
            oL = at("soL", RX + 32, [P, SH, S], F32R)
            Q, K, V = SQ, SK, SV
            units = [(h, half, kb) for h in range(SH) for half in range(2) for kb in range(4 * half + 3, -1, -1)]
            first = [u for u, (h, half, kb) in enumerate(units) if kb == 4 * half + 3]
            ends = [u for u, (h, half, kb) in enumerate(units) if kb == 0]
            out_q, out_k, out_v = sem("s_out_q"), sem("s_out_k"), sem("s_out_v")
            z_full, na, ex, ln, spr, spm, sph, spl_ok, c_full, rest, arg, argm, prob, pv, o_out = (
                sem("s_" + n) for n in ("z_full", "negabs", "exp", "ln", "softplus", "softplus_diag", "softplus_high",
                                        "softplus_low", "c_full", "rest", "arg", "arg_diag", "prob", "pv", "o_out"))
            fixed, zeroed, zs_ok = sem("s_fixed"), sem("s_zero"), sem("s_scores_out")
            oh_done, ol_done = sem("s_oh"), sem("s_ol")
            scale = SD ** -0.5

            def off(u):
                h, half, kb = units[u]
                return max(0, kb - 4 * half) * P

            def diag(u):
                h, half, kb = units[u]
                return kb >= 4 * half

            ndiag = [0]
            for u in range(len(units)):
                ndiag.append(ndiag[-1] + diag(u))
            nend = [0]
            for u in range(len(units)):
                nend.append(nend[-1] + (u in ends))
            nrest = [0]
            for u in range(len(units)):
                nrest.append(nrest[-1] + (u not in ends))
            n_units = len(units)

            def free_halves(eng, u):
                if u >= 2:
                    eng.wait_ge(c_full, u - 1)
                    if nrest[u - 1]:
                        eng.wait_ge(rest, nrest[u - 1])

            with nc.Block() as block:
                @block.sync
                def _(sp):
                    load_weights(sp, Q, start=2)
                    for g in (K, V):
                        load_weights(sp, g)
                    load_weights(sp, MERGE1[0][0], stop=2)

                @block.gpsimd
                def _(pool):
                    split_weights(pool, Q, start=2)
                    for g in (K, V):
                        split_weights(pool, g)
                    pool.memset(zerob[:, :], 0.0).then_inc(zeroed, 1)
                    split_weights(pool, MERGE1[0][0], stop=2)
                    for u in range(n_units):
                        o_ = off(u)
                        pool.wait_ge(sph, u + 1)
                        free_halves(pool, u)
                        pool.tensor_tensor(spL[u % 2][:, o_:512], spl[u % 2][:, o_:512],
                                           spH[u % 2][:, o_:512].bitcast(F32), ALU.subtract).then_inc(spl_ok, 1)

                def ready_sp(eng, u):
                    if diag(u):
                        eng.wait_ge(spm, ndiag[u + 1])
                    else:
                        eng.wait_ge(spr, u + 1)

                @block.tensor
                def _(pe):
                    product(pe, Q, hH, hL, always)
                    product(pe, K, hH, hL, lambda b: pe.wait_ge(out_q, b + 1))
                    product(pe, V, hH, hL, lambda b: pe.wait_ge(out_k, b + 1))
                    pe.wait_ge(out_v, 8)

                    pe.wait_ge(fixed, 2)
                    pe.wait_ge(zeroed, 1)

                    def scores(u):
                        h, half, kb = units[u]
                        o_ = off(u)
                        if u >= 4:
                            pe.wait_ge(spr, u - 3)
                        pe.matmul(bank[u % 4][:, o_:512], k[:, h, kb * P:(kb + 1) * P],
                                  q[:, h, half * HALF + o_:(half + 1) * HALF], start=True, stop=True).then_inc(z_full, 1)

                    def sums(u):
                        o_ = off(u)
                        R = bank[4 + nend[u] % 2]
                        if u in first:
                            if nend[u] >= 2:
                                pe.wait_ge(arg, ends[nend[u] - 2] + 1)
                            pe.matmul(R, zerob[:, :], with_dim(zerob[:, :], 1, 4), start=True, stop=True)
                        pe.wait_ge(spl_ok, u + 1)
                        pe.matmul(R[:, o_:512], triR[:, :], spH[u % 2][:, o_:512], start=False, stop=True, skip_group_check=True)
                        pe.matmul(R[:, o_:512], triR[:, :], spL[u % 2][:, o_:512], start=False, stop=True,
                                  skip_group_check=True).then_inc(c_full, 1)

                    def others(u):
                        if u in ends:
                            return
                        o_ = off(u)
                        R = bank[4 + nend[u] % 2]
                        pe.wait_ge(arg, u + 1)
                        pe.matmul(R[:, o_:512], strictR[:, :], spH[u % 2][:, o_:512], start=False, stop=True, skip_group_check=True)
                        pe.matmul(R[:, o_:512], strictR[:, :], spL[u % 2][:, o_:512], start=False, stop=True,
                                  skip_group_check=True).then_inc(rest, 1)

                    def values(u):
                        h, half, kb = units[u]
                        o_ = off(u)
                        pe.wait_ge(prob, u + 1)
                        if u in first and nend[u] >= 2:
                            pe.wait_ge(o_out, nend[u] - 1)
                        last = pe.matmul(bank[6 + nend[u] % 2][:, o_:512], v[:, kb, h * P:(h + 1) * P],
                                         a[u % 5][:, o_:512], start=(u in first), stop=(kb == 0), skip_group_check=True)
                        last.then_inc(pv, 1)

                    scores(0)
                    for s in range(n_units + 4):
                        if 3 <= s < n_units + 3:
                            sums(s - 3)
                        if s + 1 < n_units:
                            scores(s + 1)
                        if s >= 4:
                            values(s - 4)
                        if 3 <= s < n_units + 3:
                            others(s - 3)

                @block.scalar
                def _(act):
                    act.copy(triR[:, :], const("tri")).then_inc(fixed, 1)
                    act.copy(strictR[:, :], const("strict")).then_inc(fixed, 1)
                    for b in range(8):
                        wait_bank(act, Q, b)
                        act.activation(q[:, b // 2, (b % 2) * HALF:(b % 2 + 1) * HALF], bank[b][:, :], ACT.Copy,
                                       scale=scale).then_inc(out_q, 1)
                    for b in range(8):
                        wait_bank(act, K, b)
                        act.copy(k[:, b // 2, (b % 2) * HALF:(b % 2 + 1) * HALF], bank[b][:, :]).then_inc(out_k, 1)
                    for b in range(8):
                        wait_bank(act, V, b)
                        act.copy(v[:, b, :], bank[b][:, :]).then_inc(out_v, 1)

                    act.preload_act_table_set("natural_log_exp_and_others")
                    def out_of_bank(u):
                        o_ = off(u)
                        act.wait_ge(z_full, u + 1)
                        if u >= 5:
                            act.wait_ge(pv, u - 4)
                        act.copy(a[u % 5][:, o_:512], bank[u % 4][:, o_:512]).then_inc(zs_ok, 1)

                    def logs(u):
                        o_ = off(u)
                        act.wait_ge(na, u + 1)
                        act.activation(e[u % 2][:, o_:512], e[u % 2][:, o_:512], ACT.Exp).then_inc(ex, 1)
                        act.wait_ge(ex, u + 1)
                        act.activation(e[u % 2][:, o_:512], e[u % 2][:, o_:512], ACT.Ln, bias=1.0).then_inc(ln, 1)

                    def high(u):
                        o_ = off(u)
                        ready_sp(act, u)
                        free_halves(act, u)
                        act.copy(spH[u % 2][:, o_:512], spl[u % 2][:, o_:512]).then_inc(sph, 1)

                    def probs(u):
                        o_ = off(u)
                        if diag(u):
                            act.wait_ge(argm, ndiag[u + 1])
                        else:
                            act.wait_ge(arg, u + 1)
                        act.activation(a[u % 5][:, o_:512], a[u % 5][:, o_:512], ACT.Exp).then_inc(prob, 1)

                    for s in range(n_units + 3):
                        if s < n_units:
                            out_of_bank(s)
                        if 2 <= s < n_units + 2:
                            high(s - 2)
                        if 1 <= s < n_units + 1:
                            logs(s - 1)
                        if s >= 3:
                            probs(s - 3)
                    for h in range(SH):
                        act.wait_ge(o_out, 2 * h + 2)
                        act.copy(oH[:, h, :], oT[:, h, :]).then_inc(oh_done, 1)

                @block.vector
                def _(dve):
                    def front(u):
                        o_ = off(u)
                        dve.wait_ge(zs_ok, u + 1)
                        if u >= 2:
                            dve.wait_ge(spr, u - 1)
                        dve.scalar_tensor_tensor(out=e[u % 2][:, o_:512], in0=bank[u % 4][:, o_:512], scalar=-1.0,
                                                 in1=a[u % 5][:, o_:512],
                                                 op0=ALU.mult, op1=ALU.min).then_inc(na, 1)

                    def softplus(u):
                        o_ = off(u)
                        dve.wait_ge(ln, u + 1)
                        free_halves(dve, u)
                        dve.scalar_tensor_tensor(out=spl[u % 2][:, o_:512], in0=bank[u % 4][:, o_:512], scalar=0.0,
                                                 in1=e[u % 2][:, o_:512], op0=ALU.max, op1=ALU.add).then_inc(spr, 1)
                        if diag(u):
                            dve.wait_ge(spr, u + 1)
                            dve.tensor_tensor(spl[u % 2][:, o_:o_ + P], spl[u % 2][:, o_:o_ + P], const("strict"),
                                              ALU.mult).then_inc(spm, 1)

                    def argument(u):
                        o_ = off(u)
                        dve.wait_ge(c_full, u + 1)
                        dve.tensor_tensor(a[u % 5][:, o_:512], a[u % 5][:, o_:512], bank[4 + nend[u] % 2][:, o_:512],
                                          ALU.subtract).then_inc(arg, 1)
                        if diag(u):
                            dve.wait_ge(arg, u + 1)
                            dve.tensor_tensor(a[u % 5][:, o_:o_ + P], a[u % 5][:, o_:o_ + P], const("strictneg"),
                                              ALU.add).then_inc(argm, 1)

                    def out(i):
                        h, half, _ = units[ends[i]]
                        dve.wait_ge(pv, ends[i] + 1)
                        dve.tensor_copy(oT[:, h, half * HALF:(half + 1) * HALF], bank[6 + i % 2][:, :]).then_inc(o_out, 1)

                    outs = 0
                    for s in range(n_units + 5):
                        if 2 <= s < n_units + 2:
                            softplus(s - 2)
                        if 3 <= s < n_units + 3:
                            argument(s - 3)
                        if s < n_units:
                            front(s)
                        if s >= 5 and (s - 5) in ends:
                            out(outs)
                            outs += 1
                    for h in range(SH):
                        dve.wait_ge(oh_done, h + 1)
                        dve.tensor_tensor(oL[:, h, :], oT[:, h, :], oH[:, h, :].bitcast(F32), ALU.subtract).then_inc(ol_done, 1)
            return oH, oL
        def nsa():
            RH_T, RH_Q, RH_K, RH_S = RH, RH + 32, RH + 48, RH + 56
            qtok = at("nq", RX, [P, NT, 512])
            kvtok = at("nkv", RX + 16, [P, NT, KVW])
            kcv = at("nkcv", RX + 25, [P, S])
            kc2, vc2 = at("nkc2", RX + 29, [P, S]), at("nvc2", RX + 33, [P, S])
            sqt = at("nsqt", RX + 37, [P, 512])
            gC = at("ngateC", RX + 40, [P, KT, S])
            onehot, urev = at("nonehot", RX + 42, [33, REV]), at("nurev", RX + 48, [NH, REV + 1])
            relb = at("nrelb", RX + 41, [33, NH])
            rel_in, rel_neg, rel_full, rel_out, rel_put = (sem("n_rel_" + n) for n in ("in", "neg", "full", "out", "put"))
            out_q, out_cv, out_kv, moved, out_gc = (sem("n_out_" + n) for n in ("q", "cv", "kv", "moved", "gc"))
            sq_a, sq_b, qn1, qn2, kn1, kn2 = (sem("n_" + n) for n in ("sq", "sumsq", "qn1", "qn2", "kn1", "kn2"))
            steps = tuple(sem("na_" + n) for n in ("mean", "ln", "exp", "newton"))
            steps2 = tuple(sem("nb_" + n) for n in ("mean", "ln", "exp", "newton"))
            q4 = qtok[:, :, :].rearrange("p t (h d) -> p t h d", h=NH)
            qstat = [stat[:, n, 0:64] for n in range(4)]
            kstat = [stat[:, 4 + n, 0:16] for n in range(4)]
            with nc.Block() as block:
                @block.sync
                def _(sp):
                    sp.dma_start(relb[0:32, :], w["rel_bias"]).then_inc(rel_in, 16)
                    sp.dma_start(onehot[:, :], w["onehot"]).then_inc(rel_in, 16)
                    load_weights(sp, NQ, start=2)
                    for g in (CV, KV):
                        load_weights(sp, g)
                    sp.wait_ge(rel_out, 3)
                    sp.dma_start(w["bias_rev"][:, 0:REV], urev[:, 0:REV]).then_inc(rel_put, 16)
                    sp.wait_ge(out_cv, 2)
                    sp.dma_start(kc2[0:64, :], kcv[0:64, :]).then_inc(moved, 16)
                    sp.dma_start(kc2[64:128, 0:S - 1], kcv[0:64, 1:S]).then_inc(moved, 16)
                    sp.dma_start(vc2[0:64, :], kcv[64:128, :]).then_inc(moved, 16)
                    sp.dma_start(vc2[64:128, 0:S - 1], kcv[64:128, 1:S]).then_inc(moved, 16)
                    for g in GC:
                        load_weights(sp, g)
                    sp.wait_ge(moved, 64)
                    sp.wait_ge(rel_put, 16)

                @block.gpsimd
                def _(pool):
                    pool.memset(relb[32:33, :], NEG).then_inc(rel_neg, 1)
                    pool.wait_ge(rel_neg, 1)
                    split_weights(pool, NQ, start=2)
                    for g in [CV, KV] + GC:
                        split_weights(pool, g)

                @block.tensor
                def _(pe):
                    product(pe, NQ, hH, hL, always)
                    pe.wait_ge(rel_in, 32)
                    pe.wait_ge(rel_neg, 1)
                    for n in range(3):
                        a, b = n * 512, min(REV, n * 512 + 512)
                        pe.wait_ge(out_q, n + 3)
                        pe.matmul(bank[2 + n][0:NH, 0:b - a], relb[:, :], onehot[:, a:b], start=True, stop=True).then_inc(rel_full, 1)
                    product(pe, CV, hH, hL, always)
                    product(pe, KV, hH, hL, lambda b: pe.wait_ge(out_cv, b + 1) if b < 2 else
                            pe.wait_ge(rel_out, b - 1) if b < 5 else pe.wait_ge(out_q, b + 1))
                    product(pe, GC[0], hH, hL, lambda b: pe.wait_ge(out_kv, b + 1))
                    product(pe, GC[1], hH, hL, lambda b: pe.wait_ge(out_gc, b + 1))

                @block.scalar
                def _(act):
                    for b in range(8):
                        wait_bank(act, NQ, b)
                        act.copy(qtok[:, b, :], bank[b][:, :]).then_inc(out_q, 1)
                    for n in range(3):
                        a, b = n * 512, min(REV, n * 512 + 512)
                        act.wait_ge(rel_full, n + 1)
                        act.copy(urev[:, a:b], bank[2 + n][0:NH, 0:b - a]).then_inc(rel_out, 1)
                    for b in range(2):
                        wait_bank(act, CV, b)
                        act.copy(kcv[:, b * HALF:(b + 1) * HALF], bank[b][:, :]).then_inc(out_cv, 1)
                    for b in range(8):
                        wait_bank(act, KV, b)
                        act.copy(kvtok[:, b, :], bank[b][:, 0:KVW]).then_inc(out_kv, 1)
                    act.wait_ge(steps[0], 1)
                    inv_root(act, None, 1, steps, *qstat, ND, "act")
                    act.wait_ge(steps2[0], 1)
                    inv_root(act, None, 1, steps2, *kstat, ND, "act")
                    act.wait_ge(rel_put, 16)
                    act.activation(gatef[:, :, :], kvtok[:, :, 256:280], ACT.Sigmoid)
                    for g in range(2):
                        for b in range(8):
                            wait_bank(act, GC[g], b)
                            act.activation(gC[:, 4 * g + b // 2, (b % 2) * HALF:(b % 2 + 1) * HALF], bank[b][:, :],
                                           ACT.Sigmoid).then_inc(out_gc, 1)

                @block.vector
                def _(dve):
                    for t in range(NT):
                        dve.wait_ge(out_q, t + 1)
                        if t:
                            dve.wait_ge(sq_b, t)
                        dve.tensor_tensor(sqt[:, :], qtok[:, t, :], qtok[:, t, :], ALU.mult).then_inc(sq_a, 1)
                        dve.wait_ge(sq_a, t + 1)
                        dve.tensor_reduce(qstat[0][:, 8 * t:8 * t + 8], sqt[:, :].rearrange("p (h d) -> p h d", h=NH),
                                          AX.X, ALU.add).then_inc(sq_b, 1)
                    dve.wait_ge(sq_b, NT)
                    inv_root(None, dve, 1, steps, *qstat, ND, "dve1")
                    n = NT
                    for t in range(NT):
                        for k in range(2):
                            dve.wait_ge(out_kv, t + 1)
                            dve.wait_ge(sq_b, n)
                            src = kvtok[:, t, 128 * k:128 * k + 64]
                            dve.tensor_tensor(sqt[:, 0:64], src, src, ALU.mult).then_inc(sq_a, 1)
                            n += 1
                            dve.wait_ge(sq_a, n)
                            dve.tensor_reduce(kstat[0][:, 2 * t + k:2 * t + k + 1], sqt[:, 0:64], AX.X, ALU.add).then_inc(sq_b, 1)
                    dve.wait_ge(sq_b, n)
                    inv_root(None, dve, 1, steps2, *kstat, ND, "dve1")
                    dve.wait_ge(steps[2], 1)
                    inv_root(None, dve, 1, steps, *qstat, ND, "dve2")
                    for t in range(NT):
                        dve.tensor_tensor(q4[:, t, :, :], q4[:, t, :, :],
                                          with_dim(qstat[2][:, 8 * t:8 * t + 8], 2, ND), ALU.mult).then_inc(qn1, 1)
                        dve.wait_ge(qn1, t + 1)
                        dve.scalar_tensor_tensor(out=q4[:, t, :, :], in0=q4[:, t, :, :], scalar=ND ** -0.5,
                                                 in1=with_dim(qgain[:, :], 1, NH), op0=ALU.mult, op1=ALU.mult).then_inc(qn2, 1)
                    dve.wait_ge(steps2[2], 1)
                    inv_root(None, dve, 1, steps2, *kstat, ND, "dve2")
                    for t in range(NT):
                        for k in range(2):
                            src = kvtok[:, t, 128 * k:128 * k + 64]
                            dve.scalar_tensor_tensor(out=src, in0=src, scalar=kstat[2][:, 2 * t + k:2 * t + k + 1],
                                                     in1=kgain[:, :], op0=ALU.mult, op1=ALU.mult).then_inc(kn2, 1)

            Tt = at("nT", RH_T, [P, NH, S])
            kH = [at("nksH", RH_Q, [P, S], F32R), at("nkwH", RH_Q + 8, [P, S], F32R)]
            kL = [at("nksL", RH_Q + 4, [P, S], F32R), at("nkwL", RH_Q + 12, [P, S], F32R)]
            kraw = [at(f"nkraw{i}", RH + 56 + i, [64, 2, P]) for i in range(2)]
            w1 = [at("nw1k", RH_T, [P, 16, CMP_HID]), at("nw1v", RH_T + 16, [P, 16, CMP_HID])]
            flipped = [at(f"nflip{i}", RING + 8 * i, [P, 2, S]) for i in range(2)]
            blk = [at(f"nblk{i}", RING + 16 + 4 * i, [P, 16, NCMP]) for i in range(2)]
            w2 = [at(f"nw2{i}", RX + 37 + 0.5 * i, [P, 2, ND]) for i in range(2)]
            pe2 = [at(f"npe{i}", RX + 38 + 0.0625 * i, [P, 16]) for i in range(2)]
            RP = RH + 48
            hx, hu, hg = (at(f"nhid{i}", RP + i, [P, 4, NCMP]) for i in range(3))
            kcr, kcd = at("nkcr", RP + 3, [NCMP, ND]), at("nkcd", RP + 3.25, [NCMP, ND])
            vcn = at("nvcn", RX + 38.25, [NCMP, ND])
            kcH, kcL = at("nkcH", RX + 38.5, [P, 64], F32R), at("nkcL", RX + 38.75, [P, 64], F32R)
            kcraw = at("nkcraw", RP + 3.5, [64, 64])
            expandb = at("nexpandb", RX + 25, [NSEL, S], BF16)
            expandf = at("nexpandf", RP + 4, [NSEL, S])
            k_in = [sem(f"n_w1_in{i}") for i in range(2)]
            ex_in, tt_in = sem("n_expand_in"), [sem("n_table_in0"), sem("n_table_in1")]
            tt_full, tt_out = sem("n_table_full"), sem("n_table_out")
            blk_ok, hid_full, hx_ok, hs1, hs2, hs3, hsig, hg_ok, kc_full, kcs = (
                sem("n_" + n) for n in ("blk", "hid_full", "hx", "hs1", "hs2", "hs3", "hsig", "hg", "kc_full", "kcs"))
            kc_ok, kct_full, kct_out, tfull, tout, casts, ksplit = (
                sem("n_" + n) for n in ("kc_ok", "kct_full", "kct_out", "tfull", "tout", "casts", "ksplit"))
            steps3 = tuple(sem("nc_" + n) for n in ("mean", "ln", "exp", "newton"))
            cstat = [stat[0:NCMP, n, 0:1] for n in range(4)]

            def skew(h0, h1):
                return bass.AP(w["bias_rev"].tensor, h0 * (REV + 1), [[1, P], [REV + 1, h1 - h0], [1, S]])

            with nc.Block() as block:
                @block.sync
                def _(sp):
                    sp.dma_start(w1[0][:, :, :], w["nsa_wk1"].rearrange("(m q) n -> q m n", q=P)).then_inc(k_in[0], 16)
                    with nc.allow_non_contiguous_dma(reason="2048 positional terms onto partitions"):
                        for i, src in enumerate(("nsa_pe_k", "nsa_pe_v")):
                            sp.dma_start(pe2[i][:, :], w[src].rearrange("(m p) d -> (p d) m", p=2)).then_inc(k_in[0], 16)
                    for i, src in enumerate(("nsa_wk2", "nsa_wv2")):
                        sp.dma_start(w2[i][:, :, :], w[src].rearrange("(j p) d -> p j d", p=P)).then_inc(k_in[0], 16)
                    sp.dma_start(w1[1][:, :, :], w["nsa_wv1"].rearrange("(m q) n -> q m n", q=P)).then_inc(k_in[1], 16)
                    sp.dma_start(expandf[:, :], w["expand"]).then_inc(ex_in, 16)
                    for g in range(4):
                        if g >= 2:
                            sp.wait_ge(tt_full, 4 * (g - 1))
                        sp.dma_start(flipped[g % 2][:, :, :], skew(2 * g, 2 * g + 2)).then_inc(tt_in[g % 2], 16)

                @block.tensor
                def _(pe):
                    for t in range(NT):
                        if t >= 2:
                            pe.wait_ge(tout, t - 1)
                        for j in range(2):
                            last = pe.transpose(bank[t % 2][0:64, j * P:(j + 1) * P],
                                                kvtok[:, t, 128 * j:128 * j + 64], const("ident"))
                        last.then_inc(tfull, 1)
                    pe.wait_ge(k_in[0], 80)
                    for i in range(2):
                        if i:
                            pe.wait_ge(k_in[1], 16)
                        pe.wait_ge(blk_ok, i + 1)
                        for j in range(2):
                            c0 = (2 * i + j) * NCMP
                            for m in range(16):
                                last = pe.matmul(bank[2][:, c0:c0 + NCMP], w1[i][:, m, j * P:(j + 1) * P], blk[i][:, m, :],
                                                 start=(m == 0), stop=(m == 15))
                        last.then_inc(hid_full, 1)
                    for g in range(4):
                        pe.wait_ge(tt_in[g % 2], 16 * (g // 2 + 1))
                        for j in range(4):
                            n = 4 * g + j
                            if n >= 2:
                                pe.wait_ge(tt_out, n - 1)
                            pe.matmul(bank[5 + n % 2][:, :], const("flip"), flipped[g % 2][:, j // 2, (j % 2) * 512:(j % 2 + 1) * 512],
                                      start=True, stop=True).then_inc(tt_full, 1)
                    pe.wait_ge(hg_ok, 1)
                    for i in range(2):
                        for j in range(2):
                            last = pe.matmul(bank[3][0:NCMP, i * ND:(i + 1) * ND], hg[:, 2 * i + j, :], w2[i][:, j, :],
                                             start=(j == 0), stop=(j == 1))
                    last.then_inc(kc_full, 1)
                    pe.wait_ge(kc_ok, 1)
                    pe.transpose(bank[4][0:64, 0:NCMP], kcd[:, :], const("ident", NCMP)[:, 0:NCMP]).then_inc(kct_full, 1)

                @block.scalar
                def _(act):
                    for t in range(NT):
                        act.wait_ge(tfull, t + 1)
                        if t >= 2:
                            act.wait_ge(ksplit, 8 * (t - 1))
                        act.copy(kraw[t % 2][:, :, :], bank[t % 2][0:64, 0:2 * P].rearrange("p (j c) -> p j c", j=2)).then_inc(tout, 1)
                    act.wait_ge(hs3, 1)
                    act.activation(hu[:, :, :], hu[:, :, :], ACT.Sigmoid, scale=2 * 0.7978845608028654).then_inc(hsig, 1)
                    act.wait_ge(kc_full, 1)
                    act.copy(vcn[:, :], bank[3][0:NCMP, ND:2 * ND])
                    act.copy(kcr[:, :], bank[3][0:NCMP, 0:ND]).then_inc(kcs, 1)
                    act.wait_ge(steps3[0], 1)
                    inv_root(act, None, 1, steps3, *cstat, ND, "act")
                    act.wait_ge(kct_full, 1)
                    act.copy(kcraw[:, 0:NCMP], bank[4][0:64, 0:NCMP]).then_inc(kct_out, 1)
                    act.wait_ge(ex_in, 16)
                    act.copy(expandb[:, :], expandf[:, :])
                    act.copy(identb[:, :], const("ident"))
                    act.copy(windowb[:, :], const("window"))

                @block.vector
                def _(dve):
                    def stack(raw, high, low, done, n):
                        dve.tensor_copy(high[0:64], raw).then_inc(done, 1)
                        dve.tensor_copy(high[64:128], raw).then_inc(done, 1)
                        dve.wait_ge(done, n + 1)
                        dve.tensor_tensor(low[0:64], raw, high[0:64].bitcast(F32), ALU.subtract).then_inc(done, 1)
                        dve.tensor_tensor(low[64:128], raw, high[0:64].bitcast(F32), ALU.subtract).then_inc(done, 1)

                    dve.wait_ge(k_in[0], 80)
                    for i, src in enumerate((kc2, vc2)):
                        row = src[:, :].ap[0][0]
                        win = bass.AP(src[:, :].tensor, src[:, :].offset, [[row, P], [2, 16], [CMP_STRIDE, NCMP]])
                        dve.tensor_tensor(blk[i][:, :, :], win, with_dim(pe2[i][:, :], 2, NCMP), ALU.add).then_inc(blk_ok, 1)
                    for t in range(NT):
                        dve.wait_ge(tout, t + 1)
                        for j in range(2):
                            cs = slice(t * P, (t + 1) * P)
                            stack(kraw[t % 2][:, j, :], kH[j][:, cs], kL[j][:, cs], ksplit, 8 * t + 4 * j)
                    dve.memset(kcraw[:, NCMP:64], 0.0).then_inc(hs1, 1)
                    dve.wait_ge(hs1, 1)
                    dve.wait_ge(hid_full, 2)
                    dve.tensor_copy(hx[:, :, :].rearrange("p a n -> p (a n)"), bank[2][:, 0:4 * NCMP]).then_inc(hx_ok, 1)
                    dve.wait_ge(hx_ok, 1)
                    dve.tensor_tensor(hu[:, :, :], hx[:, :, :], hx[:, :, :], ALU.mult).then_inc(hs1, 1)
                    dve.wait_ge(hs1, 2)
                    dve.tensor_scalar(hu[:, :, :], hu[:, :, :], 0.044715, 1.0, ALU.mult, ALU.add).then_inc(hs2, 1)
                    dve.wait_ge(hs2, 1)
                    dve.tensor_tensor(hu[:, :, :], hu[:, :, :], hx[:, :, :], ALU.mult).then_inc(hs3, 1)
                    dve.wait_ge(hsig, 1)
                    dve.tensor_tensor(hg[:, :, :], hx[:, :, :], hu[:, :, :], ALU.mult).then_inc(hg_ok, 1)
                    for n in range(16):
                        dve.wait_ge(tt_full, n + 1)
                        dve.tensor_copy(Tt[:, n // 2, (n % 2) * 512:(n % 2 + 1) * 512], bank[5 + n % 2][:, :]).then_inc(tt_out, 1)
                    dve.wait_ge(kcs, 1)
                    dve.tensor_tensor(kcd[:, :], kcr[:, :], kcr[:, :], ALU.mult).then_inc(hx_ok, 1)
                    dve.wait_ge(hx_ok, 2)
                    dve.tensor_reduce(cstat[0], kcd[:, :], AX.X, ALU.add).then_inc(hx_ok, 1)
                    dve.wait_ge(hx_ok, 3)
                    inv_root(None, dve, 1, steps3, *cstat, ND, "dve1")
                    dve.wait_ge(steps3[2], 1)
                    inv_root(None, dve, 1, steps3, *cstat, ND, "dve2")
                    dve.scalar_tensor_tensor(out=kcd[:, :], in0=kcr[:, :], scalar=cstat[2], in1=kgain[0:NCMP, :],
                                             op0=ALU.mult, op1=ALU.mult).then_inc(kc_ok, 1)
                    dve.wait_ge(kct_out, 1)
                    stack(kcraw[:, :], kcH[:, :], kcL[:, :], casts, 0)

            sB = [at(f"nsB{i}", x, [P, S]) for i, x in enumerate((RH + 48, RH + 52, RH + 56, RING + 20))]
            qraw = [at(f"nqraw{i}", RH + 60 + 2 * i, [64, 4, P]) for i in range(2)]
            pT = [at(f"npT{i}", RX + 27 + 4 * i, [P, 8, P]) for i in range(2)]
            qS = [at(f"nqS{i}", RING + 4 * i, [P, NH, P], F32R) for i in range(2)]
            pTc = [at(f"npTc{i}", RING + 8 + 4 * i, [64, NH, P]) for i in range(2)]
            gt, eq = at("ngt", RING + 16, [P, NSEL, NSEL]), at("neq", RING + 17, [P, NSEL, NSEL])
            impp = at("nimp", RING + 18, [P, 72])
            bscore, pen = at("nbscore", RING + 18.375, [P, NSEL]), at("npen", RING + 18.5, [P, NSEL])
            penT = [at(f"npenT{i}", RING + 18.625 + 0.25 * i, [NSEL, P], BF16) for i in range(2)]
            small_ = [at(f"nsmall{i}", RING + 19.25 + 0.0625 * i, [P, 8]) for i in range(10)]
            nmax, rows = small_[0:4], small_[4:8]
            cmx, csm = small_[8], small_[9]
            diag = [at(f"ndiag{i}", RX + 35 + 0.5 * i, [P, P]) for i in range(4)]
            oT = at("noT", RX, [P, NT, 4, P])
            units = [("cmp", 0, 0)]
            for c in range(NT):
                for h in range(NH):
                    units += [("win", c, h), ("slc", c, h)]
                    if h == 2 and c + 1 < NT:
                        units.append(("cmp", c + 1, 0))
            N = len(units)
            AHEAD = 3

            def ncmp(c):
                return min(NCMP, 8 * c + 7)

            def keys(u):
                kind, c, h = units[u]
                k0 = max(0, c - 4) if kind == "win" else 0
                return k0, c + 1 - k0

            uses = [(-1, "q", 0, 0, 4), (-1, "q", 0, 4, 4)]
            for s in range(N + AHEAD):
                u = s - AHEAD
                if 0 <= u < N:
                    kind, c, h = units[u]
                    if kind == "cmp":
                        uses += [(s, "cmp", u, 0, 4), (s, "cmp", u, 4, 4)]
                    else:
                        nk = keys(u)[1]
                        uses += [(s, "p", u, a, min(4, nk - a)) for a in range(0, nk, 4)]
                        if kind == "win" and h == 0 and c + 1 < NT:
                            uses += [(s, "q", c + 1, 0, 4), (s, "q", c + 1, 4, 4)]
                        if kind == "win" and h == 5 and 4 <= c + 1 < NT:
                            uses.append((s, "pen", c + 1, 0, 1))
            use_of = {}
            for n, x in enumerate(uses):
                use_of[x[1], x[2]] = n + 1
            scores_full, add_out, max_out, exp_out, scaled, cmp_p, t_full, t_out, pv, o_out, q_split, q_low = (
                sem("n_" + n) for n in ("scores", "biased", "rowmax", "exp", "scaled", "cmp_p", "turned", "turn_out", "pv",
                                        "o_out", "q_high", "q_low"))
            chain, impz, pen_ok, pre_exp = (sem("n_" + n) for n in ("chain", "impz", "pen", "cmp_biased"))
            ncmp_before = [sum(1 for v in range(u) if units[v][0] == "cmp") for u in range(N + 1)]
            last_of_tile = {c: max(u for u in range(N) if units[u][1] == c and units[u][0] != "cmp") for c in range(NT)}
            pair = [pairs[0], pairs[1]]

            def table(c, h, k0, nk):
                a = S - P - P * c + P * k0
                return Tt[:, h, a:a + nk * P]

            with nc.Block() as block:
                @block.tensor
                def _(pe):
                    def scores(u):
                        kind, c, h = units[u]
                        if u >= 2:
                            pe.wait_ge(add_out, u - 1)
                        if kind == "cmp":
                            n = ncmp(c) + 1
                            pe.wait_ge(q_low, 2 * c + 2)
                            for h in range(NH):
                                dst = pair[u % 2][:, h * 64:h * 64 + n]
                                pe.matmul(dst, qS[c % 2][:, h, :], kcH[:, 0:n], start=True, stop=False)
                                last = pe.matmul(dst, qS[c % 2][:, h, :], kcL[:, 0:n], start=False, stop=True)
                            last.then_inc(scores_full, 1)
                            return
                        k0, nk = keys(u)
                        ks_ = 1 if kind == "win" else 0
                        if kind == "slc" and c >= 4 and h == 0:
                            pe.wait_ge(t_out, use_of["pen", c])
                        for a in range(0, nk, 4):
                            m = min(4, nk - a)
                            dst = pair[u % 2][:, a * P:(a + m) * P]
                            cols = slice((k0 + a) * P, (k0 + a + m) * P)
                            chosen = kind == "slc" and c >= 4
                            pe.matmul(dst, qS[c % 2][:, h, :], kH[ks_][:, cols], start=True, stop=False)
                            last = pe.matmul(dst, qS[c % 2][:, h, :], kL[ks_][:, cols], start=False, stop=not chosen)
                            if chosen:
                                last = pe.matmul(dst, penT[c % 2][:, :], expandb[:, cols], start=False, stop=True)
                            elif kind == "win" and c >= 4 and a == 0:
                                last = pe.matmul(pair[u % 2][:, 0:P], identb[:, :], windowb[:, :], start=False, stop=True,
                                                 skip_group_check=True)
                        last.then_inc(scores_full, 1)

                    def values(u):
                        kind, c, h = units[u]
                        if kind == "cmp":
                            return
                        if kind == "win" and h == 0 and c >= 2:
                            pe.wait_ge(o_out, c - 1)
                        dst = bank[6 + c % 2][64 * (h % 2):64 * (h % 2) + 64, (h // 2) * P:(h // 2 + 1) * P]
                        k0, nk = keys(u)
                        at_ = 64 if kind == "slc" else 192
                        if kind == "win":
                            if h == 0:
                                pe.wait_ge(t_out, use_of["cmp", units.index(("cmp", c, 0))])
                            n = ncmp(c)
                            pe.matmul(dst, vcn[0:n, :], pTc[c % 2][0:n, h, :], start=True, stop=False)
                        pe.wait_ge(t_out, use_of["p", u])
                        for a in range(nk):
                            last = pe.matmul(dst, kvtok[:, k0 + a, at_:at_ + ND], pT[u % 2][:, a, :],
                                             start=False, stop=(kind == "slc" and a == nk - 1))
                        last.then_inc(pv, 1)

                    n = 0
                    for s in range(-1, N + AHEAD + 1):
                        if 0 <= s < N:
                            scores(s)
                        while n < len(uses) and uses[n][0] == s:
                            _, what, u, a, m = uses[n]
                            if n >= 2:
                                pe.wait_ge(t_out, n - 1)
                            tb = bank[4 + n % 2]
                            if what == "cmp":
                                pe.wait_ge(cmp_p, ncmp_before[u + 1])
                                k = ncmp(units[u][1])
                                for j in range(4):
                                    last = pe.transpose(tb[0:k, j * P:(j + 1) * P],
                                                        sB[u % 4][:, (a + j) * 64:(a + j) * 64 + k], const("ident"))
                            elif what == "p":
                                pe.wait_ge(scaled, u + 1 - ncmp_before[u + 1])
                                for j in range(m):
                                    last = pe.matmul(tb[:, j * P:(j + 1) * P], sB[u % 4][:, (a + j) * P:(a + j + 1) * P],
                                                     diag[u % 4][:, :], start=True, stop=True)
                            elif what == "pen":
                                pe.wait_ge(pen_ok, u - 3)
                                last = pe.transpose(tb[0:NSEL, 0:P], pen[:, :], const("ident"))
                            else:
                                for j in range(4):
                                    last = pe.transpose(tb[0:64, j * P:(j + 1) * P],
                                                        qtok[:, u, (a + j) * ND:(a + j + 1) * ND], const("ident"))
                            last.then_inc(t_full, 1)
                            n += 1
                        if 0 <= s - AHEAD - 1 < N:
                            values(s - AHEAD - 1)

                def nth(u):
                    return u - ncmp_before[u]

                @block.scalar
                def _(act):
                    n = 0
                    for s in range(-1, N + AHEAD + 2):
                        while n < len(uses) and uses[n][0] == s:
                            _, what, u, a, m = uses[n]
                            act.wait_ge(t_full, n + 1)
                            tb = bank[4 + n % 2]
                            if what == "cmp":
                                c = units[u][1]
                                k = ncmp(c)
                                if c >= 2:
                                    act.wait_ge(pv, nth(last_of_tile[c - 2]) + 1)
                                act.copy(pTc[c % 2][0:k, a:a + 4, :], tb[0:k, :].rearrange("p (j c) -> p j c", j=4)).then_inc(t_out, 1)
                            elif what == "p":
                                prev = [v for v in range(u) if units[v][0] != "cmp" and v % 2 == u % 2]
                                if prev:
                                    act.wait_ge(pv, nth(prev[-1]) + 1)
                                act.copy(pT[u % 2][:, a:a + m, :],
                                         tb[:, 0:m * P].rearrange("p (j c) -> p j c", j=m)).then_inc(t_out, 1)
                            elif what == "pen":
                                act.copy(penT[u % 2][:, :], tb[0:NSEL, 0:P]).then_inc(t_out, 1)
                            else:
                                if u:
                                    act.wait_ge(q_low, 2 * u + a // 4 - 1)
                                act.copy(qraw[a // 4][:, :, :], tb[0:64, :].rearrange("p (j c) -> p j c", j=4)).then_inc(t_out, 1)
                            n += 1
                        done_ = [c for c in range(NT) if last_of_tile[c] == s - AHEAD - 2]
                        if done_:
                            c = done_[0]
                            act.wait_ge(pv, nth(last_of_tile[c]) + 1)
                            act.copy(oT[:, c, :, :], bank[6 + c % 2][:, :].rearrange("p (j c) -> p j c", j=4)).then_inc(o_out, 1)
                        if 0 <= s < N:
                            kind, c, h = units[s]
                            if kind == "cmp":
                                k = ncmp(c)
                                act.wait_ge(pre_exp, ncmp_before[s + 1])
                                v = sB[s % 4][:, 0:512].rearrange("p (h n) -> p h n", h=NH)[:, :, 0:k]
                                act.activation(v, v, ACT.Exp).then_inc(exp_out, 1)
                            else:
                                nk = keys(s)[1]
                                act.wait_ge(max_out, nth(s) + 1)
                                v = sB[s % 4][:, 0:nk * P]
                                act.activation(v, v, ACT.Exp, bias=nmax[s % 4][:, 0:1],
                                               accum_out=rows[s % 4][:, 0:1]).then_inc(exp_out, 1)

                @block.vector
                def _(dve):
                    count = [0]

                    def link(ins):
                        count[0] += 1
                        ins.then_inc(chain, 1)
                        dve.wait_ge(chain, count[0])

                    def head_view(u, k):
                        return sB[u % 4][:, 0:512].rearrange("p (h n) -> p h n", h=NH)[:, :, 0:k]

                    def front(u):
                        kind, c, h = units[u]
                        dve.wait_ge(scores_full, u + 1)
                        if kind == "cmp":
                            k = ncmp(c)
                            v = head_view(u, k)
                            a = S - P - P * c + CMP_BLOCK - 1
                            full = Tt[:, :, :]
                            bias = bass.AP(full.tensor, full.offset + a, [list(full.ap[0]), [S, NH], [CMP_STRIDE, k]])
                            dve.tensor_tensor(v, pair[u % 2][:, 0:512].rearrange("p (h n) -> p h n", h=NH)[:, :, 0:k], bias,
                                              ALU.add).then_inc(add_out, 1)
                            dve.wait_ge(add_out, u + 1)
                            link(dve.tensor_reduce(cmx[:, :], v, AX.X, ALU.max))
                            link(dve.tensor_scalar(cmx[:, :], cmx[:, :], -1e20, None, ALU.max))
                            dve.tensor_tensor(v, v, with_dim(cmx[:, :], 2, k), ALU.subtract).then_inc(pre_exp, 1)
                            return
                        k0, nk = keys(u)
                        v = sB[u % 4][:, 0:nk * P]
                        dve.tensor_tensor(v, pair[u % 2][:, 0:nk * P], table(c, h, k0, nk), ALU.add).then_inc(add_out, 1)
                        dve.wait_ge(add_out, u + 1)
                        dve.tensor_reduce(nmax[u % 4][:, 0:1], v, AX.X, ALU.max, negate=True).then_inc(max_out, 1)

                    def scale(u):
                        kind, c, h = units[u]
                        dve.wait_ge(exp_out, u + 1)
                        link(dve.reciprocal(rows[u % 4][:, 0:1], rows[u % 4][:, 0:1]))
                        g = 3 * h + (2 if kind == "win" else 1)
                        dve.tensor_scalar(diag[u % 4][:, :], const("ident"), rows[u % 4][:, 0:1], gatef[:, c, g:g + 1], ALU.mult, ALU.mult).then_inc(scaled, 1)

                    def cmp_normal(u):
                        c = units[u][1]
                        k = ncmp(c)
                        v = head_view(u, k)
                        dve.wait_ge(exp_out, u + 1)
                        link(dve.tensor_reduce(csm[:, :], v, AX.X, ALU.add))
                        link(dve.tensor_scalar(csm[:, :], csm[:, :], 1e-30, None, ALU.max))
                        link(dve.reciprocal(csm[:, :], csm[:, :]))
                        link(dve.tensor_tensor(v, v, with_dim(csm[:, :], 2, k), ALU.mult))
                        if c >= 4:
                            link(dve.tensor_reduce(impp[:, 1:1 + k], v.rearrange("p h n -> p n h"), AX.X, ALU.add))
                        gate = gatef[:, c, :].rearrange("p (h b) -> p h b", b=3)[:, :, 0]
                        dve.tensor_tensor(v, v, with_dim(gate, 2, k), ALU.mult).then_inc(cmp_p, 1)

                    def choose(c):
                        full = impp[:, :]
                        win = bass.AP(full.tensor, full.offset, [list(full.ap[0]), [4, NSEL], [1, 5]])
                        link(dve.tensor_reduce(bscore[:, :], win, AX.X, ALU.add))
                        link(dve.tensor_tensor(bscore[:, :], bscore[:, :], const("selbase")[:, c * NSEL:(c + 1) * NSEL], ALU.add))
                        sj, si = with_dim(bscore[:, :], 1, NSEL), with_dim(bscore[:, :], 2, NSEL)
                        dve.tensor_tensor(gt[:, :, :], sj, si, ALU.is_gt).then_inc(impz, 1)
                        link(dve.tensor_tensor(eq[:, :, :], sj, si, ALU.is_equal))
                        link(dve.tensor_tensor(eq[:, :, :].rearrange("p a b -> p (a b)"), eq[:, :, :].rearrange("p a b -> p (a b)"),
                                               const("tie"), ALU.mult))
                        dve.wait_ge(impz, c - 4 + 2)
                        link(dve.tensor_tensor(gt[:, :, :], gt[:, :, :], eq[:, :, :], ALU.add))
                        link(dve.tensor_reduce(pen[:, :], gt[:, :, :], AX.X, ALU.add))
                        dve.tensor_scalar(pen[:, :], pen[:, :], TOPN - 0.5, NEG, ALU.is_gt, ALU.mult).then_inc(pen_ok, 1)

                    def split_queries(c):
                        for g in range(2):
                            dve.wait_ge(t_out, use_of["q", c] - 1 + g)
                            hs = slice(4 * g, 4 * g + 4)
                            dve.tensor_copy(qS[c % 2][0:64, hs, :], qraw[g][:, :, :]).then_inc(q_split, 1)
                            dve.wait_ge(q_split, 2 * c + g + 1)
                            dve.tensor_tensor(qS[c % 2][64:128, hs, :], qraw[g][:, :, :], qS[c % 2][0:64, hs, :].bitcast(F32),
                                              ALU.subtract).then_inc(q_low, 1)

                    dve.memset(impp[:, :], 0.0).then_inc(impz, 1)
                    dve.wait_ge(impz, 1)
                    split_queries(0)
                    for s in range(N + 1):
                        if s < N:
                            front(s)
                        if s:
                            if units[s - 1][0] == "cmp":
                                cmp_normal(s - 1)
                            else:
                                scale(s - 1)
                        if s >= 3 and units[s - 3][0] == "cmp" and units[s - 3][1] >= 4:
                            choose(units[s - 3][1])
                        u = s - AHEAD - 1
                        if 0 <= u < N and units[u][0] == "win" and units[u][2] == 0 and units[u][1] + 1 < NT:
                            split_queries(units[u][1] + 1)

            return oT, gC

        def merge_and_output(oT, gC):
            oH, oL = at("noH", RH, [P, 4, S], F32R), at("noL", RH + 16, [P, 4, S], F32R)
            tmp = [at(f"nmtmp{i}", RX + 32 + 2 * i, [P, 512]) for i in range(2)]
            mH = at("mH", RH + 32, [P, KT, S], F32R)
            mL = at("mL", RX + 40, [P, KT, S], F32R)
            x1 = at("x1", RX, [P, NT, D])
            junk = at("ojunk", RX + 36, [P, D])
            oh, ol, br_out, summed = (sem("n4_" + n) for n in ("oh", "ol", "br_out", "summed"))
            x_back, mh, ml, x1_out, sq_done = (sem("o_" + n) for n in ("x_back", "high", "low", "x1", "square"))
            with nc.Block() as block:
                @block.sync
                def _(sp):
                    for g in BR:
                        load_weights(sp, g)
                    sp.wait_ge(ol, 4)
                    sp.dma_start(x1[:, :, :], x.rearrange("(t p) d -> p t d", p=P)).then_inc(x_back, 16)
                    for g in WO:
                        load_weights(sp, g)

                @block.gpsimd
                def _(pool):
                    for g in BR + WO:
                        split_weights(pool, g)

                @block.tensor
                def _(pe):
                    product(pe, BR[0], oH, oL, always, before=lambda j: pe.wait_ge(ol, 2 * j + 2))
                    product(pe, BR[1], oH, oL, lambda b: pe.wait_ge(br_out, b + 1))
                    product(pe, WO[0], mH, mL, lambda b: pe.wait_ge(br_out, 8 + b + 1),
                            before=lambda j: pe.wait_ge(ml, 2 * j + 2))
                    product(pe, WO[1], mH, mL, lambda b: pe.wait_ge(x1_out, b + 1))

                @block.scalar
                def _(act):
                    for h in range(4):
                        act.copy(oH[:, h, :].rearrange("p (c q) -> p c q", c=NT), oT[:, :, h, :]).then_inc(oh, 1)
                    for kt in range(KT):
                        act.wait_ge(summed, 2 * kt + 2)
                        act.copy(mH[:, kt, :], merged[:, kt, :]).then_inc(mh, 1)
                    for b in range(NT):
                        act.wait_ge(x1_out, NT + b + 1)
                        if b:
                            act.wait_ge(sq_done, b)
                        act.activation(junk[:, :], x1[:, b, :], ACT.Square,
                                       accum_out=stat[:, 0, b:b + 1]).then_inc(sq_done, 1)

                @block.vector
                def _(dve):
                    for h in range(4):
                        dve.wait_ge(oh, h + 1)
                        dve.tensor_tensor(oL[:, h, :].rearrange("p (c q) -> p c q", c=NT), oT[:, :, h, :],
                                          oH[:, h, :].bitcast(F32).rearrange("p (c q) -> p c q", c=NT),
                                          ALU.subtract).then_inc(ol, 1)

                    def low(kt):
                        dve.wait_ge(mh, kt + 1)
                        dve.tensor_tensor(mL[:, kt, :], merged[:, kt, :], mH[:, kt, :].bitcast(F32),
                                          ALU.subtract).then_inc(ml, 1)

                    for n in range(16):
                        g, b = n // 8, n % 8
                        cols = slice((b % 2) * HALF, (b % 2 + 1) * HALF)
                        wait_bank(dve, BR[g], b)
                        dst = merged[:, n // 2, cols]
                        dve.tensor_tensor(tmp[n % 2][:, :], bank[b][:, :], gC[:, n // 2, cols], ALU.mult).then_inc(br_out, 1)
                        dve.wait_ge(br_out, n + 1)
                        dve.tensor_tensor(dst, dst, tmp[n % 2][:, :], ALU.add).then_inc(summed, 1)
                        if n % 2 == 0 and n:
                            low(n // 2 - 1)
                    low(KT - 1)
                    dve.wait_ge(x_back, 16)
                    for g in range(2):
                        for b in range(8):
                            wait_bank(dve, WO[g], b)
                            dst = x1[:, b, g * 512:(g + 1) * 512]
                            dve.tensor_tensor(dst, dst, bank[b][:, :], ALU.add).then_inc(x1_out, 1)
            return x1

        def ffn(x1):
            SLOTS, FULLS = 8, 21

            def load_ffn(sp, g, i, **part):
                if g is UP:
                    load_weights(sp, g, i, SLOTS, lambda j: w["w_up"][256 * j:256 * j + 256, bass.ds(i * 512, 512)]
                                 .rearrange("(k p) n -> p k n", p=P), **part)
                else:
                    load_weights(sp, g, i, SLOTS, lambda j: w["w_down"][
                        bass.ds(i * 512 + 256 * j, 256), g.col0:g.col0 + 512].rearrange("(k p) n -> p k n", p=P), **part)

            norm_transpose("n2", x1, w["ln_mlp_g"], False, lambda sp: load_ffn(sp, UP, 0, stop=2),
                           lambda pool: split_weights(pool, UP, 0, SLOTS, stop=2))

            uH, uL = at("uH", RM, [P, 4, S], F32R), at("uL", RM + 16, [P, 4, S], F32R)
            rr = [at(f"rr{i}", RX + 32 + 2 * i, [P, 512]) for i in range(2)]
            sqr = [at(f"sqr{i}", RX + 36 + 2 * i, [P, 512]) for i in range(2)]
            CH = FF // 512
            up, down = UP, DOWN
            done["slot"] += SLOTS * (CH - 1)
            done["full"] += FULLS * (CH - 1)
            relu, sq_, uh, ul, added, seeded = (sem("f_" + n) for n in ("relu", "square", "high", "low", "added", "seeded"))
            with nc.Block() as block:
                @block.sync
                def _(sp):
                    with sp.Fori(0, CH - 1) as i:
                        load_ffn(sp, up, i, start=2)
                        load_ffn(sp, down[0], i)
                        load_ffn(sp, down[1], i)
                        load_ffn(sp, up, i + 1, stop=2)
                    load_ffn(sp, up, CH - 1, start=2)
                    load_ffn(sp, down[0], CH - 1)
                    load_ffn(sp, down[1], CH - 1)
                    for t in range(NT):
                        sp.wait_ge(added, 8 + 16 * (CH - 1) + 8 + t + 1)
                        sp.dma_start(out[t * P:(t + 1) * P, :], x1[:, t, :]).then_inc(out_done, 16)
                    sp.wait_ge(out_done, 16 * NT)

                @block.gpsimd
                def _(pool):
                    with pool.Fori(0, CH - 1) as i:
                        split_weights(pool, up, i, SLOTS, start=2)
                        for g in down:
                            split_weights(pool, g, i, SLOTS)
                        split_weights(pool, up, i + 1, SLOTS, stop=2)
                    split_weights(pool, up, CH - 1, SLOTS, start=2)
                    for g in down:
                        split_weights(pool, g, CH - 1, SLOTS)

                @block.tensor
                def _(pe):
                    pe.wait_ge(seeded, 1)
                    with pe.Fori(0, CH) as i:
                        product(pe, up, hH2, hL2, lambda b: pe.wait_ge(added, 16 * i + b + 1), i, SLOTS)

                        product(pe, down[0], uH, uL, lambda b: pe.wait_ge(relu, 8 * i + b + 1), i, SLOTS,
                                before=lambda j: pe.wait_ge(ul, 8 * i + 4 * j + 4))
                        product(pe, down[1], uH, uL, lambda b: pe.wait_ge(added, 16 * i + 8 + b + 1), i, SLOTS)

                @block.scalar
                def _(act):
                    with act.Fori(0, CH) as i:
                        for b in range(8):
                            wait_bank(act, up, b, i, SLOTS, FULLS)
                            act.activation(rr[b % 2][:, :], bank[b][:, :], ACT.Relu).then_inc(relu, 1)
                            act.wait_ge(sq_, 8 * i + b + 1)
                            act.copy(uH[:, b // 2, (b % 2) * HALF:(b % 2 + 1) * HALF], sqr[b % 2][:, :]).then_inc(uh, 1)

                @block.vector
                def _(dve):
                    for b in range(8):
                        last = dve.memset(stat[:, 7, b:b + 1], 0.0)
                        last.then_inc(added, 1)
                    dve.wait_ge(added, 8)
                    dve.memset(stat[:, 7, 8:9], 0.0).then_inc(seeded, 1)
                    with dve.Fori(0, CH) as i:
                        for b in range(8):
                            dve.wait_ge(relu, 8 * i + b + 1)
                            dve.tensor_tensor(sqr[b % 2][:, :], rr[b % 2][:, :], rr[b % 2][:, :], ALU.mult).then_inc(sq_, 1)
                            dve.wait_ge(uh, 8 * i + b + 1)
                            dve.tensor_tensor(uL[:, b // 2, (b % 2) * HALF:(b % 2 + 1) * HALF], sqr[b % 2][:, :],
                                              uH[:, b // 2, (b % 2) * HALF:(b % 2 + 1) * HALF].bitcast(F32),
                                              ALU.subtract).then_inc(ul, 1)
                        for g in range(2):
                            for b in range(8):
                                wait_bank(dve, down[g], b, i, SLOTS, FULLS)
                                dst = x1[:, b, g * 512:(g + 1) * 512]
                                dve.tensor_tensor(dst, dst, bank[b][:, :], ALU.add).then_inc(added, 1)

        hH2, hL2 = hH, hL
        oH, oL = gla()
        merge(0, oH, oL, MERGE0, SQ, True)
        oH, oL = stick_breaking()
        merge(1, oH, oL, MERGE1, NQ, False)
        recycle()
        oT, gC = nsa()
        recycle()
        x1 = merge_and_output(oT, gC)
        ffn(x1)


_IN_NAMES = ["x", "ln_mix_g", "ln_mlp_g", "w_in", "gla_w_a2", "gla_b_a", "gla_norm_g", "nsa_q_norm_g", "nsa_k_norm_g",
             "nsa_pe_k", "nsa_pe_v", "nsa_wk1", "nsa_wk2", "nsa_wv1", "nsa_wv2", "rel_bias", "w_br_gla", "w_br_sb",
             "w_br_nsa", "w_out", "w_up", "w_down"]


def shape_constants():
    import numpy as np
    i = np.arange(P)[:, None]
    j = np.arange(P)[None, :]
    c = {
        "ident": i == j, "flip": i == P - 1 - j, "tri": i >= j, "ones": i >= 0 * j, "strict": i < j,
        "strictneg": np.where(i < j, 0.0, NEG), "window": np.where(j > i, 0.0, NEG),
    }
    q = np.arange(S).reshape(NT, P, 1)
    blk = np.arange(NSEL)[None, None, :]
    cur = q // SEL
    base = np.where((blk == cur) | (blk == cur - 1) | (blk == 0), 1000.0, 0.0)
    base = np.where(blk * SEL <= q, base, NEG)
    c["selbase"] = base.transpose(1, 0, 2).reshape(P, NT * NSEL)
    c["tie"] = np.broadcast_to((np.arange(NSEL)[None, :] < np.arange(NSEL)[:, None]).reshape(1, -1), (P, NSEL * NSEL))
    cst = np.concatenate([np.asarray(c[n], np.float32) for n, _ in CONST_COLS], axis=1)
    dist = (S - 1) - np.arange(REV)
    starts = np.asarray(BUCKET_START)
    bucket = np.where(dist < 0, 32, np.searchsorted(starts, np.maximum(dist, 0), side="right") - 1)
    onehot = (np.arange(33)[:, None] == bucket[None, :]).astype(np.float32)
    expand = (np.arange(NSEL)[:, None] == (np.arange(S) // SEL)[None, :]).astype(np.float32)
    return {"cst": np.ascontiguousarray(cst), "causal": (i <= j).astype(np.uint32), "onehot": onehot, "expand": expand}


def kernel(**inputs):
    import numpy as np
    import concourse.bacc as bacc
    from concourse.bass_utils import run_bass_kernel_spmd

    nc = bacc.Bacc("TRN2", target_bir_lowering=False, num_devices=1)
    arrays, aps = {}, {}
    for name in _IN_NAMES:
        a = np.ascontiguousarray(inputs[name])
        if name == "x" or (name != "rel_bias" and a.ndim > 1):
            a = a.reshape(a.shape[1:])
        arrays[name] = a
    arrays.update(shape_constants())
    for name, a in arrays.items():
        aps[name] = nc.dram_tensor(name, a.shape, mybir.dt.from_np(a.dtype), kind="ExternalInput").ap()
    out = nc.dram_tensor("out", (S, D), F32, kind="ExternalOutput").ap()
    aps["bias_rev"] = nc.dram_tensor("bias_rev", (NH, REV + 1), F32, kind="Internal").ap()
    build(nc, aps["x"], aps, out)
    r = run_bass_kernel_spmd(nc, [arrays], core_ids=[0])
    return r.results[0]["out"].reshape(1, S, D)
```

```python
from contextlib import ExitStack

import concourse.bass as bass
from concourse import mybir

P = 128
ALU = mybir.AluOpType
ACT = mybir.ActivationFunctionType
F32 = mybir.dt.float32
F32R = mybir.dt.float32r
BF16 = mybir.dt.bfloat16
U32 = mybir.dt.uint32
AX = mybir.AxisListType

D = 1024
S = 1024
KT = D // P
NT = S // P
HALF = 512
GH, GD, RANK, GTEMP = 4, 128, 16, 16.0
SH, SD = 4, 128
NH, ND = 8, 64
CMP_BLOCK, CMP_STRIDE, CMP_HID, NCMP = 32, 16, 256, 63
SEL, TOPN, NSEL, WINDOW = 64, 8, 16, 512
FF = 4 * D
EPS = 1e-6
NEG = -1e30
BUCKET_START = [0, 1, 2, 3, 4, 5, 6, 7, 8, 9, 10, 11, 12, 13, 14, 15,
                16, 21, 27, 35, 46, 59, 77, 99, 128, 166, 216, 280, 363, 470, 609, 790]

SIZES = [("gq", 512), ("gk", 512), ("gv", 512), ("ga", 16), ("gr", 512), ("sq", 512), ("sk", 512), ("sv", 512),
         ("nq", 512), ("kc", 64), ("vc", 64), ("ks", 64), ("vs", 64), ("kw", 64), ("vw", 64), ("ng", 24), ("mg", 3072)]
COL = {}
_at = 0
for _n, _w in SIZES:
    COL[_n] = _at
    _at += _w

CONST_COLS = [("ident", 128), ("tri", 128), ("ones", 128), ("strict", 128), ("strictneg", 128),
              ("window", 128), ("selbase", NT * NSEL), ("tie", NSEL * NSEL), ("flip", 128)]
CONST_AT = {}
_at = 0
for _n, _w in CONST_COLS:
    CONST_AT[_n] = (_at, _at + _w)
    _at += _w
CONST_W = _at
REV = S + P - 1


def with_dim(ap, axis, count):
    dims = [list(d) for d in ap.ap]
    dims.insert(axis, [0, count])
    return bass.AP(ap.tensor, ap.offset, dims)


def build(nc, x, w, out):
    ctx = ExitStack()
    with ctx:
        BASE = 17 * 1024
        KB = 1024

        def at(name, kb, shape, dt=F32):
            return nc.alloc_sbuf_tensor_at(name, list(shape), dt, offset=int(BASE + kb * KB))

        phase_sems = []

        def sem(name, keep=False):
            s = nc.alloc_semaphore(name=name)
            if not keep:
                phase_sems.append(s)
            return s

        def recycle():
            with nc.Block() as block:
                @block.gpsimd
                def _(pool):
                    for s in phase_sems[0::4]:
                        pool.sem_clear(s)

                @block.vector
                def _(dve):
                    for s in phase_sems[1::4]:
                        dve.sem_clear(s)

                @block.scalar
                def _(act):
                    for s in phase_sems[2::4]:
                        act.sem_clear(s)

                @block.sync
                def _(sp):
                    for s in phase_sems[3::4]:
                        sp.sem_clear(s)
            for s in phase_sems:
                nc.release_semaphore(s)
            phase_sems.clear()

        pairs = [ctx.enter_context(nc.psum_tensor(f"pair{i}", [P, 1024], F32)) for i in range(4)]
        bank = [pairs[i // 2][:, (i % 2) * 512:(i % 2 + 1) * 512] for i in range(8)]

        CONSTS, RING, RH, RM, RX = 0, 14, 38, 102, 134
        cst = at("cst", CONSTS, [P, CONST_W])
        kb = CONSTS + (CONST_W * 4 + 1023) / 1024.0
        kb = float(int(kb))
        causal = at("causal", kb, [P, P], U32); kb += 0.5
        identb = at("identb", kb, [P, P], BF16); kb += 0.25
        windowb = at("windowb", kb, [P, P], BF16); kb += 0.25
        gnorm = at("gnorm", kb, [P, GD]); kb += 0.5
        qgain = at("qgain", kb, [P, ND]); kb += 0.25
        kgain = at("kgain", kb, [P, ND]); kb += 0.25
        stat = at("stat", kb, [P, 8, 64]); kb += 2
        gatef = at("gatef", kb, [P, NT, 24]); kb += 0.75
        assert kb <= RING, kb

        def const(name, rows=P):
            a, b = CONST_AT[name]
            return cst[0:rows, a:b]

        stage = [at(f"stage{i}", RING + 4 * i, [P, 2, 512]) for i in range(2)]
        WH = [at(f"wh{i}", RING + 8 + 4 * i, [P, 2, 512], F32R) for i in range(2)]
        WL = [at(f"wl{i}", RING + 16 + 4 * i, [P, 2, 512], F32R) for i in range(2)]
        hH = at("hH", RH, [P, KT, S], F32R)
        hL = at("hL", RH + 32, [P, KT, S], F32R)
        merged = at("merged", RM, [P, KT, S])

        w_loaded = [sem("w_loaded0", True), sem("w_loaded1", True)]
        w_high = sem("w_high", True)
        w_split = sem("w_split", True)
        w_used = sem("w_used", True)
        bank_full = sem("bank_full", True)
        out_done = sem("out_done", True)

        KVW = 280
        done = {"slot": 0, "full": 0}

        class Product:

            def __init__(self, kind, mat, row0, col0, nslots, ncols=512, nbanks=8):
                self.kind, self.mat, self.row0, self.col0 = kind, mat, row0, col0
                self.nslots, self.ncols, self.nbanks = nslots, ncols, nbanks
                self.slot0, self.full0 = done["slot"], done["full"]
                done["slot"] += nslots
                done["full"] += nbanks - 1

        def more(n, per, i):
            return n if i is None else n + per * i

        def load_weights(sp, g, i=None, slots=0, src=None, start=0, stop=None):
            for j in range(start, g.nslots if stop is None else stop):
                s = g.slot0 + j
                if s >= 2:
                    sp.wait_ge(w_split, more(s - 1, slots, i))
                if src is None:
                    r = g.row0 + 256 * j
                    ap = g.mat[r:r + 256, g.col0:g.col0 + g.ncols].rearrange("(k p) n -> p k n", p=P)
                else:
                    ap = src(j)
                sp.dma_start(stage[s % 2][:, :, 0:g.ncols], ap).then_inc(w_loaded[s % 2], 16)

        def split_weights(pool, g, i=None, slots=0, start=0, stop=None):
            n = g.ncols
            for j in range(start, g.nslots if stop is None else stop):
                s = g.slot0 + j
                pool.wait_ge(w_loaded[s % 2], more(16 * (s // 2 + 1), 8 * slots, i))
                if s >= 2:
                    pool.wait_ge(w_used, more(s - 1, slots, i))
                pool.tensor_tensor(WH[s % 2][:, :, 0:n], stage[s % 2][:, :, 0:n],
                                   with_dim(with_dim(const("ones")[:, 0], 1, 2), 2, n), ALU.mult).then_inc(w_high, 1)
                pool.wait_ge(w_high, more(s + 1, slots, i))
                pool.tensor_tensor(WL[s % 2][:, :, 0:n], stage[s % 2][:, :, 0:n],
                                   WH[s % 2][:, :, 0:n].bitcast(F32), ALU.subtract).then_inc(w_split, 1)

        def product(pe, g, XH, XL, free, i=None, slots=0, before=None):
            for j in range(g.nslots):
                s = g.slot0 + j
                pe.wait_ge(w_split, more(s + 1, slots, i))
                if before is not None:
                    before(j)
                for b in range(g.nbanks):
                    if j == 0:
                        free(b)
                    n = 0
                    for kk in range(2):
                        kt = 2 * j + kk
                        for wt, xt in ((WH, XH), (WH, XL), (WL, XH)):
                            if g.kind == "T":
                                m, half = b // 2, b % 2
                                lhs = wt[s % 2][:, kk, m * P:(m + 1) * P]
                                rhs = xt[:, kt, half * HALF:(half + 1) * HALF]
                                dst = bank[b][:, :]
                            else:
                                lhs = xt[:, kt, b * P:(b + 1) * P]
                                rhs = wt[s % 2][:, kk, 0:g.ncols]
                                dst = bank[b][:, 0:g.ncols]
                            last = pe.matmul(dst, lhs, rhs, start=(j == 0 and n == 0),
                                             stop=(j == g.nslots - 1 and n == 5))
                            n += 1
                    if b == g.nbanks - 1:
                        last.then_inc(w_used, 1)
                    elif j == g.nslots - 1:
                        last.then_inc(bank_full, 1)

        def wait_bank(eng, g, b, i=None, slots=0, fulls=0):
            if b < g.nbanks - 1:
                eng.wait_ge(bank_full, more(g.full0 + b + 1, fulls, i))
            else:
                eng.wait_ge(w_used, more(g.slot0 + g.nslots, slots, i))

        def always(b):
            pass

        def w_in(kind, col, **shape):
            return Product(kind, w["w_in"], 0, col, 4, **shape)

        def merge_products(m, w_br):
            order = [(w_in("T", COL["mg"] + m * D + g * 512), Product("T", w_br, 0, g * 512, 2)) for g in range(2)]
            return [x[0] for x in order], [x[1] for x in order]

        G = {"a": w_in("T", COL["ga"], ncols=128, nbanks=2), "q": w_in("T", COL["gq"]), "k": w_in("T", COL["gk"]),
             "r": w_in("N", COL["gr"]), "v": w_in("N", COL["gv"])}
        MERGE0 = merge_products(0, w["w_br_gla"])
        SQ, SK, SV = w_in("T", COL["sq"]), w_in("T", COL["sk"]), w_in("N", COL["sv"])
        MERGE1 = merge_products(1, w["w_br_sb"])
        NQ, CV = w_in("N", COL["nq"]), w_in("T", COL["kc"], ncols=128, nbanks=2)
        KV = w_in("N", COL["ks"], ncols=KVW)
        GC = [w_in("T", COL["mg"] + 2 * D + g * 512) for g in range(2)]
        BR = [Product("T", w["w_br_nsa"], 0, g * 512, 2) for g in range(2)]
        WO = [Product("N", w["w_out"], 0, g * 512, 4) for g in range(2)]
        UP = Product("T", w["w_up"], 0, 0, 4)
        DOWN = [Product("N", w["w_down"], 0, g * 512, 2) for g in range(2)]

        def inv_root(act, dve, ready, steps, ss, ms, r, t, count, part):
            mean, ln, ex, nwt = steps
            if part == "dve1":
                dve.tensor_scalar(ms, ss, 1.0 / count, EPS, ALU.mult, ALU.add).then_inc(mean, 1)
            elif part == "act":
                act.preload_act_table_set("natural_log_exp_and_others")
                act.activation(r, ms, ACT.Ln).then_inc(ln, 1)
                act.wait_ge(ln, ready)
                act.activation(r, r, ACT.Exp, scale=-0.5).then_inc(ex, 1)
            else:
                dve.tensor_tensor(t, r, r, ALU.mult).then_inc(nwt, 1)
                dve.wait_ge(nwt, 4 * ready - 3)
                dve.tensor_tensor(t, t, ms, ALU.mult).then_inc(nwt, 1)
                dve.wait_ge(nwt, 4 * ready - 2)
                dve.tensor_scalar(t, t, -0.5, 1.5, ALU.mult, ALU.add).then_inc(nwt, 1)
                dve.wait_ge(nwt, 4 * ready - 1)
                dve.tensor_tensor(r, r, t, ALU.mult).then_inc(nwt, 1)
                dve.wait_ge(nwt, 4 * ready)

        def norm_transpose(tag, xin, gain_dram, load_x, load_ahead, split_ahead):
            gB = at(tag + "gB", RM, [P, D])
            junk = at(tag + "junk", RM + 4, [P, D])
            xn = [at(tag + f"xn{i}", RM + 8 + 4 * i, [P, D]) for i in range(2)]
            x_loaded = [sem(tag + f"x_loaded{t}") for t in range(NT)] if load_x else None
            g_loaded, more_in = sem(tag + "g_loaded"), sem(tag + "constants_in")
            sq_done = sem(tag + "sq_done")
            steps = tuple(sem(tag + n) for n in ("mean", "ln", "exp", "newton"))
            xn_ready = sem(tag + "xn_ready")
            turned = sem(tag + "turned")
            high_out, low_out = sem(tag + "high_out"), sem(tag + "low_out")
            groups = 4 if load_x else 1
            per = NT // groups
            lag = per if groups > 1 else 1

            def cols(g):
                return tuple(stat[:, k, g * per:(g + 1) * per] for k in range(4))

            r = stat[:, 2, 0:NT]
            with nc.Block() as block:
                @block.sync
                def _(sp):
                    def tiles(first, last):
                        for i in range(first, last):
                            sp.dma_start(xin[:, i, :], x[i * P:(i + 1) * P, :]).then_inc(x_loaded[i], 16)

                    if load_x:
                        tiles(0, 2)
                    sp.dma_start(gB[:, :], gain_dram.partition_broadcast(P)).then_inc(g_loaded, 16)
                    if load_x:
                        sp.dma_start(cst[:, :], w["cst"]).then_inc(g_loaded, 16)
                        tiles(2, NT)
                        sp.dma_start(causal[:, :], w["causal"]).then_inc(more_in, 16)
                        for dst, src in ((gnorm, "gla_norm_g"), (qgain, "nsa_q_norm_g"), (kgain, "nsa_k_norm_g")):
                            sp.dma_start(dst[:, :], w[src].partition_broadcast(P)).then_inc(more_in, 16)
                    load_ahead(sp)
                    if load_x:
                        sp.wait_ge(more_in, 64)

                @block.gpsimd
                def _(pool):
                    if load_x:
                        pool.wait_ge(g_loaded, 32)
                    split_ahead(pool)

                @block.scalar
                def _(act):
                    def high(i):
                        for q in range(2):
                            n = 2 * i + q
                            act.wait_ge(turned, n + 1)
                            act.copy(hH[:, 4 * q:4 * q + 4, i * P:(i + 1) * P],
                                     bank[n % 8][:, :].rearrange("p (k c) -> p k c", k=4)).then_inc(high_out, 1)

                    for g in range(groups):
                        if load_x:
                            for i in range(g * per, (g + 1) * per):
                                act.wait_ge(x_loaded[i], 16)
                                if i:
                                    act.wait_ge(sq_done, i)
                                act.activation(junk[:, :], xin[:, i, :], ACT.Square,
                                               accum_out=stat[:, 0, i:i + 1]).then_inc(sq_done, 1)
                        act.wait_ge(steps[0], g + 1)
                        inv_root(act, None, g + 1, steps, *cols(g), D, "act")
                        if g:
                            for i in range((g - 1) * per, g * per):
                                high(i)
                    for i in range((groups - 1) * per, NT):
                        high(i)

                @block.vector
                def _(dve):
                    def roots(g):
                        if load_x:
                            dve.wait_ge(sq_done, (g + 1) * per)
                        inv_root(None, dve, g + 1, steps, *cols(g), D, "dve1")
                        dve.wait_ge(steps[2], g + 1)
                        inv_root(None, dve, g + 1, steps, *cols(g), D, "dve2")

                    def low(n):
                        i, q = n // 2, n % 2
                        dve.wait_ge(high_out, n + 1)
                        dst = slice(i * P, (i + 1) * P)
                        dve.tensor_tensor(hL[:, 4 * q:4 * q + 4, dst],
                                          bank[n % 8][:, :].rearrange("p (k c) -> p k c", k=4),
                                          hH[:, 4 * q:4 * q + 4, dst].bitcast(F32), ALU.subtract).then_inc(low_out, 1)

                    for i in range(NT):
                        if i % per == 0:
                            roots(i // per)
                        if i == 0:
                            dve.wait_ge(g_loaded, 32 if load_x else 16)
                        if i >= 2:
                            dve.wait_ge(turned, 2 * (i - 1))
                        dve.scalar_tensor_tensor(out=xn[i % 2][:, :], in0=xin[:, i, :], scalar=r[:, i:i + 1],
                                                 in1=gB[:, :], op0=ALU.mult, op1=ALU.mult).then_inc(xn_ready, 1)
                        if i >= lag:
                            low(2 * (i - lag))
                            low(2 * (i - lag) + 1)
                    for n in range(2 * (NT - lag), 2 * NT):
                        low(n)

                @block.tensor
                def _(pe):
                    if load_x:
                        pe.wait_ge(g_loaded, 32)
                    for i in range(NT):
                        pe.wait_ge(xn_ready, i + 1)
                        for q in range(2):
                            n = 2 * i + q
                            if n >= 8:
                                pe.wait_ge(low_out, n - 7)
                            for k in range(4):
                                kt = 4 * q + k
                                last = pe.transpose(bank[n % 8][:, k * P:(k + 1) * P],
                                                    xn[i % 2][:, kt * P:(kt + 1) * P], const("ident"))
                            last.then_inc(turned, 1)

        xin = at("xin", RX, [P, NT, D])
        norm_transpose("n1", xin, w["ln_mix_g"], True, lambda sp: load_weights(sp, G["a"], stop=2),
                       lambda pool: split_weights(pool, G["a"], stop=2))

        def gla():
            la = at("la", RM, [P, GH, S])
            sr = at("sr", RM, [P, NT, 512])
            e = [at(f"ge{i}", RM + 16 + 4 * i, [P, S]) for i in range(2)]
            rsig = at("rsig", RM + 24, [P, 2, 512])
            q = at("gqT", RX, [P, GH, S])
            k = at("gkT", RX + 16, [P, GH, S])
            v = at("gv", RX + 32, [P, NT, 512])
            o = at("go", RX + 48, [P, NT, 512])
            sTm = [at(f"gsT{i}", RX + 64 + 2 * i, [P, GH, P]) for i in range(2)]
            ktok = at("gktok", RX + 68, [P, GH, P])
            St = [at("gSt0", RX + 70, [P, GH, P]), at("gSt1", RM + 24, [P, GH, P])]
            St0 = at("gS", RM + 16, [P, GH, P])
            upd = at("gupd", RM + 18, [P, GH, P])
            wa2 = at("wa2", RX + 64, [RANK, 512])
            ba = at("ba", RX + 66, [P, GH])
            keep = at("gkeep", RM + 28, [P, S])
            lowT = at("glowT", RX + 48, [RANK, S])
            midc = at("gmidc", RX + 66.5, [P, GH, NT])
            em, eb, ebm = (at(f"gem{n}", CONSTS + 13.25 + 0.125 * n, [P, GH, NT]) for n in range(3))

            small = sem("g_small")
            out_q, out_k, out_v, out_a, out_r = (sem(f"g_out_{n}") for n in "qkvar")
            a_full, u_out, neg_abs, ex1, ln1, la_out, cum_out, dev_out = (
                sem(n) for n in ("g_a_full", "g_u_out", "g_negabs", "g_exp1", "g_ln1", "g_la", "g_cum", "g_dev"))
            eplus, eminus, decayed, mids, mid_e, keep_ok, rs_ok, sr_ok = (
                sem(n) for n in ("g_eplus", "g_eminus", "g_decayed", "g_mids", "g_mid_e", "g_keep", "g_rsig", "g_sr"))
            sc_full, sc_out, kt_full, kt_out, o_full, o_out, kv_full, st_upd, st_tmp = (
                sem(n) for n in ("g_scores", "g_scores_out", "g_kturn", "g_kturn_out", "g_o", "g_o_out", "g_kv",
                                 "g_state", "g_state_tmp"))
            osq, steps = sem("g_osq"), tuple(sem("g_" + n) for n in ("mean", "ln", "exp", "newton"))
            normed, gated, turned, high_out, low_out = (
                sem(n) for n in ("g_normed", "g_gated", "g_turned", "g_high", "g_low"))
            oH = at("goH", RX, [P, GH, S], F32R)
            oL = at("goL", RX + 16, [P, GH, S], F32R)
            sq = at("gsq", RM + 20, [P, 2, 512])

            def turn_bank(t):
                return bank[3] if t < 4 else bank[t - 4]

            STEPS = NT + 4

            def root_args(g):
                return (steps, *(stat[:, n, 8 * g:8 * g + 8] for n in range(4)), GD)

            with nc.Block() as block:
                @block.sync
                def _(sp):
                    sp.dma_start(wa2[:, :], w["gla_w_a2"]).then_inc(small, 16)
                    with nc.allow_non_contiguous_dma(reason="512 biases onto partitions"):
                        sp.dma_start(ba[:, :], w["gla_b_a"].rearrange("(h p) -> p h", p=P)).then_inc(small, 16)
                    load_weights(sp, G["a"], start=2)
                    for g in "qkrv":
                        load_weights(sp, G[g])
                    load_weights(sp, MERGE0[0][0], stop=2)

                @block.gpsimd
                def _(pool):
                    pool.memset(keep[:, :], 1.0).then_inc(keep_ok, 1)
                    pool.wait_ge(keep_ok, 1)
                    pool.memset(keep[:, :].rearrange("p (c t) -> p c t", t=P)[:, :, 0:1], 0.0).then_inc(keep_ok, 1)
                    split_weights(pool, G["a"], start=2)
                    for g in "qkrv":
                        split_weights(pool, G[g])
                    split_weights(pool, MERGE0[0][0], stop=2)
                    for t in range(NT):
                        pool.wait_ge(out_r, t + 1)
                        srt = sr[:, t, :].rearrange("p (h d) -> p h d", h=GH)
                        pool.tensor_tensor(srt, srt, with_dim(gnorm[:, :], 1, GH), ALU.mult).then_inc(sr_ok, 1)
                    for t in range(NT):
                        pool.wait_ge(normed, t + 1)
                        pool.wait_ge(sr_ok, t + 1)
                        pool.tensor_tensor(o[:, t, :], o[:, t, :], sr[:, t, :], ALU.mult).then_inc(gated, 1)

                @block.tensor
                def _(pe):
                    product(pe, G["a"], hH, hL, always)
                    pe.wait_ge(small, 32)
                    pe.wait_ge(out_a, 2)
                    for h in range(GH):
                        for half in range(2):
                            pe.matmul(bank[2 * h + half][:, :], wa2[:, h * P:(h + 1) * P],
                                      lowT[:, half * HALF:(half + 1) * HALF], start=True, stop=True).then_inc(a_full, 1)
                    product(pe, G["q"], hH, hL, lambda b: pe.wait_ge(u_out, b + 1))
                    product(pe, G["k"], hH, hL, lambda b: pe.wait_ge(out_q, b + 1))
                    product(pe, G["r"], hH, hL, lambda b: pe.wait_ge(out_k, b + 1))
                    product(pe, G["v"], hH, hL, lambda b: pe.wait_ge(out_r, b + 1))
                    pe.wait_ge(decayed, 2 * GH)

                    def scores(c):
                        if c >= 2:
                            pe.wait_ge(sc_out, c - 1)
                        else:
                            pe.wait_ge(out_v, c + 1)
                        cs = slice(c * P, (c + 1) * P)
                        for h in range(GH):
                            last = pe.matmul(bank[c % 2][:, h * P:(h + 1) * P], k[:, h, cs], q[:, h, cs],
                                             start=True, stop=True)
                        last.then_inc(sc_full, 1)

                    def keys_turned(c):
                        if c:
                            pe.wait_ge(kt_out, c)
                        else:
                            pe.wait_ge(out_v, 3)
                        for h in range(GH):
                            last = pe.transpose(bank[2][:, h * P:(h + 1) * P], k[:, h, c * P:(c + 1) * P], const("ident"))
                        last.then_inc(kt_full, 1)

                    def update(c):
                        if c >= 2:
                            pe.wait_ge(st_upd, c - 1)
                        else:
                            pe.wait_ge(out_v, c + 7)
                        pe.wait_ge(kt_out, c + 1)
                        for h in range(GH):
                            hs = slice(h * P, (h + 1) * P)
                            last = pe.matmul(bank[6 + c % 2][:, hs], ktok[:, h, :], v[:, c, hs], start=True, stop=True)
                        last.then_inc(kv_full, 1)

                    def output(c):
                        if c >= 2:
                            pe.wait_ge(o_out, c - 1)
                        else:
                            pe.wait_ge(out_v, c + 5)
                        pe.wait_ge(sc_out, c + 1)
                        if c:
                            pe.wait_ge(st_upd, c)
                        for h in range(GH):
                            hs = slice(h * P, (h + 1) * P)
                            last = pe.matmul(bank[4 + c % 2][:, hs], sTm[c % 2][:, h, :], v[:, c, hs], start=True, stop=(c == 0))
                            if c:
                                last = pe.matmul(bank[4 + c % 2][:, hs], q[:, h, c * P:(c + 1) * P], St[c % 2][:, h, :],
                                                 start=False, stop=True)
                        last.then_inc(o_full, 1)

                    def turn(t):
                        pe.wait_ge(gated, t + 1)
                        if t in (1, 2, 3, 7):
                            pe.wait_ge(low_out, min(t, 4))
                        for h in range(GH):
                            last = pe.transpose(turn_bank(t)[:, h * P:(h + 1) * P], o[:, t, h * P:(h + 1) * P], const("ident"))
                        last.then_inc(turned, 1)

                    scores(0)
                    keys_turned(0)
                    for c in range(STEPS):
                        if c + 1 < NT:
                            scores(c + 1)
                            update(c)
                        if c < NT:
                            output(c)
                        if c + 1 < NT - 1:
                            keys_turned(c + 1)
                        if c >= 4:
                            turn(c - 4)

                @block.scalar
                def _(act):
                    for b in range(2):
                        wait_bank(act, G["a"], b)
                        act.copy(lowT[:, b * HALF:(b + 1) * HALF], bank[b][0:RANK, :]).then_inc(out_a, 1)
                    act.preload_act_table_set("natural_log_exp_and_others")
                    for h in range(GH):
                        eh = e[h % 2][:, :]
                        act.wait_ge(neg_abs, h + 1)
                        act.activation(eh, eh, ACT.Exp).then_inc(ex1, 1)
                        act.wait_ge(ex1, h + 1)
                        act.activation(eh, eh, ACT.Ln, bias=1.0).then_inc(ln1, 1)
                    act.wait_ge(mids, 3)
                    for src, dst in ((0, em), (1, eb), (2, ebm)):
                        act.activation(dst[:, :, :], dst[:, :, :], ACT.Exp, scale=1.0 / GTEMP).then_inc(mid_e, 1)
                    for b in range(8):
                        wait_bank(act, G["q"], b)
                        act.copy(q[:, b // 2, (b % 2) * HALF:(b % 2 + 1) * HALF], bank[b][:, :]).then_inc(out_q, 1)
                    for h in range(GH):
                        act.wait_ge(dev_out, h + 1)
                        if h >= 2:
                            act.wait_ge(decayed, h - 1)
                        act.activation(e[h % 2][:, :], la[:, h, :], ACT.Exp, scale=1.0 / GTEMP).then_inc(eplus, 1)
                    for b in range(8):
                        wait_bank(act, G["k"], b)
                        act.copy(k[:, b // 2, (b % 2) * HALF:(b % 2 + 1) * HALF], bank[b][:, :]).then_inc(out_k, 1)
                    for h in range(GH):
                        act.wait_ge(decayed, GH + h - 1)
                        act.activation(e[h % 2][:, :], la[:, h, :], ACT.Exp, scale=-1.0 / GTEMP).then_inc(eminus, 1)
                    for b in range(8):
                        wait_bank(act, G["r"], b)
                        if b >= 2:
                            act.wait_ge(out_r, b - 1)
                        act.activation(rsig[:, b % 2, :], bank[b][:, :], ACT.Sigmoid).then_inc(rs_ok, 1)
                    for b in range(8):
                        wait_bank(act, G["v"], b)
                        act.copy(v[:, b, :], bank[b][:, :]).then_inc(out_v, 1)

                    def keys_out(c):
                        act.wait_ge(kt_full, c + 1)
                        if c:
                            act.wait_ge(kv_full, c)
                        act.copy(ktok[:, :, :].rearrange("p h c -> p (h c)"), bank[2][:, :]).then_inc(kt_out, 1)

                    keys_out(0)
                    for c in range(STEPS):
                        if c < NT:
                            act.wait_ge(o_full, c + 1)
                            act.copy(o[:, c, :], bank[4 + c % 2][:, :]).then_inc(o_out, 1)
                        if c + 1 < NT - 1:
                            keys_out(c + 1)
                        if c < NT:
                            if c >= 2:
                                act.wait_ge(osq, GH * (c - 1))
                            act.wait_ge(o_out, c + 1)
                            for h in range(GH):
                                hs = slice(h * P, (h + 1) * P)
                                act.activation(sq[:, c % 2, hs], o[:, c, hs], ACT.Square,
                                               accum_out=stat[:, 0, 4 * c + h:4 * c + h + 1]).then_inc(osq, 1)
                        if c >= 4:
                            t = c - 4
                            act.wait_ge(turned, t + 1)
                            act.copy(oH[:, :, t * P:(t + 1) * P],
                                     turn_bank(t)[:, :].rearrange("p (h c) -> p h c", h=GH)).then_inc(high_out, 1)
                        if c % 2 == 0 and 2 <= c <= NT:
                            act.wait_ge(steps[0], c // 2)
                            inv_root(act, None, c // 2, *root_args(c // 2 - 1), "act")

                @block.vector
                def _(dve):
                    dve.wait_ge(small, 32)
                    for h in range(GH):
                        for half in range(2):
                            n = 2 * h + half
                            dve.wait_ge(a_full, n + 1)
                            dve.tensor_scalar(la[:, h, half * HALF:(half + 1) * HALF], bank[n][:, :], ba[:, h:h + 1],
                                              None, ALU.add).then_inc(u_out, 1)
                    for h in range(GH + 1):
                        if h < GH:
                            if h >= 2:
                                dve.wait_ge(la_out, h - 1)
                            dve.wait_ge(u_out, 2 * h + 2)
                            dve.scalar_tensor_tensor(out=e[h % 2][:, :], in0=la[:, h, :], scalar=-1.0, in1=la[:, h, :],
                                                     op0=ALU.mult, op1=ALU.min).then_inc(neg_abs, 1)
                        if h:
                            i = h - 1
                            dve.wait_ge(ln1, i + 1)
                            dve.scalar_tensor_tensor(out=la[:, i, :], in0=la[:, i, :], scalar=0.0, in1=e[i % 2][:, :],
                                                     op0=ALU.min, op1=ALU.subtract).then_inc(la_out, 1)
                            dve.wait_ge(la_out, i + 1)
                            if i == 0:
                                dve.wait_ge(keep_ok, 2)
                            dve.tensor_tensor_scan(la[:, i, :], keep[:, :], la[:, i, :], 0.0, ALU.mult, ALU.add).then_inc(cum_out, 1)
                    dve.wait_ge(cum_out, GH)
                    lac = la[:, :, :].rearrange("p h (c t) -> p h c t", t=P)
                    dve.tensor_copy(em[:, :, :], lac[:, :, :, P // 2 - 1]).then_inc(mids, 1)
                    dve.tensor_copy(eb[:, :, :], lac[:, :, :, P - 1]).then_inc(mids, 1)
                    dve.tensor_tensor(ebm[:, :, :], lac[:, :, :, P - 1], lac[:, :, :, P // 2 - 1],
                                      ALU.subtract).then_inc(mids, 1)
                    dve.tensor_copy(midc[:, :, :], lac[:, :, :, P // 2 - 1]).then_inc(mids, 1)
                    dve.wait_ge(mids, 4)
                    for h in range(GH):
                        dve.tensor_tensor(lac[:, h, :, :], lac[:, h, :, :], with_dim(midc[:, h, :], 2, P),
                                          ALU.subtract).then_inc(dev_out, 1)
                    dve.wait_ge(out_q, 8)
                    for h in range(GH):
                        dve.wait_ge(eplus, h + 1)
                        dve.scalar_tensor_tensor(out=q[:, h, :], in0=q[:, h, :], scalar=GD ** -0.5, in1=e[h % 2][:, :],
                                                 op0=ALU.mult, op1=ALU.mult).then_inc(decayed, 1)
                    dve.wait_ge(out_k, 8)
                    for h in range(GH):
                        dve.wait_ge(eminus, h + 1)
                        dve.tensor_tensor(k[:, h, :], k[:, h, :], e[h % 2][:, :], ALU.mult).then_inc(decayed, 1)
                    for b in range(8):
                        dve.wait_ge(rs_ok, b + 1)
                        dve.tensor_tensor(sr[:, b, :], bank[b][:, :], rsig[:, b % 2, :], ALU.mult).then_inc(out_r, 1)


                    def masked(c):
                        dve.wait_ge(sc_full, c + 1)
                        if c >= 2:
                            dve.wait_ge(o_full, c - 1)
                        dve.copy_predicated(sTm[c % 2][:, :, :], with_dim(causal[:, :], 1, GH),
                                            bank[c % 2][:, :].rearrange("p (h t) -> p h t", h=GH)).then_inc(sc_out, 1)

                    for i in range(2):
                        dve.memset(sTm[i][:, :, :], 0.0).then_inc(st_tmp, 1)
                    dve.wait_ge(st_tmp, 2)
                    masked(0)
                    dve.wait_ge(mid_e, 3)
                    n = 2
                    for c in range(STEPS):
                        if c + 1 < NT:
                            if c:
                                dve.tensor_tensor(St0[:, :, :], St0[:, :, :], with_dim(eb[:, :, c], 2, P), ALU.mult).then_inc(st_tmp, 1)
                            dve.wait_ge(kv_full, c + 1)
                            kv = bank[6 + c % 2][:, :].rearrange("p (h d) -> p h d", h=GH)
                            dst = upd if c else St0
                            dve.tensor_tensor(dst[:, :, :], kv, with_dim(ebm[:, :, c], 2, P), ALU.mult).then_inc(st_tmp, 1)
                            n += 1
                            if c:
                                dve.wait_ge(st_tmp, n + 1)
                                dve.tensor_tensor(St0[:, :, :], St0[:, :, :], upd[:, :, :], ALU.add).then_inc(st_tmp, 1)
                                n += 2
                            dve.wait_ge(st_tmp, n)
                            if c:
                                dve.wait_ge(o_full, c)
                            dve.tensor_tensor(St[(c + 1) % 2][:, :, :], St0[:, :, :], with_dim(em[:, :, c + 1], 2, P),
                                              ALU.mult).then_inc(st_upd, 1)
                            masked(c + 1)
                        if c % 2 == 0 and 2 <= c <= NT:
                            dve.wait_ge(osq, 2 * GH * (c // 2))
                            inv_root(None, dve, c // 2, *root_args(c // 2 - 1), "dve1")
                        if c % 2 and 3 <= c <= NT + 1:
                            g = (c - 3) // 2
                            dve.wait_ge(steps[2], g + 1)
                            inv_root(None, dve, g + 1, *root_args(g), "dve2")
                            for t in (c - 3, c - 2):
                                ot = o[:, t, :].rearrange("p (h d) -> p h d", h=GH)
                                dve.wait_ge(o_out, t + 1)
                                dve.tensor_tensor(ot, ot, with_dim(stat[:, 2, 4 * t:4 * t + 4], 2, GD), ALU.mult).then_inc(normed, 1)
                        if c >= 4:
                            t = c - 4
                            cs = slice(t * P, (t + 1) * P)
                            dve.wait_ge(high_out, t + 1)
                            dve.tensor_tensor(oL[:, :, cs], turn_bank(t)[:, :].rearrange("p (h c) -> p h c", h=GH),
                                              oH[:, :, cs].bitcast(F32), ALU.subtract).then_inc(low_out, 1)

            return oH, oL

        def merge(m, oH, oL, products, following, first):
            tag = f"m{m}_"
            gate = at(tag + "gate", RX + 48, [P, 4, S])
            tmp = [at(tag + f"tmp{i}", RX + 64 + 2 * i, [P, 512]) for i in range(2)]
            gates, branches = products
            gate_out, br_out, summed = sem(tag + "gate_out"), sem(tag + "br_out"), sem(tag + "summed")
            with nc.Block() as block:
                @block.sync
                def _(sp):
                    for g in range(2):
                        load_weights(sp, gates[g], start=0 if g else 2)
                        load_weights(sp, branches[g])
                    load_weights(sp, following, stop=2)

                @block.gpsimd
                def _(pool):
                    for g in range(2):
                        split_weights(pool, gates[g], start=0 if g else 2)
                        split_weights(pool, branches[g])
                    split_weights(pool, following, stop=1)

                @block.tensor
                def _(pe):
                    for g in range(2):
                        product(pe, gates[g], hH, hL, (lambda b: pe.wait_ge(br_out, b + 1)) if g else always)
                        product(pe, branches[g], oH, oL, lambda b: pe.wait_ge(gate_out, 8 * g + b + 1))

                @block.scalar
                def _(act):
                    for g in range(2):
                        for b in range(8):
                            wait_bank(act, gates[g], b)
                            if g:
                                act.wait_ge(br_out, b + 1)
                            act.activation(gate[:, b // 2, (b % 2) * HALF:(b % 2 + 1) * HALF], bank[b][:, :],
                                           ACT.Sigmoid).then_inc(gate_out, 1)

                @block.vector
                def _(dve):
                    for g in range(2):
                        for b in range(8):
                            n = 8 * g + b
                            cols = slice((b % 2) * HALF, (b % 2 + 1) * HALF)
                            dve.wait_ge(gate_out, n + 1)
                            wait_bank(dve, branches[g], b)
                            dst = merged[:, 4 * g + b // 2, cols]
                            if first:
                                dve.tensor_tensor(dst, bank[b][:, :], gate[:, b // 2, cols], ALU.mult).then_inc(br_out, 1)
                            else:
                                dve.tensor_tensor(tmp[n % 2][:, :], bank[b][:, :], gate[:, b // 2, cols],
                                                  ALU.mult).then_inc(br_out, 1)
                                dve.wait_ge(br_out, n + 1)
                                dve.tensor_tensor(dst, dst, tmp[n % 2][:, :], ALU.add).then_inc(summed, 1)

        def stick_breaking():
            q = at("sqT", RX, [P, SH, S])
            k = at("skT", RX + 16, [P, SH, S])
            v = at("sv", RX + 32, [P, NT, 512])
            e = [at(f"se{i}", RX + 48 + 2 * i, [P, 512]) for i in range(2)]
            spl = [at(f"ssp{i}", RX + 52 + 2 * i, [P, 512]) for i in range(2)]
            spL = [at(f"sspL{i}", RX + 52 + 2 * i, [P, 512], F32R) for i in range(2)]
            spH = [at(f"sspH{i}", RX + 56 + 2 * i, [P, 512], F32R) for i in range(2)]
            a = [at(f"sa{i}", RX + 60 + 2 * i, [P, 512]) for i in range(5)]
            triR, strictR = at("striR", RX + 70, [P, P], F32R), at("sstrictR", RX + 70.5, [P, P], F32R)
            zerob = at("szerob", RX + 71, [P, P], BF16)
            oT = at("soT", RX, [P, SH, S])
            oH = at("soH", RX + 16, [P, SH, S], F32R)
            oL = at("soL", RX, [P, SH, S], F32R)
            units = [(h, half, kb) for h in range(SH) for half in range(2) for kb in range(4 * half + 3, -1, -1)]
            first = [u for u, (h, half, kb) in enumerate(units) if kb == 4 * half + 3]
            ends = [u for u, (h, half, kb) in enumerate(units) if kb == 0]
            out_q, out_k, out_v = sem("s_out_q"), sem("s_out_k"), sem("s_out_v")
            z_full, na, ex, ln, spr, spm, spl_ok, c_full, rest, arg, argm, prob, pv, o_out = (
                sem("s_" + n) for n in ("z_full", "negabs", "exp", "ln", "softplus", "softplus_diag",
                                        "softplus_low", "c_full", "rest", "arg", "arg_diag", "prob", "pv", "o_out"))
            sph = [sem(f"s_softplus_high{i}") for i in range(2)]
            fixed, zeroed, zs_ok = sem("s_fixed"), sem("s_zero"), sem("s_scores_out")
            oh_done, ol_done = sem("s_oh"), sem("s_ol")
            scale = SD ** -0.5

            def off(u):
                h, half, kb = units[u]
                return max(0, kb - 4 * half) * P

            def diag(u):
                h, half, kb = units[u]
                return kb >= 4 * half

            ndiag = [0]
            for u in range(len(units)):
                ndiag.append(ndiag[-1] + diag(u))
            nend = [0]
            for u in range(len(units)):
                nend.append(nend[-1] + (u in ends))
            nrest = [0]
            for u in range(len(units)):
                nrest.append(nrest[-1] + (u not in ends))
            n_units = len(units)

            def high(copy, eng, u):
                o_ = off(u)
                ready_sp(eng, u)
                free_halves(eng, u)
                copy(spH[u % 2][:, o_:512], spl[u % 2][:, o_:512]).then_inc(sph[u % 2], 1)

            def piece(i):
                return slice((i % 2) * HALF, (i % 2 + 1) * HALF)

            def free_halves(eng, u):
                if u >= 2:
                    eng.wait_ge(c_full, u - 1)
                    if nrest[u - 1]:
                        eng.wait_ge(rest, nrest[u - 1])

            with nc.Block() as block:
                @block.sync
                def _(sp):
                    load_weights(sp, SQ, start=2)
                    for g in (SK, SV):
                        load_weights(sp, g)
                    load_weights(sp, MERGE1[0][0], stop=2)

                @block.gpsimd
                def _(pool):
                    split_weights(pool, SQ, start=1)
                    for g in (SK, SV):
                        split_weights(pool, g)
                    pool.memset(zerob[:, :], 0.0).then_inc(zeroed, 1)
                    split_weights(pool, MERGE1[0][0], stop=2)
                    for u in range(n_units):
                        o_ = off(u)
                        pool.wait_ge(sph[u % 2], u // 2 + 1)
                        free_halves(pool, u)
                        pool.tensor_tensor(spL[u % 2][:, o_:512], spl[u % 2][:, o_:512],
                                           spH[u % 2][:, o_:512].bitcast(F32), ALU.subtract).then_inc(spl_ok, 1)

                def ready_sp(eng, u):
                    if diag(u):
                        eng.wait_ge(spm, ndiag[u + 1])
                    else:
                        eng.wait_ge(spr, u + 1)

                @block.tensor
                def _(pe):
                    product(pe, SQ, hH, hL, always)
                    product(pe, SK, hH, hL, lambda b: pe.wait_ge(out_q, b + 1))
                    product(pe, SV, hH, hL, lambda b: pe.wait_ge(out_k, b + 1))
                    pe.wait_ge(out_v, 8)

                    pe.wait_ge(fixed, 2)
                    pe.wait_ge(zeroed, 1)

                    def scores(u):
                        h, half, kb = units[u]
                        o_ = off(u)
                        if u >= 4:
                            pe.wait_ge(spr, u - 3)
                        pe.matmul(bank[u % 4][:, o_:512], k[:, h, kb * P:(kb + 1) * P],
                                  q[:, h, half * HALF + o_:(half + 1) * HALF], start=True, stop=True).then_inc(z_full, 1)

                    def sums(u):
                        o_ = off(u)
                        R = bank[4 + nend[u] % 2]
                        if u in first:
                            if nend[u] >= 2:
                                pe.wait_ge(arg, ends[nend[u] - 2] + 1)
                            pe.matmul(R, zerob[:, :], with_dim(zerob[:, :], 1, 4), start=True, stop=True)
                        pe.wait_ge(spl_ok, u + 1)
                        pe.matmul(R[:, o_:512], triR[:, :], spH[u % 2][:, o_:512], start=False, stop=True, skip_group_check=True)
                        pe.matmul(R[:, o_:512], triR[:, :], spL[u % 2][:, o_:512], start=False, stop=True,
                                  skip_group_check=True).then_inc(c_full, 1)

                    def others(u):
                        if u in ends:
                            return
                        o_ = off(u)
                        R = bank[4 + nend[u] % 2]
                        pe.wait_ge(arg, u + 1)
                        pe.matmul(R[:, o_:512], strictR[:, :], spH[u % 2][:, o_:512], start=False, stop=True, skip_group_check=True)
                        pe.matmul(R[:, o_:512], strictR[:, :], spL[u % 2][:, o_:512], start=False, stop=True,
                                  skip_group_check=True).then_inc(rest, 1)

                    def values(u):
                        h, half, kb = units[u]
                        o_ = off(u)
                        pe.wait_ge(prob, u + 1)
                        if u in first and nend[u] >= 2:
                            pe.wait_ge(o_out, nend[u] - 1)
                        last = pe.matmul(bank[6 + nend[u] % 2][:, o_:512], v[:, kb, h * P:(h + 1) * P],
                                         a[u % 5][:, o_:512], start=(u in first), stop=(kb == 0), skip_group_check=True)
                        last.then_inc(pv, 1)

                    scores(0)
                    for s in range(n_units + 4):
                        if 3 <= s < n_units + 3:
                            sums(s - 3)
                        if s + 1 < n_units:
                            scores(s + 1)
                        if s >= 4:
                            values(s - 4)
                        if 3 <= s < n_units + 3:
                            others(s - 3)

                @block.scalar
                def _(act):
                    act.copy(triR[:, :], const("tri")).then_inc(fixed, 1)
                    act.copy(strictR[:, :], const("strict")).then_inc(fixed, 1)
                    for b in range(8):
                        wait_bank(act, SQ, b)
                        act.activation(q[:, b // 2, (b % 2) * HALF:(b % 2 + 1) * HALF], bank[b][:, :], ACT.Copy,
                                       scale=scale).then_inc(out_q, 1)
                    for b in range(8):
                        wait_bank(act, SK, b)
                        act.copy(k[:, b // 2, (b % 2) * HALF:(b % 2 + 1) * HALF], bank[b][:, :]).then_inc(out_k, 1)
                    for b in range(8):
                        wait_bank(act, SV, b)
                        act.copy(v[:, b, :], bank[b][:, :]).then_inc(out_v, 1)

                    act.preload_act_table_set("natural_log_exp_and_others")
                    def out_of_bank(u):
                        o_ = off(u)
                        act.wait_ge(z_full, u + 1)
                        if u >= 5:
                            act.wait_ge(pv, u - 4)
                        act.copy(a[u % 5][:, o_:512], bank[u % 4][:, o_:512]).then_inc(zs_ok, 1)

                    def logs(u):
                        o_ = off(u)
                        act.wait_ge(na, u + 1)
                        act.activation(e[u % 2][:, o_:512], e[u % 2][:, o_:512], ACT.Exp).then_inc(ex, 1)
                        act.wait_ge(ex, u + 1)
                        act.activation(e[u % 2][:, o_:512], e[u % 2][:, o_:512], ACT.Ln, bias=1.0).then_inc(ln, 1)

                    def probs(u):
                        o_ = off(u)
                        if diag(u):
                            act.wait_ge(argm, ndiag[u + 1])
                        else:
                            act.wait_ge(arg, u + 1)
                        act.activation(a[u % 5][:, o_:512], a[u % 5][:, o_:512], ACT.Exp).then_inc(prob, 1)

                    for s in range(n_units + 7):
                        if s < n_units:
                            out_of_bank(s)
                        if 2 <= s < n_units + 2 and s % 2 == 0:
                            high(act.copy, act, s - 2)
                        if 1 <= s < n_units + 1:
                            logs(s - 1)
                        if 3 <= s < n_units + 3:
                            probs(s - 3)
                        if s >= 7 and s - 7 in ends and ends.index(s - 7) % 2:
                            for i in (ends.index(s - 7) - 1, ends.index(s - 7)):
                                act.wait_ge(o_out, i + 1)
                                act.copy(oH[:, i // 2, piece(i)], oT[:, i // 2, piece(i)]).then_inc(oh_done, 1)

                @block.vector
                def _(dve):
                    def front(u):
                        o_ = off(u)
                        dve.wait_ge(zs_ok, u + 1)
                        if u >= 2:
                            dve.wait_ge(spr, u - 1)
                        dve.scalar_tensor_tensor(out=e[u % 2][:, o_:512], in0=bank[u % 4][:, o_:512], scalar=-1.0,
                                                 in1=a[u % 5][:, o_:512],
                                                 op0=ALU.mult, op1=ALU.min).then_inc(na, 1)

                    def softplus(u):
                        o_ = off(u)
                        dve.wait_ge(ln, u + 1)
                        free_halves(dve, u)
                        dve.scalar_tensor_tensor(out=spl[u % 2][:, o_:512], in0=bank[u % 4][:, o_:512], scalar=0.0,
                                                 in1=e[u % 2][:, o_:512], op0=ALU.max, op1=ALU.add).then_inc(spr, 1)
                        if diag(u):
                            dve.wait_ge(spr, u + 1)
                            dve.tensor_tensor(spl[u % 2][:, o_:o_ + P], spl[u % 2][:, o_:o_ + P], const("strict"),
                                              ALU.mult).then_inc(spm, 1)

                    def argument(u):
                        o_ = off(u)
                        dve.wait_ge(c_full, u + 1)
                        dve.tensor_tensor(a[u % 5][:, o_:512], a[u % 5][:, o_:512], bank[4 + nend[u] % 2][:, o_:512],
                                          ALU.subtract).then_inc(arg, 1)
                        if diag(u):
                            dve.wait_ge(arg, u + 1)
                            dve.tensor_tensor(a[u % 5][:, o_:o_ + P], a[u % 5][:, o_:o_ + P], const("strictneg"),
                                              ALU.add).then_inc(argm, 1)

                    def out(i):
                        h, half, _ = units[ends[i]]
                        dve.wait_ge(pv, ends[i] + 1)
                        dve.tensor_copy(oT[:, h, half * HALF:(half + 1) * HALF], bank[6 + i % 2][:, :]).then_inc(o_out, 1)

                    outs = 0
                    for s in range(n_units + 8):
                        if 2 <= s < n_units + 2:
                            softplus(s - 2)
                            if s % 2:
                                high(dve.tensor_copy, dve, s - 2)
                        if 3 <= s < n_units + 3:
                            argument(s - 3)
                        if s < n_units:
                            front(s)
                        if s >= 5 and (s - 5) in ends:
                            out(outs)
                            outs += 1
                        if s >= 8 and s - 8 in ends and ends.index(s - 8) % 2:
                            for i in (ends.index(s - 8) - 1, ends.index(s - 8)):
                                dve.wait_ge(oh_done, i + 1)
                                dve.tensor_tensor(oL[:, i // 2, piece(i)], oT[:, i // 2, piece(i)],
                                                  oH[:, i // 2, piece(i)].bitcast(F32), ALU.subtract).then_inc(ol_done, 1)
            return oH, oL
        def nsa():
            RH_T, RH_Q = RH, RH + 32
            qtok = at("nq", RX, [P, NT, 512])
            kvtok = at("nkv", RX + 16, [P, NT, KVW])
            kcv = at("nkcv", RX + 25, [P, S])
            kc2, vc2 = at("nkc2", RX + 29, [P, S]), at("nvc2", RX + 33, [P, S])
            sqt = at("nsqt", RX + 37, [P, 512])
            gC = at("ngateC", RX + 40, [P, KT, S])
            onehot, urev = at("nonehot", RX + 42, [33, REV]), at("nurev", RX + 48, [NH, REV + 1])
            relb = at("nrelb", RX + 41, [33, NH])
            rel_in, rel_neg, rel_full, rel_out, rel_put = (sem("n_rel_" + n) for n in ("in", "neg", "full", "out", "put"))
            out_q, out_cv, out_kv, moved, out_gc = (sem("n_out_" + n) for n in ("q", "cv", "kv", "moved", "gc"))
            sq_a, sq_b, qn1, qn2, kn2 = (sem("n_" + n) for n in ("sq", "sumsq", "q_normed", "q_scaled", "k_normed"))
            steps = tuple(sem("na_" + n) for n in ("mean", "ln", "exp", "newton"))
            steps2 = tuple(sem("nb_" + n) for n in ("mean", "ln", "exp", "newton"))
            q4 = qtok[:, :, :].rearrange("p t (h d) -> p t h d", h=NH)
            qstat = [stat[:, n, 0:64] for n in range(4)]
            kstat = [stat[:, 4 + n, 0:16] for n in range(4)]
            with nc.Block() as block:
                @block.sync
                def _(sp):
                    sp.dma_start(relb[0:32, :], w["rel_bias"]).then_inc(rel_in, 16)
                    sp.dma_start(onehot[:, :], w["onehot"]).then_inc(rel_in, 16)
                    load_weights(sp, NQ, start=2)
                    for g in (CV, KV):
                        load_weights(sp, g)
                    sp.wait_ge(rel_out, 3)
                    sp.dma_start(w["bias_rev"][:, 0:REV], urev[:, 0:REV]).then_inc(rel_put, 16)
                    sp.wait_ge(out_cv, 2)
                    sp.dma_start(kc2[0:64, :], kcv[0:64, :]).then_inc(moved, 16)
                    sp.dma_start(kc2[64:128, 0:S - 1], kcv[0:64, 1:S]).then_inc(moved, 16)
                    sp.dma_start(vc2[0:64, :], kcv[64:128, :]).then_inc(moved, 16)
                    sp.dma_start(vc2[64:128, 0:S - 1], kcv[64:128, 1:S]).then_inc(moved, 16)
                    for g in GC:
                        load_weights(sp, g)
                    sp.wait_ge(moved, 64)
                    sp.wait_ge(rel_put, 16)

                @block.gpsimd
                def _(pool):
                    pool.memset(relb[32:33, :], NEG).then_inc(rel_neg, 1)
                    pool.wait_ge(rel_neg, 1)
                    split_weights(pool, NQ, start=1)
                    for g in [CV, KV] + GC:
                        split_weights(pool, g)

                @block.tensor
                def _(pe):
                    product(pe, NQ, hH, hL, always)
                    pe.wait_ge(rel_in, 32)
                    pe.wait_ge(rel_neg, 1)
                    for n in range(3):
                        a, b = n * 512, min(REV, n * 512 + 512)
                        pe.wait_ge(out_q, n + 3)
                        pe.matmul(bank[2 + n][0:NH, 0:b - a], relb[:, :], onehot[:, a:b], start=True, stop=True).then_inc(rel_full, 1)
                    product(pe, CV, hH, hL, always)
                    product(pe, KV, hH, hL, lambda b: pe.wait_ge(out_cv, b + 1) if b < 2 else
                            pe.wait_ge(rel_out, b - 1) if b < 5 else pe.wait_ge(out_q, b + 1))
                    product(pe, GC[0], hH, hL, lambda b: pe.wait_ge(out_kv, b + 1))
                    product(pe, GC[1], hH, hL, lambda b: pe.wait_ge(out_gc, b + 1))

                @block.scalar
                def _(act):
                    for b in range(8):
                        wait_bank(act, NQ, b)
                        act.copy(qtok[:, b, :], bank[b][:, :]).then_inc(out_q, 1)
                    for n in range(3):
                        a, b = n * 512, min(REV, n * 512 + 512)
                        act.wait_ge(rel_full, n + 1)
                        act.copy(urev[:, a:b], bank[2 + n][0:NH, 0:b - a]).then_inc(rel_out, 1)
                    for b in range(2):
                        wait_bank(act, CV, b)
                        act.copy(kcv[:, b * HALF:(b + 1) * HALF], bank[b][:, :]).then_inc(out_cv, 1)
                    for b in range(8):
                        wait_bank(act, KV, b)
                        act.copy(kvtok[:, b, :], bank[b][:, 0:KVW]).then_inc(out_kv, 1)
                    act.wait_ge(steps[0], 1)
                    inv_root(act, None, 1, steps, *qstat, ND, "act")
                    act.wait_ge(steps2[0], 1)
                    inv_root(act, None, 1, steps2, *kstat, ND, "act")
                    act.wait_ge(rel_put, 16)
                    act.activation(gatef[:, :, :], kvtok[:, :, 256:280], ACT.Sigmoid)
                    for g in range(2):
                        for b in range(8):
                            wait_bank(act, GC[g], b)
                            act.activation(gC[:, 4 * g + b // 2, (b % 2) * HALF:(b % 2 + 1) * HALF], bank[b][:, :],
                                           ACT.Sigmoid).then_inc(out_gc, 1)

                @block.vector
                def _(dve):
                    for t in range(NT):
                        dve.wait_ge(out_q, t + 1)
                        if t:
                            dve.wait_ge(sq_b, t)
                        dve.tensor_tensor(sqt[:, :], qtok[:, t, :], qtok[:, t, :], ALU.mult).then_inc(sq_a, 1)
                        dve.wait_ge(sq_a, t + 1)
                        dve.tensor_reduce(qstat[0][:, 8 * t:8 * t + 8], sqt[:, :].rearrange("p (h d) -> p h d", h=NH),
                                          AX.X, ALU.add).then_inc(sq_b, 1)
                    dve.wait_ge(sq_b, NT)
                    inv_root(None, dve, 1, steps, *qstat, ND, "dve1")
                    n = NT
                    for t in range(NT):
                        for k in range(2):
                            dve.wait_ge(out_kv, t + 1)
                            dve.wait_ge(sq_b, n)
                            src = kvtok[:, t, 128 * k:128 * k + 64]
                            dve.tensor_tensor(sqt[:, 0:64], src, src, ALU.mult).then_inc(sq_a, 1)
                            n += 1
                            dve.wait_ge(sq_a, n)
                            dve.tensor_reduce(kstat[0][:, 2 * t + k:2 * t + k + 1], sqt[:, 0:64], AX.X, ALU.add).then_inc(sq_b, 1)
                    dve.wait_ge(sq_b, n)
                    inv_root(None, dve, 1, steps2, *kstat, ND, "dve1")
                    dve.wait_ge(steps[2], 1)
                    inv_root(None, dve, 1, steps, *qstat, ND, "dve2")
                    for t in range(NT):
                        dve.tensor_tensor(q4[:, t, :, :], q4[:, t, :, :],
                                          with_dim(qstat[2][:, 8 * t:8 * t + 8], 2, ND), ALU.mult).then_inc(qn1, 1)
                        dve.wait_ge(qn1, t + 1)
                        dve.scalar_tensor_tensor(out=q4[:, t, :, :], in0=q4[:, t, :, :], scalar=ND ** -0.5,
                                                 in1=with_dim(qgain[:, :], 1, NH), op0=ALU.mult, op1=ALU.mult).then_inc(qn2, 1)
                    dve.wait_ge(steps2[2], 1)
                    inv_root(None, dve, 1, steps2, *kstat, ND, "dve2")
                    for t in range(NT):
                        for k in range(2):
                            src = kvtok[:, t, 128 * k:128 * k + 64]
                            dve.scalar_tensor_tensor(out=src, in0=src, scalar=kstat[2][:, 2 * t + k:2 * t + k + 1],
                                                     in1=kgain[:, :], op0=ALU.mult, op1=ALU.mult).then_inc(kn2, 1)

            Tt = at("nT", RH_T, [P, NH, S])
            kH = [at("nksH", RH_Q, [P, S], F32R), at("nkwH", RH_Q + 8, [P, S], F32R)]
            kL = [at("nksL", RH_Q + 4, [P, S], F32R), at("nkwL", RH_Q + 12, [P, S], F32R)]
            kraw = [at(f"nkraw{i}", RH + 56 + i, [64, 2, P]) for i in range(2)]
            w1 = [at("nw1k", RH_T, [P, 16, CMP_HID]), at("nw1v", RH_T + 16, [P, 16, CMP_HID])]
            flipped = [at(f"nflip{i}", RING + 8 * i, [P, 2, S]) for i in range(2)]
            blk = [at(f"nblk{i}", RING + 16 + 4 * i, [P, 16, NCMP]) for i in range(2)]
            w2 = [at(f"nw2{i}", RX + 37 + 0.5 * i, [P, 2, ND]) for i in range(2)]
            pe2 = [at(f"npe{i}", RX + 38 + 0.0625 * i, [P, 16]) for i in range(2)]
            RP = RH + 48
            hx, hu, hg = (at(f"nhid{i}", x, [NCMP, 2 * CMP_HID]) for i, x in enumerate((RP + 1, RH + 58, RH + 60)))
            hgT = at("nhidT", RP, [P, 4, NCMP])
            kcr, kcd = at("nkcr", RP + 3, [NCMP, ND]), at("nkcd", RP + 3.25, [NCMP, ND])
            vcn = at("nvcn", RX + 38.25, [NCMP, ND])
            kcH, kcL = at("nkcH", RX + 38.5, [P, 64], F32R), at("nkcL", RX + 38.75, [P, 64], F32R)
            kcraw = at("nkcraw", RP + 3.5, [64, 64])
            expandb = at("nexpandb", RX + 25, [NSEL, S], BF16)
            expandf = at("nexpandf", RP + 4, [NSEL, S])
            k_in = [sem(f"n_w1_in{i}") for i in range(2)]
            pe_in, w2_in, hid_turned, hgt_ok = sem("n_pe_in"), sem("n_w2_in"), sem("n_hid_turned"), sem("n_hidT")
            ex_in, tt_in = sem("n_expand_in"), [sem("n_table_in0"), sem("n_table_in1")]
            tt_full, tt_out = sem("n_table_full"), sem("n_table_out")
            blk_ok, hid_full, hx_ok, hs1, hs2, hs3, hsig, hg_ok, kc_full, kcs = (
                sem("n_" + n) for n in ("blk", "hid_full", "hx", "hs1", "hs2", "hs3", "hsig", "hg", "kc_full", "kcs"))
            kc_ok, kct_full, kct_out, tfull, tout, casts, ksplit = (
                sem("n_" + n) for n in ("kc_ok", "kct_full", "kct_out", "tfull", "tout", "casts", "ksplit"))
            steps3 = tuple(sem("nc_" + n) for n in ("mean", "ln", "exp", "newton"))
            cstat = [stat[0:NCMP, n, 0:1] for n in range(4)]

            def skew(h0, h1):
                return bass.AP(w["bias_rev"].tensor, h0 * (REV + 1), [[1, P], [REV + 1, h1 - h0], [1, S]])

            with nc.Block() as block:
                @block.sync
                def _(sp):
                    with nc.allow_non_contiguous_dma(reason="2048 positional terms onto partitions"):
                        for i, src in enumerate(("nsa_pe_k", "nsa_pe_v")):
                            sp.dma_start(pe2[i][:, :], w[src].rearrange("(m p) d -> (p d) m", p=2)).then_inc(pe_in, 16)

                    def table(g):
                        if g >= 2:
                            sp.wait_ge(tt_full, 4 * (g - 1))
                        sp.dma_start(flipped[g % 2][:, :, :], skew(2 * g, 2 * g + 2)).then_inc(tt_in[g % 2], 16)

                    sp.dma_start(w1[0][:, :, :], w["nsa_wk1"].rearrange("(m q) n -> q m n", q=P)).then_inc(k_in[0], 16)
                    table(0)
                    sp.dma_start(w1[1][:, :, :], w["nsa_wv1"].rearrange("(m q) n -> q m n", q=P)).then_inc(k_in[1], 16)
                    table(1)
                    for i, src in enumerate(("nsa_wk2", "nsa_wv2")):
                        sp.dma_start(w2[i][:, :, :], w[src].rearrange("(j p) d -> p j d", p=P)).then_inc(w2_in, 16)
                    sp.dma_start(expandf[:, :], w["expand"]).then_inc(ex_in, 16)
                    table(2)
                    table(3)

                @block.tensor
                def _(pe):
                    for t in range(NT):
                        if t >= 2:
                            pe.wait_ge(tout, t - 1)
                        for j in range(2):
                            last = pe.transpose(bank[t % 2][0:64, j * P:(j + 1) * P],
                                                kvtok[:, t, 128 * j:128 * j + 64], const("ident"))
                        last.then_inc(tfull, 1)
                    def hidden(i):
                        pe.wait_ge(k_in[i], 16)
                        pe.wait_ge(blk_ok, i + 1)
                        for m in range(16):
                            last = pe.matmul(bank[2][0:NCMP, i * CMP_HID:(i + 1) * CMP_HID], blk[i][:, m, :], w1[i][:, m, :],
                                             start=(m == 0), stop=(m == 15))
                        last.then_inc(hid_full, 1)

                    def flips(g):
                        pe.wait_ge(tt_in[g % 2], 16 * (g // 2 + 1))
                        for j in range(4):
                            n = 4 * g + j
                            if n >= 2:
                                pe.wait_ge(tt_out, n - 1)
                            pe.matmul(bank[5 + n % 2][:, :], const("flip"), flipped[g % 2][:, j // 2, (j % 2) * 512:(j % 2 + 1) * 512],
                                      start=True, stop=True).then_inc(tt_full, 1)

                    hidden(0)
                    flips(0)
                    hidden(1)
                    flips(1)
                    pe.wait_ge(hg_ok, 1)
                    for j in range(4):
                        last = pe.transpose(bank[7][:, j * NCMP:(j + 1) * NCMP], hg[:, j * P:(j + 1) * P],
                                            const("ident", NCMP)[:, 0:NCMP])
                    last.then_inc(hid_turned, 1)
                    flips(2)
                    pe.wait_ge(w2_in, 32)
                    pe.wait_ge(hgt_ok, 1)
                    for i in range(2):
                        for j in range(2):
                            last = pe.matmul(bank[3][0:NCMP, i * ND:(i + 1) * ND], hgT[:, 2 * i + j, :], w2[i][:, j, :],
                                             start=(j == 0), stop=(j == 1))
                    last.then_inc(kc_full, 1)
                    flips(3)
                    pe.wait_ge(kc_ok, 1)
                    pe.transpose(bank[4][0:64, 0:NCMP], kcd[:, :], const("ident", NCMP)[:, 0:NCMP]).then_inc(kct_full, 1)

                @block.scalar
                def _(act):
                    for t in range(NT):
                        act.wait_ge(tfull, t + 1)
                        if t >= 2:
                            act.wait_ge(ksplit, 8 * (t - 1))
                        act.copy(kraw[t % 2][:, :, :], bank[t % 2][0:64, 0:2 * P].rearrange("p (j c) -> p j c", j=2)).then_inc(tout, 1)
                    act.wait_ge(hs3, 1)
                    act.activation(hu[:, :], hu[:, :], ACT.Sigmoid, scale=2 * 0.7978845608028654).then_inc(hsig, 1)
                    act.wait_ge(hid_turned, 1)
                    act.copy(hgT[:, :, :].rearrange("p a n -> p (a n)"), bank[7][:, 0:4 * NCMP]).then_inc(hgt_ok, 1)
                    act.wait_ge(kc_full, 1)
                    act.copy(vcn[:, :], bank[3][0:NCMP, ND:2 * ND])
                    act.copy(kcr[:, :], bank[3][0:NCMP, 0:ND]).then_inc(kcs, 1)
                    act.wait_ge(steps3[0], 1)
                    inv_root(act, None, 1, steps3, *cstat, ND, "act")
                    act.wait_ge(kct_full, 1)
                    act.copy(kcraw[:, 0:NCMP], bank[4][0:64, 0:NCMP]).then_inc(kct_out, 1)
                    act.wait_ge(ex_in, 16)
                    act.copy(expandb[:, :], expandf[:, :])
                    act.copy(identb[:, :], const("ident"))
                    act.copy(windowb[:, :], const("window"))

                @block.vector
                def _(dve):
                    def stack(raw, high, low, done, n):
                        dve.tensor_copy(high[0:64], raw).then_inc(done, 1)
                        dve.tensor_copy(high[64:128], raw).then_inc(done, 1)
                        dve.wait_ge(done, n + 1)
                        dve.tensor_tensor(low[0:64], raw, high[0:64].bitcast(F32), ALU.subtract).then_inc(done, 1)
                        dve.tensor_tensor(low[64:128], raw, high[0:64].bitcast(F32), ALU.subtract).then_inc(done, 1)

                    dve.wait_ge(pe_in, 32)
                    for i, src in enumerate((kc2, vc2)):
                        row = src[:, :].ap[0][0]
                        win = bass.AP(src[:, :].tensor, src[:, :].offset, [[row, P], [2, 16], [CMP_STRIDE, NCMP]])
                        dve.tensor_tensor(blk[i][:, :, :], win, with_dim(pe2[i][:, :], 2, NCMP), ALU.add).then_inc(blk_ok, 1)
                    for t in range(NT):
                        dve.wait_ge(tout, t + 1)
                        for j in range(2):
                            cs = slice(t * P, (t + 1) * P)
                            stack(kraw[t % 2][:, j, :], kH[j][:, cs], kL[j][:, cs], ksplit, 8 * t + 4 * j)
                    dve.memset(kcraw[:, NCMP:64], 0.0).then_inc(hs1, 1)
                    dve.wait_ge(hs1, 1)

                    def table(n0, n1):
                        for n in range(n0, n1):
                            dve.wait_ge(tt_full, n + 1)
                            dve.tensor_copy(Tt[:, n // 2, (n % 2) * 512:(n % 2 + 1) * 512], bank[5 + n % 2][:, :]).then_inc(tt_out, 1)

                    table(0, 4)
                    dve.wait_ge(hid_full, 2)
                    dve.tensor_copy(hx[:, :], bank[2][0:NCMP, :]).then_inc(hx_ok, 1)
                    dve.wait_ge(hx_ok, 1)
                    dve.tensor_tensor(hu[:, :], hx[:, :], hx[:, :], ALU.mult).then_inc(hs1, 1)
                    dve.wait_ge(hs1, 2)
                    dve.tensor_scalar(hu[:, :], hu[:, :], 0.044715, 1.0, ALU.mult, ALU.add).then_inc(hs2, 1)
                    dve.wait_ge(hs2, 1)
                    dve.tensor_tensor(hu[:, :], hu[:, :], hx[:, :], ALU.mult).then_inc(hs3, 1)
                    table(4, 6)
                    dve.wait_ge(hsig, 1)
                    dve.tensor_tensor(hg[:, :], hx[:, :], hu[:, :], ALU.mult).then_inc(hg_ok, 1)
                    table(6, 12)
                    dve.wait_ge(kcs, 1)
                    dve.tensor_tensor(kcd[:, :], kcr[:, :], kcr[:, :], ALU.mult).then_inc(hx_ok, 1)
                    dve.wait_ge(hx_ok, 2)
                    dve.tensor_reduce(cstat[0], kcd[:, :], AX.X, ALU.add).then_inc(hx_ok, 1)
                    dve.wait_ge(hx_ok, 3)
                    inv_root(None, dve, 1, steps3, *cstat, ND, "dve1")
                    table(12, 16)
                    dve.wait_ge(steps3[2], 1)
                    inv_root(None, dve, 1, steps3, *cstat, ND, "dve2")
                    dve.scalar_tensor_tensor(out=kcd[:, :], in0=kcr[:, :], scalar=cstat[2], in1=kgain[0:NCMP, :],
                                             op0=ALU.mult, op1=ALU.mult).then_inc(kc_ok, 1)
                    dve.wait_ge(kct_out, 1)
                    stack(kcraw[:, :], kcH[:, :], kcL[:, :], casts, 0)

            sB = [at(f"nsB{i}", x, [P, S]) for i, x in enumerate((RH + 48, RH + 52, RH + 56, RING + 20))]
            qraw = [at(f"nqraw{i}", RH + 60 + 2 * i, [64, 4, P]) for i in range(2)]
            pT = [at(f"npT{i}", RX + 27 + 4 * i, [P, 8, P]) for i in range(2)]
            qS = [at(f"nqS{i}", RING + 4 * i, [P, NH, P], F32R) for i in range(2)]
            pTc = [at(f"npTc{i}", RING + 8 + 4 * i, [64, NH, P]) for i in range(2)]
            gt, eq = at("ngt", RING + 16, [P, NSEL, NSEL]), at("neq", RING + 17, [P, NSEL, NSEL])
            impp = at("nimp", RING + 18, [P, 72])
            bscore, pen = at("nbscore", RING + 18.375, [P, NSEL]), at("npen", RING + 18.5, [P, NSEL])
            penT = [at(f"npenT{i}", RING + 18.625 + 0.25 * i, [NSEL, P], BF16) for i in range(2)]
            small_ = [at(f"nsmall{i}", RING + 19.25 + 0.0625 * i, [P, 8]) for i in range(10)]
            nmax, rows = small_[0:4], small_[4:8]
            cmx, csm = small_[8], small_[9]
            diag = [at(f"ndiag{i}", RX + 35 + 0.5 * i, [P, P]) for i in range(4)]
            oT = at("noT", RX, [P, NT, 4, P])
            units = [("cmp", 0, 0)]
            for c in range(NT):
                for h in range(NH):
                    units += [("win", c, h), ("slc", c, h)]
                    if h == 2 and c + 1 < NT:
                        units.append(("cmp", c + 1, 0))
            N = len(units)
            AHEAD = 3

            def ncmp(c):
                return min(NCMP, 8 * c + 7)

            def keys(u):
                kind, c, h = units[u]
                k0 = max(0, c - WINDOW // P) if kind == "win" else 0
                return k0, c + 1 - k0

            uses = [(-1, "q", 0, 0, 4), (-1, "q", 0, 4, 4)]
            for s in range(N + AHEAD):
                u = s - AHEAD
                if 0 <= u < N:
                    kind, c, h = units[u]
                    if kind == "cmp":
                        uses += [(s, "cmp", u, 0, 4), (s, "cmp", u, 4, 4)]
                    else:
                        nk = keys(u)[1]
                        uses += [(s, "p", u, a, min(4, nk - a)) for a in range(0, nk, 4)]
                        if kind == "win" and h == 0 and c + 1 < NT:
                            uses += [(s, "q", c + 1, 0, 4), (s, "q", c + 1, 4, 4)]
                        if kind == "win" and h == 5 and 4 <= c + 1 < NT:
                            uses.append((s, "pen", c + 1, 0, 1))
            use_of = {}
            for n, x in enumerate(uses):
                use_of[x[1], x[2]] = n + 1
            scores_full, add_out, max_out, exp_out, scaled, cmp_p, t_full, t_out, pv, o_out, q_split, q_low = (
                sem("n_" + n) for n in ("scores", "biased", "rowmax", "exp", "scaled", "cmp_p", "turned", "turn_out", "pv",
                                        "o_out", "q_high", "q_low"))
            chain, impz, pen_ok, pre_exp, factor = (sem("n_" + n) for n in ("chain", "impz", "pen", "cmp_biased", "factor"))
            ncmp_before = [sum(1 for v in range(u) if units[v][0] == "cmp") for u in range(N + 1)]
            last_of_tile = {c: max(u for u in range(N) if units[u][1] == c and units[u][0] != "cmp") for c in range(NT)}
            pair = [pairs[0], pairs[1]]

            def table(c, h, k0, nk):
                a = S - P - P * c + P * k0
                return Tt[:, h, a:a + nk * P]

            with nc.Block() as block:
                @block.tensor
                def _(pe):
                    def scores(u):
                        kind, c, h = units[u]
                        if u >= 2:
                            pe.wait_ge(add_out, u - 1)
                        if kind == "cmp":
                            n = ncmp(c) + 1
                            pe.wait_ge(q_low, 2 * c + 2)
                            for h in range(NH):
                                dst = pair[u % 2][:, h * 64:h * 64 + n]
                                pe.matmul(dst, qS[c % 2][:, h, :], kcH[:, 0:n], start=True, stop=False)
                                last = pe.matmul(dst, qS[c % 2][:, h, :], kcL[:, 0:n], start=False, stop=True)
                            last.then_inc(scores_full, 1)
                            return
                        k0, nk = keys(u)
                        ks_ = 1 if kind == "win" else 0
                        if kind == "slc" and c >= 4 and h == 0:
                            pe.wait_ge(t_out, use_of["pen", c])
                        for a in range(0, nk, 4):
                            m = min(4, nk - a)
                            dst = pair[u % 2][:, a * P:(a + m) * P]
                            cols = slice((k0 + a) * P, (k0 + a + m) * P)
                            chosen = kind == "slc" and c >= 4
                            pe.matmul(dst, qS[c % 2][:, h, :], kH[ks_][:, cols], start=True, stop=False)
                            last = pe.matmul(dst, qS[c % 2][:, h, :], kL[ks_][:, cols], start=False, stop=not chosen)
                            if chosen:
                                last = pe.matmul(dst, penT[c % 2][:, :], expandb[:, cols], start=False, stop=True)
                            elif kind == "win" and c >= 4 and a == 0:
                                last = pe.matmul(pair[u % 2][:, 0:P], identb[:, :], windowb[:, :], start=False, stop=True,
                                                 skip_group_check=True)
                        last.then_inc(scores_full, 1)

                    def values(u):
                        kind, c, h = units[u]
                        if kind == "cmp":
                            return
                        if kind == "win" and h == 0 and c >= 2:
                            pe.wait_ge(o_out, c - 1)
                        dst = bank[6 + c % 2][64 * (h % 2):64 * (h % 2) + 64, (h // 2) * P:(h // 2 + 1) * P]
                        k0, nk = keys(u)
                        at_ = 64 if kind == "slc" else 192
                        if kind == "win":
                            if h == 0:
                                pe.wait_ge(t_out, use_of["cmp", units.index(("cmp", c, 0))])
                            n = ncmp(c)
                            pe.matmul(dst, vcn[0:n, :], pTc[c % 2][0:n, h, :], start=True, stop=False)
                        pe.wait_ge(t_out, use_of["p", u])
                        for a in range(nk):
                            last = pe.matmul(dst, kvtok[:, k0 + a, at_:at_ + ND], pT[u % 2][:, a, :],
                                             start=False, stop=(kind == "slc" and a == nk - 1))
                        last.then_inc(pv, 1)

                    n = 0
                    for s in range(-1, N + AHEAD + 1):
                        if 0 <= s < N:
                            scores(s)
                        while n < len(uses) and uses[n][0] == s:
                            _, what, u, a, m = uses[n]
                            if n >= 2:
                                pe.wait_ge(t_out, n - 1)
                            tb = bank[4 + n % 2]
                            if what == "cmp":
                                pe.wait_ge(cmp_p, ncmp_before[u + 1])
                                k = ncmp(units[u][1])
                                for j in range(4):
                                    last = pe.transpose(tb[0:k, j * P:(j + 1) * P],
                                                        sB[u % 4][:, (a + j) * 64:(a + j) * 64 + k], const("ident"))
                            elif what == "p":
                                pe.wait_ge(scaled, u + 1 - ncmp_before[u + 1])
                                for j in range(m):
                                    last = pe.matmul(tb[:, j * P:(j + 1) * P], sB[u % 4][:, (a + j) * P:(a + j + 1) * P],
                                                     diag[u % 4][:, :], start=True, stop=True)
                            elif what == "pen":
                                pe.wait_ge(pen_ok, u - 3)
                                last = pe.transpose(tb[0:NSEL, 0:P], pen[:, :], const("ident"))
                            else:
                                for j in range(4):
                                    last = pe.transpose(tb[0:64, j * P:(j + 1) * P],
                                                        qtok[:, u, (a + j) * ND:(a + j + 1) * ND], const("ident"))
                            last.then_inc(t_full, 1)
                            n += 1
                        if 0 <= s - AHEAD - 1 < N:
                            values(s - AHEAD - 1)

                def nth(u):
                    return u - ncmp_before[u]

                @block.sync
                def _(sp):
                    sp.wait_ge(scores_full, last_of_tile[NT - 2] + 1)
                    load_weights(sp, BR[0], stop=1)

                @block.gpsimd
                def _(pool):
                    for u in range(N):
                        if units[u][0] != "cmp":
                            pool.wait_ge(factor, nth(u) + 1)
                            pool.tensor_tensor(diag[u % 4][:, :], const("ident"), with_dim(rows[u % 4][:, 1], 1, P),
                                               ALU.mult).then_inc(scaled, 1)

                @block.scalar
                def _(act):
                    n = 0
                    for s in range(-1, N + AHEAD + 2):
                        while n < len(uses) and uses[n][0] == s:
                            _, what, u, a, m = uses[n]
                            act.wait_ge(t_full, n + 1)
                            tb = bank[4 + n % 2]
                            if what == "cmp":
                                c = units[u][1]
                                k = ncmp(c)
                                if c >= 2:
                                    act.wait_ge(pv, nth(last_of_tile[c - 2]) + 1)
                                act.copy(pTc[c % 2][0:k, a:a + 4, :], tb[0:k, :].rearrange("p (j c) -> p j c", j=4)).then_inc(t_out, 1)
                            elif what == "p":
                                prev = [v for v in range(u) if units[v][0] != "cmp" and v % 2 == u % 2]
                                if prev:
                                    act.wait_ge(pv, nth(prev[-1]) + 1)
                                act.copy(pT[u % 2][:, a:a + m, :],
                                         tb[:, 0:m * P].rearrange("p (j c) -> p j c", j=m)).then_inc(t_out, 1)
                            elif what == "pen":
                                act.copy(penT[u % 2][:, :], tb[0:NSEL, 0:P]).then_inc(t_out, 1)
                            else:
                                if u:
                                    act.wait_ge(q_low, 2 * u + a // 4 - 1)
                                act.copy(qraw[a // 4][:, :, :], tb[0:64, :].rearrange("p (j c) -> p j c", j=4)).then_inc(t_out, 1)
                                act.wait_ge(t_out, n + 1)
                                act.copy(qS[u % 2][0:64, a:a + 4, :], qraw[a // 4][:, :, :]).then_inc(q_split, 1)
                            n += 1
                        done_ = [c for c in range(NT) if last_of_tile[c] == s - AHEAD - 2]
                        if done_:
                            c = done_[0]
                            act.wait_ge(pv, nth(last_of_tile[c]) + 1)
                            act.copy(oT[:, c, :, :], bank[6 + c % 2][:, :].rearrange("p (j c) -> p j c", j=4)).then_inc(o_out, 1)
                        if 0 <= s < N:
                            kind, c, h = units[s]
                            if kind == "cmp":
                                k = ncmp(c)
                                act.wait_ge(pre_exp, ncmp_before[s + 1])
                                v = sB[s % 4][:, 0:512].rearrange("p (h n) -> p h n", h=NH)[:, :, 0:k]
                                act.activation(v, v, ACT.Exp).then_inc(exp_out, 1)
                            else:
                                nk = keys(s)[1]
                                act.wait_ge(max_out, nth(s) + 1)
                                v = sB[s % 4][:, 0:nk * P]
                                act.activation(v, v, ACT.Exp, bias=nmax[s % 4][:, 0:1],
                                               accum_out=rows[s % 4][:, 0:1]).then_inc(exp_out, 1)

                @block.vector
                def _(dve):
                    count = [0]

                    def link(ins):
                        count[0] += 1
                        ins.then_inc(chain, 1)
                        dve.wait_ge(chain, count[0])

                    def head_view(u, k):
                        return sB[u % 4][:, 0:512].rearrange("p (h n) -> p h n", h=NH)[:, :, 0:k]

                    def front(u):
                        kind, c, h = units[u]
                        dve.wait_ge(scores_full, u + 1)
                        if kind == "cmp":
                            k = ncmp(c)
                            v = head_view(u, k)
                            a = S - P - P * c + CMP_BLOCK - 1
                            full = Tt[:, :, :]
                            bias = bass.AP(full.tensor, full.offset + a, [list(full.ap[0]), [S, NH], [CMP_STRIDE, k]])
                            dve.tensor_tensor(v, pair[u % 2][:, 0:512].rearrange("p (h n) -> p h n", h=NH)[:, :, 0:k], bias,
                                              ALU.add).then_inc(add_out, 1)
                            dve.wait_ge(add_out, u + 1)
                            link(dve.tensor_reduce(cmx[:, :], v, AX.X, ALU.max))
                            link(dve.tensor_scalar(cmx[:, :], cmx[:, :], -1e20, None, ALU.max))
                            dve.tensor_tensor(v, v, with_dim(cmx[:, :], 2, k), ALU.subtract).then_inc(pre_exp, 1)
                            return
                        k0, nk = keys(u)
                        v = sB[u % 4][:, 0:nk * P]
                        dve.tensor_tensor(v, pair[u % 2][:, 0:nk * P], table(c, h, k0, nk), ALU.add).then_inc(add_out, 1)
                        dve.wait_ge(add_out, u + 1)
                        dve.tensor_reduce(nmax[u % 4][:, 0:1], v, AX.X, ALU.max, negate=True).then_inc(max_out, 1)

                    def scale(u):
                        kind, c, h = units[u]
                        dve.wait_ge(exp_out, u + 1)
                        link(dve.reciprocal(rows[u % 4][:, 0:1], rows[u % 4][:, 0:1]))
                        g = 3 * h + (2 if kind == "win" else 1)
                        dve.tensor_tensor(rows[u % 4][:, 1:2], rows[u % 4][:, 0:1], gatef[:, c, g:g + 1], ALU.mult).then_inc(factor, 1)

                    def cmp_normal(u):
                        c = units[u][1]
                        k = ncmp(c)
                        v = head_view(u, k)
                        dve.wait_ge(exp_out, u + 1)
                        link(dve.tensor_reduce(csm[:, :], v, AX.X, ALU.add))
                        link(dve.tensor_scalar(csm[:, :], csm[:, :], 1e-30, None, ALU.max))
                        link(dve.reciprocal(csm[:, :], csm[:, :]))
                        link(dve.tensor_tensor(v, v, with_dim(csm[:, :], 2, k), ALU.mult))
                        if c >= 4:
                            link(dve.tensor_reduce(impp[:, 1:1 + k], v.rearrange("p h n -> p n h"), AX.X, ALU.add))
                        gate = gatef[:, c, :].rearrange("p (h b) -> p h b", b=3)[:, :, 0]
                        dve.tensor_tensor(v, v, with_dim(gate, 2, k), ALU.mult).then_inc(cmp_p, 1)

                    def choose(c):
                        full = impp[:, :]
                        win = bass.AP(full.tensor, full.offset, [list(full.ap[0]), [4, NSEL], [1, 5]])
                        link(dve.tensor_reduce(bscore[:, :], win, AX.X, ALU.add))
                        link(dve.tensor_tensor(bscore[:, :], bscore[:, :], const("selbase")[:, c * NSEL:(c + 1) * NSEL], ALU.add))
                        sj, si = with_dim(bscore[:, :], 1, NSEL), with_dim(bscore[:, :], 2, NSEL)
                        dve.tensor_tensor(gt[:, :, :], sj, si, ALU.is_gt).then_inc(impz, 1)
                        link(dve.tensor_tensor(eq[:, :, :], sj, si, ALU.is_equal))
                        link(dve.tensor_tensor(eq[:, :, :].rearrange("p a b -> p (a b)"), eq[:, :, :].rearrange("p a b -> p (a b)"),
                                               const("tie"), ALU.mult))
                        dve.wait_ge(impz, c - 4 + 2)
                        link(dve.tensor_tensor(gt[:, :, :], gt[:, :, :], eq[:, :, :], ALU.add))
                        link(dve.tensor_reduce(pen[:, :], gt[:, :, :], AX.X, ALU.add))
                        dve.tensor_scalar(pen[:, :], pen[:, :], TOPN - 0.5, NEG, ALU.is_gt, ALU.mult).then_inc(pen_ok, 1)

                    def split_queries(c):
                        for g in range(2):
                            hs = slice(4 * g, 4 * g + 4)
                            dve.wait_ge(q_split, 2 * c + g + 1)
                            dve.tensor_tensor(qS[c % 2][64:128, hs, :], qraw[g][:, :, :], qS[c % 2][0:64, hs, :].bitcast(F32),
                                              ALU.subtract).then_inc(q_low, 1)

                    dve.memset(impp[:, :], 0.0).then_inc(impz, 1)
                    dve.wait_ge(impz, 1)
                    split_queries(0)
                    for s in range(N + 1):
                        if s < N:
                            front(s)
                        if s:
                            if units[s - 1][0] == "cmp":
                                cmp_normal(s - 1)
                            else:
                                scale(s - 1)
                        if s >= 3 and units[s - 3][0] == "cmp" and units[s - 3][1] >= 4:
                            choose(units[s - 3][1])
                        u = s - AHEAD - 1
                        if 0 <= u < N and units[u][0] == "win" and units[u][2] == 0 and units[u][1] + 1 < NT:
                            split_queries(units[u][1] + 1)

            return oT, gC

        def merge_and_output(oT, gC):
            oH, oL = at("noH", RH, [P, 4, S], F32R), at("noL", RH + 16, [P, 4, S], F32R)
            tmp = [at(f"nmtmp{i}", RX + 32 + 2 * i, [P, 512]) for i in range(2)]
            mH = at("mH", RH + 32, [P, KT, S], F32R)
            mL = at("mL", RX + 40, [P, KT, S], F32R)
            x1 = at("x1", RX, [P, NT, D])
            junk = at("ojunk", RX + 36, [P, D])
            oh, ol, br_out, summed = (sem("n4_" + n) for n in ("oh", "ol", "br_out", "summed"))
            x_back, mh, ml, x1_out, sq_done = (sem("o_" + n) for n in ("x_back", "high", "low", "x1", "square"))
            with nc.Block() as block:
                @block.sync
                def _(sp):
                    load_weights(sp, BR[0], start=1)
                    load_weights(sp, BR[1])
                    sp.wait_ge(ol, 4)
                    sp.dma_start(x1[:, :, :], x.rearrange("(t p) d -> p t d", p=P)).then_inc(x_back, 16)
                    for g in WO:
                        load_weights(sp, g)

                @block.gpsimd
                def _(pool):
                    for g in BR + WO:
                        split_weights(pool, g)

                @block.tensor
                def _(pe):
                    product(pe, BR[0], oH, oL, always, before=lambda j: pe.wait_ge(ol, 2 * j + 2))
                    product(pe, BR[1], oH, oL, lambda b: pe.wait_ge(br_out, b + 1))
                    product(pe, WO[0], mH, mL, lambda b: pe.wait_ge(br_out, 8 + b + 1),
                            before=lambda j: pe.wait_ge(ml, 2 * j + 2))
                    product(pe, WO[1], mH, mL, lambda b: pe.wait_ge(x1_out, b + 1))

                @block.scalar
                def _(act):
                    for h in range(4):
                        act.copy(oH[:, h, :].rearrange("p (c q) -> p c q", c=NT), oT[:, :, h, :]).then_inc(oh, 1)
                    for kt in range(KT):
                        act.wait_ge(summed, 2 * kt + 2)
                        act.copy(mH[:, kt, :], merged[:, kt, :]).then_inc(mh, 1)
                    for b in range(NT):
                        act.wait_ge(x1_out, NT + b + 1)
                        if b:
                            act.wait_ge(sq_done, b)
                        act.activation(junk[:, :], x1[:, b, :], ACT.Square,
                                       accum_out=stat[:, 0, b:b + 1]).then_inc(sq_done, 1)

                @block.vector
                def _(dve):
                    for h in range(4):
                        dve.wait_ge(oh, h + 1)
                        dve.tensor_tensor(oL[:, h, :].rearrange("p (c q) -> p c q", c=NT), oT[:, :, h, :],
                                          oH[:, h, :].bitcast(F32).rearrange("p (c q) -> p c q", c=NT),
                                          ALU.subtract).then_inc(ol, 1)

                    def low(kt):
                        dve.wait_ge(mh, kt + 1)
                        dve.tensor_tensor(mL[:, kt, :], merged[:, kt, :], mH[:, kt, :].bitcast(F32),
                                          ALU.subtract).then_inc(ml, 1)

                    for n in range(16):
                        g, b = n // 8, n % 8
                        cols = slice((b % 2) * HALF, (b % 2 + 1) * HALF)
                        wait_bank(dve, BR[g], b)
                        dst = merged[:, n // 2, cols]
                        dve.tensor_tensor(tmp[n % 2][:, :], bank[b][:, :], gC[:, n // 2, cols], ALU.mult).then_inc(br_out, 1)
                        dve.wait_ge(br_out, n + 1)
                        dve.tensor_tensor(dst, dst, tmp[n % 2][:, :], ALU.add).then_inc(summed, 1)
                        if n % 2 == 0 and n:
                            low(n // 2 - 1)
                    low(KT - 1)
                    dve.wait_ge(x_back, 16)
                    for g in range(2):
                        for b in range(8):
                            wait_bank(dve, WO[g], b)
                            dst = x1[:, b, g * 512:(g + 1) * 512]
                            dve.tensor_tensor(dst, dst, bank[b][:, :], ALU.add).then_inc(x1_out, 1)
            return x1

        def ffn(x1):
            SLOTS, FULLS = 8, 21

            def load_ffn(sp, g, i, **part):
                if g is UP:
                    load_weights(sp, g, i, SLOTS, lambda j: w["w_up"][256 * j:256 * j + 256, bass.ds(i * 512, 512)]
                                 .rearrange("(k p) n -> p k n", p=P), **part)
                else:
                    load_weights(sp, g, i, SLOTS, lambda j: w["w_down"][
                        bass.ds(i * 512 + 256 * j, 256), g.col0:g.col0 + 512].rearrange("(k p) n -> p k n", p=P), **part)

            norm_transpose("n2", x1, w["ln_mlp_g"], False, lambda sp: load_ffn(sp, UP, 0, stop=2),
                           lambda pool: split_weights(pool, UP, 0, SLOTS, stop=2))

            uH, uL = at("uH", RM, [P, 4, S], F32R), at("uL", RM + 16, [P, 4, S], F32R)
            rr = [at(f"rr{i}", RX + 32 + 2 * i, [P, 512]) for i in range(2)]
            sqr = [at(f"sqr{i}", RX + 36 + 2 * i, [P, 512]) for i in range(2)]
            CH = FF // 512
            up, down = UP, DOWN
            done["slot"] += SLOTS * (CH - 1)
            done["full"] += FULLS * (CH - 1)
            relu, sq_, uh, ul, added, seeded = (sem("f_" + n) for n in ("relu", "square", "high", "low", "added", "seeded"))
            with nc.Block() as block:
                @block.sync
                def _(sp):
                    with sp.Fori(0, CH - 1) as i:
                        load_ffn(sp, up, i, start=2)
                        load_ffn(sp, down[0], i)
                        load_ffn(sp, down[1], i)
                        load_ffn(sp, up, i + 1, stop=2)
                    load_ffn(sp, up, CH - 1, start=2)
                    load_ffn(sp, down[0], CH - 1)
                    load_ffn(sp, down[1], CH - 1)
                    for t in range(NT):
                        sp.wait_ge(added, 8 + 16 * (CH - 1) + 8 + t + 1)
                        sp.dma_start(out[t * P:(t + 1) * P, :], x1[:, t, :]).then_inc(out_done, 16)
                    sp.wait_ge(out_done, 16 * NT)

                @block.gpsimd
                def _(pool):
                    with pool.Fori(0, CH - 1) as i:
                        split_weights(pool, up, i, SLOTS, start=2)
                        for g in down:
                            split_weights(pool, g, i, SLOTS)
                        split_weights(pool, up, i + 1, SLOTS, stop=2)
                    split_weights(pool, up, CH - 1, SLOTS, start=2)
                    for g in down:
                        split_weights(pool, g, CH - 1, SLOTS)

                @block.tensor
                def _(pe):
                    pe.wait_ge(seeded, 1)
                    with pe.Fori(0, CH) as i:
                        product(pe, up, hH2, hL2, lambda b: pe.wait_ge(added, 16 * i + b + 1), i, SLOTS)

                        product(pe, down[0], uH, uL, lambda b: pe.wait_ge(relu, 8 * i + b + 1), i, SLOTS,
                                before=lambda j: pe.wait_ge(ul, 8 * i + 4 * j + 4))
                        product(pe, down[1], uH, uL, lambda b: pe.wait_ge(added, 16 * i + 8 + b + 1), i, SLOTS)

                @block.scalar
                def _(act):
                    with act.Fori(0, CH) as i:
                        for b in range(8):
                            wait_bank(act, up, b, i, SLOTS, FULLS)
                            act.activation(rr[b % 2][:, :], bank[b][:, :], ACT.Relu).then_inc(relu, 1)
                            act.wait_ge(sq_, 8 * i + b + 1)
                            act.copy(uH[:, b // 2, (b % 2) * HALF:(b % 2 + 1) * HALF], sqr[b % 2][:, :]).then_inc(uh, 1)

                @block.vector
                def _(dve):
                    for b in range(8):
                        last = dve.memset(stat[:, 7, b:b + 1], 0.0)
                        last.then_inc(added, 1)
                    dve.wait_ge(added, 8)
                    dve.memset(stat[:, 7, 8:9], 0.0).then_inc(seeded, 1)
                    with dve.Fori(0, CH) as i:
                        for b in range(8):
                            dve.wait_ge(relu, 8 * i + b + 1)
                            dve.tensor_tensor(sqr[b % 2][:, :], rr[b % 2][:, :], rr[b % 2][:, :], ALU.mult).then_inc(sq_, 1)
                            dve.wait_ge(uh, 8 * i + b + 1)
                            dve.tensor_tensor(uL[:, b // 2, (b % 2) * HALF:(b % 2 + 1) * HALF], sqr[b % 2][:, :],
                                              uH[:, b // 2, (b % 2) * HALF:(b % 2 + 1) * HALF].bitcast(F32),
                                              ALU.subtract).then_inc(ul, 1)
                        for g in range(2):
                            for b in range(8):
                                wait_bank(dve, down[g], b, i, SLOTS, FULLS)
                                dst = x1[:, b, g * 512:(g + 1) * 512]
                                dve.tensor_tensor(dst, dst, bank[b][:, :], ALU.add).then_inc(added, 1)

        hH2, hL2 = hH, hL
        oH, oL = gla()
        merge(0, oH, oL, MERGE0, SQ, True)
        oH, oL = stick_breaking()
        merge(1, oH, oL, MERGE1, NQ, False)
        recycle()
        oT, gC = nsa()
        recycle()
        x1 = merge_and_output(oT, gC)
        ffn(x1)


_IN_NAMES = ["x", "ln_mix_g", "ln_mlp_g", "w_in", "gla_w_a2", "gla_b_a", "gla_norm_g", "nsa_q_norm_g", "nsa_k_norm_g",
             "nsa_pe_k", "nsa_pe_v", "nsa_wk1", "nsa_wk2", "nsa_wv1", "nsa_wv2", "rel_bias", "w_br_gla", "w_br_sb",
             "w_br_nsa", "w_out", "w_up", "w_down"]


def shape_constants():
    import numpy as np
    i = np.arange(P)[:, None]
    j = np.arange(P)[None, :]
    c = {
        "ident": i == j, "flip": i == P - 1 - j, "tri": i >= j, "ones": i >= 0 * j, "strict": i < j,
        "strictneg": np.where(i < j, 0.0, NEG), "window": np.where(j > i, 0.0, NEG),
    }
    q = np.arange(S).reshape(NT, P, 1)
    blk = np.arange(NSEL)[None, None, :]
    cur = q // SEL
    base = np.where((blk == cur) | (blk == cur - 1) | (blk == 0), 1000.0, 0.0)
    base = np.where(blk * SEL <= q, base, NEG)
    c["selbase"] = base.transpose(1, 0, 2).reshape(P, NT * NSEL)
    c["tie"] = np.broadcast_to((np.arange(NSEL)[None, :] < np.arange(NSEL)[:, None]).reshape(1, -1), (P, NSEL * NSEL))
    cst = np.concatenate([np.asarray(c[n], np.float32) for n, _ in CONST_COLS], axis=1)
    dist = (S - 1) - np.arange(REV)
    starts = np.asarray(BUCKET_START)
    bucket = np.where(dist < 0, 32, np.searchsorted(starts, np.maximum(dist, 0), side="right") - 1)
    onehot = (np.arange(33)[:, None] == bucket[None, :]).astype(np.float32)
    expand = (np.arange(NSEL)[:, None] == (np.arange(S) // SEL)[None, :]).astype(np.float32)
    return {"cst": np.ascontiguousarray(cst), "causal": (i <= j).astype(np.uint32), "onehot": onehot, "expand": expand}


def kernel(**inputs):
    import numpy as np
    import concourse.bacc as bacc
    from concourse.bass_utils import run_bass_kernel_spmd

    nc = bacc.Bacc("TRN2", target_bir_lowering=False, num_devices=1)
    arrays, aps = {}, {}
    for name in _IN_NAMES:
        a = np.ascontiguousarray(inputs[name])
        if name == "x" or (name != "rel_bias" and a.ndim > 1):
            a = a.reshape(a.shape[1:])
        arrays[name] = a
    arrays.update(shape_constants())
    for name, a in arrays.items():
        aps[name] = nc.dram_tensor(name, a.shape, mybir.dt.from_np(a.dtype), kind="ExternalInput").ap()
    out = nc.dram_tensor("out", (S, D), F32, kind="ExternalOutput").ap()
    aps["bias_rev"] = nc.dram_tensor("bias_rev", (NH, REV + 1), F32, kind="Internal").ap()
    build(nc, aps["x"], aps, out)
    r = run_bass_kernel_spmd(nc, [arrays], core_ids=[0])
    return r.results[0]["out"].reshape(1, S, D)
```
